# Optimizing a Trainium2 kernel written in Bass

```python
import jax, jax.numpy as jnp
from jax import lax
import numpy as np

D_MODEL = 1024
BATCH = 1
SEQ = 256
DEPTH = 1

CHUNK = 64
POOL_GROUPS = 4
POOL_WINDOWS = (2, 4, 8, 16)
POOL_WIDTH = D_MODEL // 2
POOL_GROUP_DIM = POOL_WIDTH // POOL_GROUPS
SB_HEAD_DIM = 64
SB_HEADS = D_MODEL // 128
SB_WIDTH = SB_HEADS * SB_HEAD_DIM
SB_BLOCK = 128
MEM_LEN = 256
X_HEADS = 4
X_HEAD_DIM = D_MODEL // 16
X_WIDTH = X_HEADS * X_HEAD_DIM
N_BRANCHES = 3
D_FF = -(-8 * D_MODEL // (3 * 256)) * 256
RMS_EPS = 1e-6
IN_WIDTH = POOL_WIDTH + 3 * SB_WIDTH + X_WIDTH + N_BRANCHES * D_MODEL


def rmsnorm(x, g):
    xf = x.astype(jnp.float32)
    y = xf * lax.rsqrt(jnp.mean(xf * xf, axis=-1, keepdims=True) + RMS_EPS) * g.astype(jnp.float32)
    return y.astype(x.dtype)

def pool_mixer(p, w_mix, scale):
    b, s, _ = p.shape
    pg = p.astype(jnp.float32).reshape(b, s, POOL_GROUPS, POOL_GROUP_DIM)
    c = jnp.concatenate([jnp.zeros((b, 1, POOL_GROUPS, POOL_GROUP_DIM), jnp.float32),
                         jnp.cumsum(pg, axis=1)], axis=1)
    windows = jnp.array(POOL_WINDOWS, jnp.int32)
    t1 = jnp.arange(1, s + 1, dtype=jnp.int32)[:, None]
    lo = jnp.maximum(t1 - windows[None, :], 0)
    g_idx = jnp.arange(POOL_GROUPS, dtype=jnp.int32)[None, :]
    c_lo = c[:, lo, g_idx]
    count = jnp.minimum(t1, windows[None, :]).astype(jnp.float32)
    mixed = (c[:, 1:] - c_lo) / count[None, :, :, None] - pg
    mixed = mixed.astype(p.dtype)
    y = jnp.einsum('bsgc,gcd->bsgd', mixed, w_mix)
    return y.reshape(b, s, POOL_WIDTH) * scale

def stick_breaking_attention(q, k, v):
    b, s, h, dh = q.shape
    nb = s // SB_BLOCK
    scale = 1.0 / float(np.sqrt(dh))
    kf = k.astype(jnp.float32).transpose(0, 2, 1, 3)
    vf = v.astype(jnp.float32).transpose(0, 2, 1, 3)
    qb = q.astype(jnp.float32).transpose(0, 2, 1, 3).reshape(b, h, nb, SB_BLOCK, dh)
    qb = qb.transpose(2, 0, 1, 3, 4)
    key_pos = jnp.arange(s, dtype=jnp.int32)[None, :]

    def one_block(args):
        q_blk, bi = args
        z = jnp.einsum('bhqd,bhkd->bhqk', q_blk, kf) * scale
        qpos = bi * SB_BLOCK + jnp.arange(SB_BLOCK, dtype=jnp.int32)[:, None]
        mask = key_pos < qpos
        log1m = jnp.where(mask, jax.nn.log_sigmoid(-z), 0.0)
        excl = lax.cumsum(log1m, axis=3, reverse=True) - log1m
        a = jnp.where(mask, jnp.exp(jax.nn.log_sigmoid(z) + excl), 0.0)
        return jnp.einsum('bhqk,bhkd->bhqd', a, vf)

    out = lax.map(one_block, (qb, jnp.arange(nb, dtype=jnp.int32)))
    out = out.transpose(1, 0, 3, 2, 4).reshape(b, s, h * dh)
    return out.astype(q.dtype)

def memory_cross_attention(q, mem_n, w_mem_kv):
    b, s = q.shape[:2]
    m = mem_n.shape[1]
    kv = (mem_n @ w_mem_kv).reshape(b, m, 2, X_HEADS, X_HEAD_DIM)
    mk, mv = kv[:, :, 0], kv[:, :, 1]
    scores = jnp.einsum('bshd,bmhd->bhsm', q.astype(jnp.float32), mk.astype(jnp.float32))
    p = jax.nn.softmax(scores / float(np.sqrt(X_HEAD_DIM)), axis=-1)
    out = jnp.einsum('bhsm,bmhd->bshd', p, mv.astype(jnp.float32))
    return out.reshape(b, s, X_WIDTH).astype(q.dtype)

def first_inputs(seed: int = 0) -> dict:
    key = jax.random.key(seed)
    ks = jax.random.split(key, 20)
    f32 = jnp.float32

    def nrm(k, shape, fan_in):
        return jax.random.normal(k, shape, f32) * (fan_in ** -0.5)

    def gain(k, shape):
        return 1.0 + 0.02 * jax.random.normal(k, shape, f32)

    L = DEPTH
    return {
        "x": jax.random.normal(ks[0], (BATCH, SEQ, D_MODEL), f32),
        "mem": jax.random.normal(ks[1], (BATCH, MEM_LEN, D_MODEL), f32),
        "norm_mix_pre": gain(ks[2], (L, D_MODEL)),
        "w_in": nrm(ks[3], (L, D_MODEL, IN_WIDTH), D_MODEL),
        "w_pool_mix": nrm(ks[4], (L, POOL_GROUPS, POOL_GROUP_DIM, POOL_GROUP_DIM), POOL_GROUP_DIM),
        "pool_scale": gain(ks[5], (L, POOL_WIDTH)),
        "w_pool_o": nrm(ks[6], (L, POOL_WIDTH, D_MODEL), POOL_WIDTH),
        "w_sb_o": nrm(ks[7], (L, SB_WIDTH, D_MODEL), SB_WIDTH),
        "norm_mem": gain(ks[8], (L, D_MODEL)),
        "w_mem_kv": nrm(ks[9], (L, D_MODEL, 2 * X_WIDTH), D_MODEL),
        "w_x_o": nrm(ks[10], (L, X_WIDTH, D_MODEL), X_WIDTH),
        "w_out": nrm(ks[11], (L, D_MODEL, D_MODEL), D_MODEL),
        "norm_mix_post": gain(ks[12], (L, D_MODEL)),
        "norm_ffn_pre": gain(ks[13], (L, D_MODEL)),
        "w_ffn_in": nrm(ks[14], (L, D_MODEL, 2 * D_FF), D_MODEL),
        "w_ffn_out": nrm(ks[15], (L, D_FF, D_MODEL), D_FF),
        "norm_ffn_post": gain(ks[16], (L, D_MODEL)),
    }

def first_block(x, mem, norm_mix_pre, w_in, w_pool_mix, pool_scale, w_pool_o, w_sb_o,
              norm_mem, w_mem_kv, w_x_o, w_out, norm_mix_post, norm_ffn_pre,
              w_ffn_in, w_ffn_out, norm_ffn_post):
    b, s, d = x.shape
    h = x
    for l in range(DEPTH):
        n = rmsnorm(h, norm_mix_pre[l])
        proj = n @ w_in[l]
        o0 = POOL_WIDTH
        o1 = o0 + 3 * SB_WIDTH
        o2 = o1 + X_WIDTH
        p_in = proj[..., :o0]
        qkv = proj[..., o0:o1].reshape(b, s, 3, SB_HEADS, SB_HEAD_DIM)
        xq = proj[..., o1:o2].reshape(b, s, X_HEADS, X_HEAD_DIM)
        gates = jax.nn.sigmoid(proj[..., o2:].astype(jnp.float32)).reshape(b, s, N_BRANCHES, d)

        y_pool = pool_mixer(p_in, w_pool_mix[l], pool_scale[l]) @ w_pool_o[l]
        y_sb = stick_breaking_attention(qkv[:, :, 0], qkv[:, :, 1], qkv[:, :, 2]) @ w_sb_o[l]
        mem_n = rmsnorm(mem, norm_mem[l])
        y_x = memory_cross_attention(xq, mem_n, w_mem_kv[l]) @ w_x_o[l]

        merged = (gates[:, :, 0] * y_pool.astype(jnp.float32)
                  + gates[:, :, 1] * y_sb.astype(jnp.float32)
                  + gates[:, :, 2] * y_x.astype(jnp.float32)).astype(h.dtype)
        h = h + rmsnorm(merged @ w_out[l], norm_mix_post[l])

        n2 = rmsnorm(h, norm_ffn_pre[l])
        gu = n2 @ w_ffn_in[l]
        ff = (jax.nn.silu(gu[..., :D_FF]) * gu[..., D_FF:]) @ w_ffn_out[l]
        h = h + rmsnorm(ff, norm_ffn_post[l])
    return h


HEAD_DIM = 64
MOBA_HEADS = 8
MOBA_BLOCK = 256
MOBA_TOPK = 3
DSA_HEADS = 8
DSA_MAX_TOPK = 256
IDX_HEADS = 8
IDX_DIM = 64
N_GROUPS = 4
EXPERTS_PER_GROUP = 8
N_EXPERTS = N_GROUPS * EXPERTS_PER_GROUP
EXPERT_TOPK = 2
EXPERT_FF = 512
DISPATCH_BLOCK = 256
Q_CHUNK = 128
ROPE_THETA = 10000.0
NEG = -1e30

MOBA_WIDTH = MOBA_HEADS * HEAD_DIM
DSA_WIDTH = DSA_HEADS * HEAD_DIM
IDX_SCALE = (IDX_HEADS * IDX_DIM) ** -0.5
IN_SIZES = (MOBA_WIDTH,) * 3 + (DSA_WIDTH,) * 3 + (IDX_HEADS * IDX_DIM, IDX_DIM, IDX_HEADS, D_MODEL, D_MODEL)
IN_COLS = sum(IN_SIZES)
SPLIT_POINTS = tuple(int(v) for v in np.cumsum(IN_SIZES)[:-1])


def rms_norm(x, g):
    xf = x.astype(jnp.float32)
    y = xf * lax.rsqrt(jnp.mean(xf * xf, axis=-1, keepdims=True) + RMS_EPS)
    return (y * g.astype(jnp.float32)).astype(x.dtype)

def rope(x):
    s, d = x.shape[1], x.shape[-1]
    inv = jnp.power(ROPE_THETA, -jnp.arange(0, d, 2, dtype=jnp.float32) / d)
    ang = jnp.arange(s, dtype=jnp.float32)[:, None] * inv[None, :]
    ang = ang.reshape((s,) + (1,) * (x.ndim - 3) + (d // 2,))
    cos, sin = jnp.cos(ang), jnp.sin(ang)
    x1, x2 = jnp.split(x.astype(jnp.float32), 2, axis=-1)
    return jnp.concatenate([x1 * cos - x2 * sin, x1 * sin + x2 * cos], axis=-1).astype(x.dtype)

def masked_softmax(scores, mask):
    return jax.nn.softmax(jnp.where(mask, scores.astype(jnp.float32), NEG), axis=-1)

def moba_attend(q, k, v):
    h, s, d = q.shape
    nb = -(-s // MOBA_BLOCK)
    pad = nb * MOBA_BLOCK - s
    kb = jnp.pad(k, ((0, 0), (0, pad), (0, 0))).reshape(h, nb, MOBA_BLOCK, d)
    vb = jnp.pad(v, ((0, 0), (0, pad), (0, 0))).reshape(h, nb, MOBA_BLOCK, d)
    n_sel = max(1, min(MOBA_TOPK, nb - 1))
    own = jnp.arange(s) // MOBA_BLOCK
    k_mean = jnp.mean(kb.astype(jnp.float32), axis=2)
    gate = jnp.einsum('hsd,hnd->hsn', q.astype(jnp.float32), k_mean)
    past = jnp.arange(nb)[None, :] < own[:, None]
    gate = jnp.where(past[None], gate, NEG)
    _, sel = lax.top_k(gate, n_sel)
    sel_ok = sel < own[None, :, None]
    n_chunks = s // Q_CHUNK
    qc = q.reshape(h, n_chunks, Q_CHUNK, d).transpose(1, 0, 2, 3)
    selc = sel.reshape(h, n_chunks, Q_CHUNK, n_sel).transpose(1, 0, 2, 3)
    okc = sel_ok.reshape(h, n_chunks, Q_CHUNK, n_sel).transpose(1, 0, 2, 3)
    scale = d ** -0.5
    head_ix = jnp.arange(h)[:, None, None]

    def one_chunk(args):
        qi, si, oki, c = args
        q_pos = c * Q_CHUNK + jnp.arange(Q_CHUNK)
        blk = (c * Q_CHUNK) // MOBA_BLOCK
        k_sel = kb[head_ix, si]
        v_sel = vb[head_ix, si]
        k_own = lax.dynamic_index_in_dim(kb, blk, axis=1, keepdims=False)
        v_own = lax.dynamic_index_in_dim(vb, blk, axis=1, keepdims=False)
        s_sel = jnp.einsum('hqd,hqnkd->hqnk', qi, k_sel).reshape(h, Q_CHUNK, n_sel * MOBA_BLOCK) * scale
        s_own = jnp.einsum('hqd,hkd->hqk', qi, k_own) * scale
        m_sel = jnp.broadcast_to(oki[..., None], oki.shape + (MOBA_BLOCK,)).reshape(h, Q_CHUNK, n_sel * MOBA_BLOCK)
        k_pos = blk * MOBA_BLOCK + jnp.arange(MOBA_BLOCK)
        m_own = jnp.broadcast_to((k_pos[None, :] <= q_pos[:, None])[None], (h, Q_CHUNK, MOBA_BLOCK))
        p = masked_softmax(jnp.concatenate([s_sel, s_own], axis=-1),
                           jnp.concatenate([m_sel, m_own], axis=-1)).astype(v.dtype)
        p_sel = p[..., :n_sel * MOBA_BLOCK].reshape(h, Q_CHUNK, n_sel, MOBA_BLOCK)
        p_own = p[..., n_sel * MOBA_BLOCK:]
        return (jnp.einsum('hqnk,hqnkd->hqd', p_sel, v_sel)
                + jnp.einsum('hqk,hkd->hqd', p_own, v_own))

    out = lax.map(one_chunk, (qc, selc, okc, jnp.arange(n_chunks)))
    return out.transpose(1, 0, 2, 3).reshape(h, s, d)

def dsa_attend(q, k, v, q_idx, k_idx, w_idx):
    h, s, d = q.shape
    top = min(DSA_MAX_TOPK, s // 4)
    n_chunks = s // Q_CHUNK
    qc = q.reshape(h, n_chunks, Q_CHUNK, d).transpose(1, 0, 2, 3)
    qic = q_idx.reshape(n_chunks, Q_CHUNK, IDX_HEADS, IDX_DIM)
    wic = w_idx.reshape(n_chunks, Q_CHUNK, IDX_HEADS)
    k_pos = jnp.arange(s)
    kf = k_idx.astype(jnp.float32)
    scale = d ** -0.5

    def one_chunk(args):
        qi, qii, wi, c = args
        q_pos = c * Q_CHUNK + jnp.arange(Q_CHUNK)
        logits = jnp.einsum('qhd,sd->qhs', qii.astype(jnp.float32), kf)
        score = jnp.einsum('qh,qhs->qs', wi.astype(jnp.float32), jax.nn.relu(logits))
        score = jnp.where(k_pos[None, :] <= q_pos[:, None], score, NEG)
        _, idx = lax.top_k(score, top)
        ok = idx <= q_pos[:, None]
        k_sel = k[:, idx]
        v_sel = v[:, idx]
        sc = jnp.einsum('hqd,hqkd->hqk', qi, k_sel) * scale
        p = masked_softmax(sc, ok[None]).astype(v.dtype)
        return jnp.einsum('hqk,hqkd->hqd', p, v_sel)

    out = lax.map(one_chunk, (qc, qic, wic, jnp.arange(n_chunks)))
    return out.transpose(1, 0, 2, 3).reshape(h, s, d)

def hier_moe(h, w_group, b_group, w_expert, b_expert, w1, w3, w2):
    b, s, d = h.shape
    t = b * s
    xt = h.reshape(t, d)
    g_logit = (xt @ w_group + b_group).astype(jnp.float32)
    g_prob = jax.nn.softmax(g_logit, axis=-1)
    g_sel = jnp.argmax(g_logit, axis=-1)
    g_w = jnp.take_along_axis(g_prob, g_sel[:, None], axis=1)
    e_logit = (xt @ w_expert + b_expert).astype(jnp.float32).reshape(t, N_GROUPS, EXPERTS_PER_GROUP)
    e_logit = jnp.take_along_axis(e_logit, g_sel[:, None, None], axis=1)[:, 0]
    top_p, top_i = lax.top_k(jax.nn.softmax(e_logit, axis=-1), EXPERT_TOPK)
    gate = g_w * top_p / jnp.sum(top_p, axis=-1, keepdims=True)
    expert = g_sel[:, None] * EXPERTS_PER_GROUP + top_i
    n_asg = t * EXPERT_TOPK
    e_flat = expert.reshape(-1)
    order = jnp.argsort(e_flat)
    e_sorted = e_flat[order]
    tok_sorted = order // EXPERT_TOPK
    gate_sorted = gate.reshape(-1)[order].astype(h.dtype)
    counts = jnp.bincount(e_flat, length=N_EXPERTS)
    padded = (counts + DISPATCH_BLOCK - 1) // DISPATCH_BLOCK * DISPATCH_BLOCK
    ends = jnp.cumsum(padded)
    starts_pad = ends - padded
    starts = jnp.cumsum(counts) - counts
    dest = starts_pad[e_sorted] + jnp.arange(n_asg) - starts[e_sorted]
    n_blocks = -(-n_asg // DISPATCH_BLOCK) + N_EXPERTS
    xs = jnp.zeros((n_blocks * DISPATCH_BLOCK, d), h.dtype).at[dest].set(xt[tok_sorted])
    block_expert = jnp.minimum(
        jnp.searchsorted(ends, jnp.arange(n_blocks) * DISPATCH_BLOCK, side='right'), N_EXPERTS - 1)

    def expert_block(args):
        xb, e = args
        hid = jax.nn.silu(xb @ w1[e]) * (xb @ w3[e])
        return hid @ w2[e]

    ys = lax.map(expert_block, (xs.reshape(n_blocks, DISPATCH_BLOCK, d), block_expert)).reshape(-1, d)
    out = jax.ops.segment_sum(ys[dest] * gate_sorted[:, None], tok_sorted, num_segments=t)
    return out.reshape(b, s, d)

def hybrid_layer(x, g_mix, w_in, w_proj_a, w_proj_b, w_out, g_ffn,
                 w_group, b_group, w_expert, b_expert, w1, w3, w2):
    b, s, _ = x.shape
    h = rms_norm(x, g_mix)
    qa, ka, va, qb, kb, vb, qi, ki, wi, ga, gb = jnp.split(h @ w_in, SPLIT_POINTS, axis=-1)

    def heads(t, n):
        return t.reshape(b, s, n, HEAD_DIM)

    qa = rope(heads(qa, MOBA_HEADS)).transpose(0, 2, 1, 3)
    ka = rope(heads(ka, MOBA_HEADS)).transpose(0, 2, 1, 3)
    va = heads(va, MOBA_HEADS).transpose(0, 2, 1, 3)
    qb = rope(heads(qb, DSA_HEADS)).transpose(0, 2, 1, 3)
    kb = rope(heads(kb, DSA_HEADS)).transpose(0, 2, 1, 3)
    vb = heads(vb, DSA_HEADS).transpose(0, 2, 1, 3)
    qi = rope(qi.reshape(b, s, IDX_HEADS, IDX_DIM))
    ki = rope(ki)
    wi = wi * IDX_SCALE
    o_a = lax.map(lambda a: moba_attend(*a), (qa, ka, va))
    o_b = lax.map(lambda a: dsa_attend(*a), (qb, kb, vb, qi, ki, wi))
    o_a = o_a.transpose(0, 2, 1, 3).reshape(b, s, MOBA_WIDTH)
    o_b = o_b.transpose(0, 2, 1, 3).reshape(b, s, DSA_WIDTH)
    mixed = jax.nn.sigmoid(ga) * (o_a @ w_proj_a) + jax.nn.sigmoid(gb) * (o_b @ w_proj_b)
    x = x + mixed @ w_out
    x = x + hier_moe(rms_norm(x, g_ffn), w_group, b_group, w_expert, b_expert, w1, w3, w2)
    return x

def second_inputs(seed: int = 0) -> dict:
    key = jax.random.key(seed)
    ks = jax.random.split(key, 16)
    nrm = jax.random.normal
    f32 = jnp.float32
    return {
        "x": nrm(ks[0], (BATCH, SEQ, D_MODEL), f32),
        "g_mix": 1.0 + 0.02 * nrm(ks[1], (DEPTH, D_MODEL), f32),
        "w_in": nrm(ks[2], (DEPTH, D_MODEL, IN_COLS), f32) * D_MODEL ** -0.5,
        "w_proj_a": nrm(ks[3], (DEPTH, MOBA_WIDTH, D_MODEL), f32) * MOBA_WIDTH ** -0.5,
        "w_proj_b": nrm(ks[4], (DEPTH, DSA_WIDTH, D_MODEL), f32) * DSA_WIDTH ** -0.5,
        "w_out": nrm(ks[5], (DEPTH, D_MODEL, D_MODEL), f32) * D_MODEL ** -0.5,
        "g_ffn": 1.0 + 0.02 * nrm(ks[6], (DEPTH, D_MODEL), f32),
        "w_group": nrm(ks[7], (DEPTH, D_MODEL, N_GROUPS), f32) * D_MODEL ** -0.5,
        "b_group": 0.01 * nrm(ks[8], (DEPTH, N_GROUPS), f32),
        "w_expert": nrm(ks[9], (DEPTH, D_MODEL, N_EXPERTS), f32) * D_MODEL ** -0.5,
        "b_expert": 0.01 * nrm(ks[10], (DEPTH, N_EXPERTS), f32),
        "w1": nrm(ks[11], (DEPTH, N_EXPERTS, D_MODEL, EXPERT_FF), f32) * D_MODEL ** -0.5,
        "w3": nrm(ks[12], (DEPTH, N_EXPERTS, D_MODEL, EXPERT_FF), f32) * D_MODEL ** -0.5,
        "w2": nrm(ks[13], (DEPTH, N_EXPERTS, EXPERT_FF, D_MODEL), f32) * EXPERT_FF ** -0.5,
        "g_final": 1.0 + 0.02 * nrm(ks[14], (D_MODEL,), f32),
    }

def second_block(x, g_mix, w_in, w_proj_a, w_proj_b, w_out, g_ffn,
              w_group, b_group, w_expert, b_expert, w1, w3, w2, g_final):
    for l in range(DEPTH):
        x = hybrid_layer(x, g_mix[l], w_in[l], w_proj_a[l], w_proj_b[l], w_out[l], g_ffn[l],
                         w_group[l], b_group[l], w_expert[l], b_expert[l], w1[l], w3[l], w2[l])
    return rms_norm(x, g_final)


def setup_inputs(seed=0):
    out = dict(first_inputs(seed))
    for name, value in second_inputs(seed + 1).items():
        if name != "x":
            out[name + "_2"] = value
    return out


def reference(
    x, mem, norm_mix_pre, w_in, w_pool_mix, pool_scale, w_pool_o, w_sb_o, norm_mem, w_mem_kv,
    w_x_o, w_out, norm_mix_post, norm_ffn_pre, w_ffn_in, w_ffn_out, norm_ffn_post, g_mix_2,
    w_in_2, w_proj_a_2, w_proj_b_2, w_out_2, g_ffn_2, w_group_2, b_group_2, w_expert_2,
    b_expert_2, w1_2, w3_2, w2_2, g_final_2,
):
    x = first_block(
        x, mem, norm_mix_pre, w_in, w_pool_mix, pool_scale, w_pool_o, w_sb_o, norm_mem,
        w_mem_kv, w_x_o, w_out, norm_mix_post, norm_ffn_pre, w_ffn_in, w_ffn_out, norm_ffn_post,
    )
    return second_block(
        x, g_mix_2, w_in_2, w_proj_a_2, w_proj_b_2, w_out_2, g_ffn_2, w_group_2, b_group_2,
        w_expert_2, b_expert_2, w1_2, w3_2, w2_2, g_final_2,
    )


_drawn_inputs = setup_inputs


def setup_inputs(seed=0):
    import zlib

    import numpy as np

    out = dict(_drawn_inputs(seed))
    spreads = {}
    factors = {'pool_scale': 2.792,
     'norm_mem': 6.942,
     'norm_ffn_post': 3.063,
     'g_mix_2': 4.26,
     'g_ffn_2': 4.033,
     'b_group_2': 8.0,
     'b_expert_2': 16.01,
     'g_final_2': 8.093}
    for name, (base, spread) in spreads.items():
        noise = np.random.default_rng([zlib.crc32(name.encode()), seed]).standard_normal(out[name].shape)
        drawn = base * np.exp(spread * noise) if base else spread * noise
        out[name] = __import__('jax').numpy.asarray(drawn.astype(out[name].dtype))
    for name, factor in factors.items():
        out[name] = (out[name] * factor).astype(out[name].dtype)
    return out
```

```python
import numpy as np
import concourse.bass as bass
from concourse import mybir

F32 = mybir.dt.float32
F32R = mybir.dt.float32r
I32 = mybir.dt.int32
ACT = mybir.ActivationFunctionType
ALU = mybir.AluOpType
AX = mybir.AxisListType

P = 128
T = 256
TB = T // P
D = 1024
KC = D // P
DH = 64
HEADS = 8
X_HEADS = 4
FF = 2816
UNIT = 2048
UC = 256
EPS = 1e-6
NEG = -1e30
TAKEN = -3e38
TOPK = T // 4
GROUPS, PER_GROUP = 4, 8
EXPERTS = GROUPS * PER_GROUP
EFF = 512
SLOTS = 32
QUAD = 4
WINDOWS = (2, 4, 8, 16)
CAUSAL = P + T

TABLE = {}
_at = 0
for _name, _n in (("ident", P), ("later", P), ("before", P), ("rotate", P), ("keep", CAUSAL), ("hide", CAUSAL),
                  ("cos", 2 * T), ("sin", 2 * T), ("slot", SLOTS), ("rev", EXPERTS), ("revg", GROUPS), ("steps", 8)):
    TABLE[_name] = (_at, _at + _n)
    _at += _n
TABLE_W = _at


def make_table():
    t = np.zeros((P, TABLE_W), np.float32)

    def put(name, value):
        a, b = TABLE[name]
        t[:, a:b] = value

    i, j = np.arange(P)[:, None], np.arange(P)[None, :]
    put("ident", i == j)
    put("later", i > j)
    put("before", i < j)
    rot = np.zeros((P, P), np.float32)
    for p in range(P):
        if p % DH < DH // 2:
            rot[p + DH // 2, p] = -1.0
        else:
            rot[p - DH // 2, p] = 1.0
    put("rotate", rot)
    put("keep", np.concatenate([i < j, np.ones((P, P)), i < j], 1))
    put("hide", np.where(np.concatenate([j <= i, np.ones((P, P), bool), j <= i], 1), 0.0, NEG))
    inv = np.power(np.float32(10000.0), -np.arange(0, DH, 2, dtype=np.float32) / np.float32(DH))
    ang = (np.arange(T, dtype=np.float32)[None, :] * inv[np.arange(P) % (DH // 2)][:, None]).astype(np.float32)
    put("cos", np.tile(np.cos(ang), (1, 2)))
    put("sin", np.tile(np.sin(ang), (1, 2)))
    put("slot", np.arange(SLOTS)[None, :])
    put("rev", EXPERTS - np.arange(EXPERTS)[None, :])
    put("revg", GROUPS - np.arange(GROUPS)[None, :])
    put("steps", SLOTS * np.arange(8)[None, :])
    return t


def make_windows():
    b = np.zeros((P, len(WINDOWS), CAUSAL), np.float32)
    for g, w in enumerate(WINDOWS):
        full = np.zeros((T, T), np.float32)
        for t in range(T):
            lo = max(t + 1 - w, 0)
            full[lo:t + 1, t] = np.float32(1.0) / np.float32(t + 1 - lo)
            full[t, t] -= 1.0
        b[:, g, 0:T] = full[0:P, :]
        b[:, g, T:CAUSAL] = full[P:T, P:T]
    return b


def unit_plan(a):
    units = []

    def add(name, w, c0, kc=KC, cols=UC, k0=0, **more):
        src = w[k0 * P:(k0 + kc) * P, c0:c0 + cols].rearrange("(c p) n -> p c n", p=P)
        units.append(dict(name=name, src=[(0, cols, src)], kc=kc, cols=cols, **more))

    kv, w_in = a["w_mem_kv"][0], a["w_in"][0]
    add("mk", kv, 0, form="B")
    add("mv", kv, UC, form="A")
    for name, c0, n, f in (("p", 0, 2, "A"), ("q", 512, 2, "B"), ("k", 1024, 2, "B"), ("v", 1536, 2, "A"),
                           ("xq", 2048, 1, "B")):
        for j in range(n):
            add(name, w_in, c0 + UC * j, form=f, j=j)
    for j in range(12):
        add("gate", w_in, 2304 + UC * j, form="B", j=j)
    for j in range(4):
        for b, (w, kc, o0) in enumerate((("w_pool_o", 4, 0), ("w_sb_o", 4, 4), ("w_x_o", 2, 8))):
            add("merge", a[w][0], UC * j, kc=kc, form="B", j=j, b=b, o0=o0, last=b == 2)
    for j in range(4):
        add("out", a["w_out"][0], UC * j, form="A", j=j)
    up, down = a["w_ffn_in"][0], a["w_ffn_out"][0]

    def add_down(i):
        src = down[i * UC:(i + 1) * UC, :].rearrange("(c p) n -> p c n", p=P)
        units.append(dict(name="down", src=[(0, D, src)], kc=2, cols=D, form="F", i=i))

    for i in range(FF // UC):
        add("g", up, UC * i, form="B", i=i)
        add("u", up, FF + UC * i, form="B", i=i)
        if i:
            add_down(i - 1)
    add_down(FF // UC - 1)
    w2 = a["w_in_2"][0]
    src = w2.rearrange("(c p) n -> p c n", p=P)
    units.append(dict(name="kiwi", kc=KC, cols=136, form="K",
                      src=[(0, DH, src[:, :, 3584:3584 + DH]), (DH, 136, src[:, :, 3584:3656])]))
    for name, c0, f in (("qi", 3072, "B"), ("kb", 2048, "B"), ("qb", 1536, "B"), ("vb", 2560, "A"),
                        ("ka", 512, "B"), ("qa", 0, "B"), ("va", 1024, "A")):
        for j in range(2):
            add(name, w2, c0 + UC * j, form=f, j=j)
    for j in range(8):
        add("gate2", w2, 3656 + UC * j, form="B", j=j)
    for j in range(4):
        for b, (w, o0) in enumerate((("w_proj_a_2", 0), ("w_proj_b_2", 4))):
            add("merge", a[w][0], UC * j, kc=4, form="B", j=j, b=b, o0=o0, last=b == 1)
    for j in range(4):
        add("out2", a["w_out_2"][0], UC * j, form="A", j=j)
    return units


ROPED = ("kiwi", "qi", "kb", "qb", "ka", "qa")
BY_VECTOR = ("merge", "u", "out2")


def step_plan(units):
    first = {}
    for u, unit in enumerate(units):
        first.setdefault(unit["name"], u)
    plan = []
    ropes = 0
    topk = 0

    def unit(u):
        plan.append(("unit", u))

    plan.append(("vectors",))
    plan.append(("norm", 0))
    unit(0)
    unit(1)
    plan.append(("norm", 1))
    for u in range(2, 11):
        unit(u)
        if u == 5:
            plan.append(("pool_window",))
        if u == 7:
            plan.append(("pool_mix",))
    for k in range(12):
        unit(first["gate"] + k)
        plan.append(("head", k, 0, 12))
    plan.append(("head", 12, 0, 12))
    plan.append(("head", 13, 0, 12))
    for u in range(first["merge"], first["merge"] + 12):
        unit(u)
    for u in range(first["out"], first["out"] + 4):
        unit(u)
    plan.append(("post", 0))
    plan.append(("norm", 2))
    plan.append(("ffn",))
    plan.append(("post", 1))
    plan.append(("norm", 3))
    waiting = []
    for u in range(first["kiwi"], first["gate2"]):
        unit(u)
        if waiting:
            plan.append(("rope", *waiting.pop()))
        if units[u]["name"] in ROPED:
            waiting.append((ropes, u))
            ropes += 1
        if u == first["kiwi"] + 3:
            plan.append(("index",))
        if u >= first["kiwi"] + 4 and topk < TOPK // 8:
            plan.append(("topk", topk))
            topk += 1
    assert not waiting and topk == TOPK // 8
    for k in range(8):
        unit(first["gate2"] + k)
        if k == 2:
            plan.append(("select",))
        plan.append(("head", 12 + 2 * k, 12, 28))
        plan.append(("head", 13 + 2 * k, 12, 28))
    plan.append(("head", 28, 12, 28))
    plan.append(("head", 29, 12, 28))
    start = first["gate2"] + 8
    for u in range(start, start + 12):
        unit(u)
    return plan


def layers_kernel(nc, a, table, windows, out):
    units = unit_plan(a)
    plan = step_plan(units)
    U = len(units)
    G0 = next(u for u, x in enumerate(units) if x["name"] == "g")
    NF = FF // UC
    assert all(x["form"] != "F" or len(x["src"]) == 1 for x in units)

    base = -(-nc.sbuf_base // 64) * 64
    at = base

    def put(name, shape, dt, where=None):
        nonlocal at
        size = 4 * int(np.prod(shape[1:]))
        t = nc.alloc_sbuf_tensor_at(name, shape, dt, offset=at if where is None else where)
        if where is None:
            at += -(-size // 32) * 32
        return t

    SLOT_B = 4 * UNIT
    arena_at = at
    arena = put("arena", [P, 12, UNIT], F32)
    split_at = at
    w_hi = put("w_hi", [P, 3, UNIT], F32R)
    w_lo = put("w_lo", [P, 3, UNIT], F32R)
    split_end = at
    x_hi = put("x_hi", [P, KC, T], F32R)
    x_lo = put("x_lo", [P, KC, T], F32R)
    o_hi = put("o_hi", [P, 10, T], F32R)
    o_lo = put("o_lo", [P, 10, T], F32R)
    h = put("h", [P, TB, D], F32)
    gain_row = put("gain_row", [P, D], F32)
    tab = put("tab", [P, TABLE_W], F32)
    vec = put("vec", [P, 36], F32)
    ones = put("ones", [P, P], F32)
    stat = put("stat", [P, 16], F32)
    softmax = put("softmax", [P, 16], F32)
    index_w = put("index_w", [P, TB, 8], F32)
    best8 = put("best8", [P, TB, 8], F32)
    passes_i = put("passes_i", [P, 1], I32)
    assert at <= nc.sbuf_usable_end, (at, nc.sbuf_usable_end)

    def const(name):
        lo, hi = TABLE[name]
        return tab[:, lo:hi]

    ident = const("ident")

    temp_at = arena_at + 3 * SLOT_B
    temp_end = arena_at + 12 * SLOT_B
    where = temp_at

    def temp(name, shape, dt=F32, at_=None):
        nonlocal where
        if at_ is None:
            at_ = where
            where += 4 * int(np.prod(shape[1:]))
            assert where <= temp_end, name
        return nc.alloc_sbuf_tensor_at(name, shape, dt, offset=at_)

    hw = [[temp(f"head_{n}{i}", [P, 2 * T]) for i in range(2)] for n in ("score", "prob", "expo", "right")]
    score_b, prob_b, expo_b, right_b = hw
    heads_end = where
    p_tok = temp("p_tok", [P, TB, 512])
    q1 = temp("q1", [P, 4, T])
    k1 = temp("k1", [P, 4, T])
    v1 = temp("v1", [P, TB, 512])
    xq = temp("xq", [P, 2, T])
    mk = temp("mk", [P, 2, T])
    mv = temp("mv", [P, TB, T])
    gates_at = where
    gates = temp("gates", [P, 24, T])
    win = temp("win", [P, 4, CAUSAL])
    pool_w_sb = temp("pool_w_sb", [P, 4, P])
    mixed = temp("mixed", [P, 4, T], at_=gates_at + 16384)
    normed = temp("normed", [P, TB, D], at_=gates_at)
    mem_tok = temp("mem_tok", [P, TB, D], at_=gates_at + 8192)
    rows = temp("rows", [36, P], at_=gates_at + 16384 + 4096)
    y_tok = temp("y_tok", [P, TB, D], at_=gates_at + 8192)
    silu_g = temp("silu_g", [P, 2 * T], at_=heads_end)
    act_f = temp("act_f", [P, 2 * T], at_=heads_end + 2048)
    where = heads_end
    qi, kb, qb, ka, qa = (temp(n, [P, 4, T]) for n in ("qi", "kb", "qb", "ka", "qa"))
    vb, va = (temp(n, [P, TB, 512]) for n in ("vb", "va"))
    ki = temp("ki", [P, T])
    score = temp("score", [P, CAUSAL])
    work = temp("work", [P, CAUSAL])
    gates2_at = arena_at + 10 * SLOT_B
    assert where <= gates2_at
    where = gates2_at
    gates2 = temp("gates2", [P, 16, T])
    normed2 = temp("normed2", [P, TB, D], at_=gates2_at)

    mo = split_at

    def moe(name, shape, dt=F32):
        nonlocal mo
        t = nc.alloc_sbuf_tensor_at(name, shape, dt, offset=mo)
        mo += -(-4 * int(np.prod(shape[1:])) // 32) * 32
        assert mo <= split_end, name
        return t

    n3 = moe("n3", [P, TB, D])
    n3T = moe("n3T", [P, KC, T])
    w_route = moe("w_route", [P, KC, 36])
    b_route = moe("b_route", [P, 36])
    logits = moe("logits", [P, TB, 36])
    exp_in = moe("exp_in", [P, TB, 36])
    exp_out = moe("exp_out", [P, TB, 36])
    masked_e = moe("masked_e", [P, TB, EXPERTS])
    pick = moe("pick", [P, TB, EXPERTS])
    pick_one = moe("pick_one", [P, TB, EXPERTS])
    pick_g = moe("pick_g", [P, TB, GROUPS])
    r_s = moe("r_s", [P, 16, TB])
    chosen = moe("chosen", [P, TB, EXPERTS])
    gate_e = moe("gate_e", [P, TB, EXPERTS])
    rank = moe("rank", [P, TB, EXPERTS])
    slot_no = moe("slot_no", [P, SLOTS])
    one_hot = moe("one_hot", [P, TB, P])
    gated_hot = moe("gated_hot", [P, TB, P])
    gate_T = moe("gate_T", [P, T])
    xg = moe("xg", [P, KC, P])
    silu_e = moe("silu_e", [P, P])
    hid = moe("hid", [P, P])
    hid_T = moe("hid_T", [P, P])
    y_quad = moe("y_quad", [P, D])

    ps = nc.alloc_psum_tensor("ps", [P, 8, 512], F32)

    bank_of, bank_before = {}, {}
    turn, last_in = 0, {}
    for u, x in enumerate(units):
        if x["form"] == "F":
            continue
        bank = {"g": 0, "u": 1}.get(x["name"], turn % 2)
        turn = bank + 1
        bank_of[u], bank_before[u] = bank, last_in.get(bank)
        last_in[bank] = u
    rope_of = {u: r for r, u in enumerate(u for u, x in enumerate(units) if x["name"] in ROPED)}
    SLOT_OF = ((6, 8, 10), (4, 0, 2))

    def sem(name):
        return nc.alloc_semaphore(name)

    landed = [sem(f"unit_landed{i}") for i in range(3)]
    hi_ready, lo_ready = sem("w_hi_ready"), sem("w_lo_ready")
    unit_done = sem("unit_done")
    out_act, out_dve = sem("unit_out_act"), sem("unit_out_dve")
    in_x, in_mem, in_rows, in_table, in_win, in_mix, in_gain = (
        sem(f"in_{n}") for n in ("x", "mem", "rows", "table", "windows", "mix", "gain"))
    gain_used = sem("gain_used")
    vec_T, vec_ready = sem("vec_T"), sem("vec_ready")
    sq_done, mean_done, root_done, normed_done = (sem(n) for n in ("sq_done", "mean_done", "root_done",
                                                                  "normed_done"))
    norm_T, x_ready = sem("norm_T"), sem("x_ready")
    pool_w, pool_mixed, pool_p, pool_out = (sem(n) for n in ("pool_w", "pool_mixed", "pool_p", "pool_out"))
    z_done, prep_done, exp_done, mid_ready, mid_done, expo_ready, a_done, right_ready, o_done, pair_out = (
        sem(n) for n in ("z_done", "prep_done", "exp_done", "mid_ready", "mid_done", "expo_ready", "a_done",
                         "right_ready", "o_done", "pair_out"))
    merged_ready = sem("merged_ready")
    act_hi, act_ready = sem("ffn_act_hi"), sem("ffn_act_ready")
    rot_done, rope_done, wi_T = sem("rot_done"), sem("rope_done"), sem("wi_out")
    ix_z, ix_relu, ix_acc = sem("index_z"), sem("index_relu"), sem("index_acc")
    select_done = sem("select_done")
    act_chain, dve_chain = sem("act_chain"), sem("dve_chain")
    in_route, n3_ready, n3_T, n3_out = sem("in_route"), sem("n3_ready"), sem("n3_T"), sem("n3T_ready")
    logit_done, route_sel, rank_done, passes_ready = (sem(n) for n in ("logit_done", "route_sel", "rank_done",
                                                                       "passes_ready"))
    w_up = [sem("e_w1a"), sem("e_w1b")]
    w_gate3 = [sem("e_w3a"), sem("e_w3b")]
    w_down = [sem("e_w2a"), sem("e_w2b")]
    route_in, route_exp = sem("route_in"), sem("route_exp")
    xg_part, hot_part, slot_moved = sem("xg_part"), sem("hot_part"), sem("slot_moved")
    hot_ready, xg_done, xg_ready, gt_done, gt_ready = (sem(n) for n in ("hot_ready", "xg_done", "xg_ready",
                                                                        "gt_done", "gt_ready"))
    e_up, e_silu, e_hid, e_T, e_hidT, e_y, e_yA, e_yD = (sem(n) for n in (
        "e_up", "e_silu", "e_hid", "e_T", "e_hidT", "e_y", "e_y_act", "e_y_dve"))
    comb_done, comb_added = sem("comb_done"), sem("comb_added")
    fin_ready, fin_out = sem("final_ready"), sem("final_out")

    def landings(u):
        return 16 * sum(len(units[v]["src"]) for v in range(u % 3, u + 1, 3))

    def outs(u, vector):
        return sum((x["name"] in BY_VECTOR) == vector for x in units[:u + 1] if x["form"] != "F")

    def wait_out(eng, u):
        if units[u]["name"] in BY_VECTOR:
            eng.wait_ge(out_dve, outs(u, True))
        else:
            eng.wait_ge(out_act, outs(u, False))

    def kind(k):
        return "sb" if k < 8 else "x" if k < 12 else "moba" if k < 20 else "dsa"

    def pair_slot(k):
        return 4 + k // 2 if k < 12 else (k - 12) // 2

    def head_in(k):
        kd = kind(k)
        j = {"sb": k, "x": k - 8, "moba": k - 12, "dsa": k - 20}[kd]
        q, kk, v = {"sb": (q1, k1, v1), "x": (xq, mk, mv), "moba": (qa, ka, va), "dsa": (qb, kb, vb)}[kd]
        p0 = DH * (j % 2)
        return q[p0:p0 + DH, j // 2, :], kk[p0:p0 + DH, j // 2, :], v[:, :, DH * j:DH * j + DH], p0

    first = {}
    for u, x in enumerate(units):
        first.setdefault(x["name"], u)
    second_merge = first["gate2"] + 8
    N_ROPE = len(rope_of)
    S2 = G0 + 2

    def ffn_loop(eng, triple):
        triple(1)
        with eng.Fori(2, NF - 1) as i:
            triple(i)
        triple(NF - 1)

    block_cm = nc.Block()
    block = block_cm.__enter__()

    @block.sync
    def _(sp):
        def load(u):
            if u >= 3:
                sp.wait_ge(lo_ready, u - 2)
            kc, cols = units[u]["kc"], units[u]["cols"]
            dst = arena[:, u % 3, 0:kc * cols].rearrange("p (c n) -> p c n", c=kc)
            for c0, c1, src in units[u]["src"]:
                sp.dma_start(dst[:, :, c0:c1], src).then_inc(landed[u % 3], 16)

        sp.dma_start(mem_tok[:, :, :], a["mem"][0].rearrange("(b p) n -> p b n", p=P)).then_inc(in_mem, 16)
        for u in range(2):
            load(u)
        sp.dma_start(h[:, :, :], a["x"][0].rearrange("(b p) n -> p b n", p=P)).then_inc(in_x, 16)
        for u in range(2, S2 + 3):
            load(u)
        up_v = a["w_ffn_in"][0].rearrange("(c p) n -> p c n", p=P)
        down_v = a["w_ffn_out"][0].rearrange("(c p) n -> p c n", p=P)
        with sp.Fori(2, NF - 1) as i:
            addresses = [sp.snap(i * UC), sp.snap(i * UC + FF), sp.snap(i * 2 - 2)]
            freed = [sp.snap(i * 3 + (S2 - 3 + j - 2)) for j in range(3)]
            for j in range(3):
                s = (S2 + j) % 3
                sp.wait_ge(lo_ready, freed[j])
                if j < 2:
                    dst = arena[:, s, :].rearrange("p (c n) -> p c n", c=KC)
                    src = up_v[:, :, bass.ds(addresses[j], UC)]
                else:
                    dst = arena[:, s, :].rearrange("p (c n) -> p c n", c=2)
                    src = down_v[:, bass.ds(addresses[j], 2), :]
                sp.dma_start(dst, src).then_inc(landed[s], 16)
        for u in range(S2 + 3 * (NF - 2), U):
            load(u)

        w1, w3, w2 = a["w1_2"][0], a["w3_2"][0], a["w2_2"][0]
        W1 = w1.rearrange("e (p c) f -> p e c f", c=KC)
        W3 = w3.rearrange("e (p c) f -> p e c f", c=KC)
        W2 = w2.rearrange("e (c p) n -> p e c n", p=P)

        def expert_load(e, odd, which):
            s, sems = {"w1": (SLOT_OF[odd][0], w_up), "w3": (SLOT_OF[odd][1], w_gate3),
                       "w2": (SLOT_OF[odd][2], w_down)}[which]
            src = {"w1": W1, "w3": W3, "w2": W2}[which]
            dst = arena[:, s:s + 2, :].rearrange("p s (c n) -> p (s c) n", c=KC // 2 if which != "w2" else 2)
            one = src[:, bass.ds(e, 1), :, :].rearrange("p e c n -> p (e c) n")
            sp.dma_start(dst, one).then_inc(sems[odd], 16)

        sp.wait_ge(o_done, 28)
        expert_load(0, 0, "w1")
        expert_load(0, 0, "w3")
        expert_load(1, 1, "w1")
        sp.wait_ge(merged_ready, 8)
        expert_load(0, 0, "w2")
        sp.wait_ge(lo_ready, U)
        expert_load(1, 1, "w3")
        expert_load(1, 1, "w2")

        def stream(pass_, lo_pair, n_pairs):
            with sp.Fori(lo_pair, n_pairs) as i:
                for odd in range(2):
                    e = sp.snap(i * 2 + odd)
                    used = sp.snap(i * 2 + (pass_ * EXPERTS + odd - 1))
                    for which in ("w1", "w3", "w2"):
                        sp.wait_ge(e_y if which == "w2" else e_up, used)
                        expert_load(e, odd, which)

        stream(0, 1, EXPERTS // 2)
        sp.wait_ge(passes_ready, 1)
        n_pass = sp.value_load(passes_i[0:1, 0:1], min_val=1, max_val=T // SLOTS)
        with sp.If(n_pass > 1):
            with sp.Fori(1, n_pass) as again:
                stream(again, 0, EXPERTS // 2)
            sp.nop()
        sp.wait_ge(fin_ready, 1)
        sp.dma_start(out[0].rearrange("(b p) n -> p b n", p=P), n3[:, :, :]).then_inc(fin_out, 16)
        sp.wait_ge(fin_out, 16)

    @block.gpsimd
    def _(pool):
        r = 0
        for name, n in (("norm_mem", 8), ("norm_mix_pre", 8), ("pool_scale", 4), ("norm_ffn_pre", 8),
                        ("g_mix_2", 8)):
            pool.dma_start(rows[r:r + n, :], a[name][0].rearrange("(r n) -> r n", n=P)).then_inc(in_rows, 16)
            r += n
        pool.dma_start(tab[:, :], table).then_inc(in_table, 16)
        pool.dma_start(win[:, :, :], windows).then_inc(in_win, 16)

        def row_load(v):
            pool.dma_start(gain_row[:, :], v.partition_broadcast(P)).then_inc(in_gain, 16)

        row_load(a["norm_mix_post"][0])
        pool.wait_ge(gain_used, 1)
        row_load(a["norm_ffn_post"][0])
        pool.wait_ge(gain_used, 2)
        row_load(a["g_ffn_2"][0])
        pool.wait_ge(unit_done, U)
        for c0, n, w, b in ((0, GROUPS, "w_group_2", "b_group_2"), (GROUPS, EXPERTS, "w_expert_2", "b_expert_2")):
            pool.dma_start(w_route[:, :, c0:c0 + n], a[w][0].rearrange("(p c) n -> p c n", c=KC))\
                .then_inc(in_route, 16)
            pool.dma_start(b_route[:, c0:c0 + n], a[b][0].partition_broadcast(P)).then_inc(in_route, 16)
        pool.wait_ge(n3_ready, 1)
        row_load(a["g_final_2"])

    @block.tensor
    def _(pe):
        mm = nc.tensor.matmul

        def three(dst, l_hi, l_lo, r_hi, r_lo, start, stop):
            mm(dst, l_hi, r_hi, start=start, stop=False)
            mm(dst, l_hi, r_lo, start=False, stop=False)
            return mm(dst, l_lo, r_hi, start=False, stop=stop)

        def unit(u):
            x = units[u]
            kc, cols, s = x["kc"], x["cols"], u % 3
            hi = w_hi[:, s, 0:kc * cols].rearrange("p (c n) -> p c n", c=kc)
            lo = w_lo[:, s, 0:kc * cols].rearrange("p (c n) -> p c n", c=kc)
            pe.wait_ge(lo_ready, u + 1)
            if x["form"] == "F":
                return down(x["i"], hi, lo)
            if bank_before[u] is not None:
                wait_out(pe, bank_before[u])
            dense(x, bank_of[u], hi, lo).then_inc(unit_done, 1)

        def dense(x, bank, hi, lo):
            kc, cols = x["kc"], x["cols"]
            a_hi, a_lo, o = x_hi, x_lo, 0
            if x["name"] == "merge":
                a_hi, a_lo, o = o_hi, o_lo, x["o0"]
            if x["form"] == "A":
                for tb in range(TB):
                    for c in range(kc):
                        tok = slice(P * tb, P * tb + P)
                        last = three(ps[:, bank, cols * tb:cols * tb + cols], a_hi[:, o + c, tok],
                                     a_lo[:, o + c, tok], hi[:, c, :], lo[:, c, :], c == 0, c == kc - 1)
            elif x["form"] == "B":
                for nb in range(cols // P):
                    for c in range(kc):
                        col = slice(P * nb, P * nb + P)
                        last = three(ps[:, bank, T * nb:T * nb + T], hi[:, c, col], lo[:, c, col],
                                     a_hi[:, o + c, :], a_lo[:, o + c, :], c == 0, c == kc - 1)
            else:
                for c in range(kc):
                    three(ps[:, bank, 0:T], hi[:, c, 0:P], lo[:, c, 0:P], a_hi[:, c, :], a_lo[:, c, :],
                          c == 0, c == kc - 1)
                for tb in range(TB):
                    for c in range(kc):
                        tok = slice(P * tb, P * tb + P)
                        last = three(ps[:, bank, T + 8 * tb:T + 8 * tb + 8], a_hi[:, c, tok], a_lo[:, c, tok],
                                     hi[:, c, P:P + 8], lo[:, c, P:P + 8], c == 0, c == kc - 1)
            return last

        def down(i, hi, lo):
            first, end = isinstance(i, int) and i == 0, isinstance(i, int) and i == NF - 1
            pe.wait_ge(act_ready, i + 1)
            for c in range(2):
                for tb in range(TB):
                    for half in range(2):
                        tok, col = slice(P * tb, P * tb + P), slice(512 * half, 512 * half + 512)
                        last = three(ps[:, 4 + 2 * tb + half, :], o_hi[:, c, tok], o_lo[:, c, tok],
                                     hi[:, c, col], lo[:, c, col], first and c == 0, end and c == 1)
            last.then_inc(unit_done, 1)

        def triple(i):
            for j in range(3):
                x, s = units[S2 + j], (S2 + j) % 3
                pe.wait_ge(lo_ready, i * 3 + (S2 - 3 + j + 1))
                shape = dict(c=x["kc"])
                hi = w_hi[:, s, :].rearrange("p (c n) -> p c n", **shape)
                lo = w_lo[:, s, :].rearrange("p (c n) -> p c n", **shape)
                if j == 2:
                    down(i - 1, hi, lo)
                    continue
                if j == 0:
                    pe.wait_ge(out_act, i + outs(G0 - 1, False))
                else:
                    pe.wait_ge(out_dve, i + outs(G0 - 1, True))
                dense(x, j, hi, lo).then_inc(unit_done, 1)

        def norm(n):
            pe.wait_ge(normed_done, n + 1)
            src = normed2 if n == 3 else normed
            for c in range(KC):
                for tb in range(TB):
                    last = nc.tensor.transpose(ps[:, 2 + c // 2, T * (c % 2) + P * tb:T * (c % 2) + P * tb + P],
                                               src[:, tb, P * c:P * c + P], ident)
                if c % 2:
                    last.then_inc(norm_T, 1)

        def head(k, lo, end):
            if k < end:
                q, kk, v, p0 = head_in(k)
                if k >= lo + 2:
                    pe.wait_ge(mid_ready, k - 1)
                bank = 4 + k % 2
                if kind(k) == "sb":
                    mm(ps[:, bank, 0:T], kk[:, 0:P], q, start=True, stop=True)
                    last = mm(ps[:, bank, T:CAUSAL], kk[:, P:T], q[:, P:T], start=True, stop=True)
                elif kind(k) == "x":
                    for tb in range(TB):
                        last = mm(ps[:, bank, T * tb:T * tb + T], q[:, P * tb:P * tb + P], kk, start=True,
                                  stop=True)
                else:
                    mm(ps[:, bank, 0:P], q[:, 0:P], kk[:, 0:P], start=True, stop=True)
                    last = mm(ps[:, bank, P:CAUSAL], q[:, P:T], kk, start=True, stop=True)
                last.then_inc(z_done, 1)
            k -= 1
            if lo <= k < end:
                pe.wait_ge(mid_ready, k + 1)
                if k >= lo + 2:
                    pe.wait_ge(right_ready, k - 1)
                m, src = ps[:, (6, 2)[k % 2], :], prob_b[k % 2]
                if kind(k) == "sb":
                    later = const("later")
                    mm(m[:, 0:T], later, src[:, 0:T], start=True, stop=False)
                    mm(m[:, P:T], ones[:, :], src[:, T:CAUSAL], start=False, stop=True)
                    last = mm(m[:, T:CAUSAL], later, src[:, T:CAUSAL], start=True, stop=True)
                elif kind(k) == "x":
                    for tb in range(TB):
                        for mb in range(TB):
                            last = nc.tensor.transpose(m[:, T * mb + P * tb:T * mb + P * tb + P],
                                                       src[:, T * tb + P * mb:T * tb + P * mb + P], ident)
                else:
                    for t in range(3):
                        last = nc.tensor.transpose(m[:, P * t:P * t + P], src[:, P * t:P * t + P], ident)
                last.then_inc(mid_done, 1)
            k -= 1
            if lo <= k < end:
                q, kk, v, p0 = head_in(k)
                pe.wait_ge(right_ready, k + 1)
                if k % 2 == 0 and k >= lo + 4:
                    pe.wait_ge(pair_out, k // 2 - 1)
                o = ps[p0:p0 + DH, (7, 3)[k // 2 % 2], :]
                r = right_b[k % 2]
                mm(o[:, 0:T], v[:, 0, :], r[:, 0:T], start=True, stop=False)
                if kind(k) == "x":
                    last = mm(o[:, 0:T], v[:, 1, :], r[:, T:2 * T], start=False, stop=True)
                else:
                    last = mm(o[:, P:T], v[:, 1, :], r[:, T:CAUSAL], start=False, stop=True)
                last.then_inc(o_done, 1)

        for step, *arg in plan:
            if step == "vectors":
                pe.wait_ge(in_rows, 80)
                pe.wait_ge(in_table, 16)
                nc.tensor.transpose(ps[:, 7, 0:36], rows[:, :], ident[0:36, 0:36]).then_inc(vec_T, 1)
            elif step == "norm":
                norm(arg[0])
                pe.wait_ge(x_ready, arg[0] + 1)
            elif step == "unit":
                u = arg[0]
                if units[u]["name"] == "merge" and units[u]["j"] == 0 and units[u]["b"] == 0:
                    if u < G0:
                        pe.wait_ge(pool_out, 1)
                        pe.wait_ge(pair_out, 6)
                    else:
                        pe.wait_ge(pair_out, 14)
                if units[u]["name"] in ("out", "out2") and units[u]["j"] == 0:
                    pe.wait_ge(merged_ready, 4 if u < G0 else 8)
                unit(u)
            elif step == "pool_window":
                wait_out(pe, first["p"] + 1)
                pe.wait_ge(in_win, 16)
                for g in range(4):
                    dst = ps[:, 6, T * g:T * g + T] if g < 2 else ps[:, 7, T * (g - 2):T * (g - 2) + T]
                    col = slice(P * g, P * g + P)
                    mm(dst, p_tok[:, 0, col], win[:, g, 0:T], start=True, stop=False)
                    last = mm(dst[:, P:T], p_tok[:, 1, col], win[:, g, T:CAUSAL], start=False, stop=True)
                last.then_inc(pool_w, 1)
            elif step == "pool_mix":
                pe.wait_ge(pool_mixed, 1)
                pe.wait_ge(in_mix, 16)
                for g in range(4):
                    dst = ps[:, 6, T * g:T * g + T] if g < 2 else ps[:, 7, T * (g - 2):T * (g - 2) + T]
                    last = mm(dst, pool_w_sb[:, g, :], mixed[:, g, :], start=True, stop=True)
                last.then_inc(pool_p, 1)
            elif step == "head":
                k, lo, end = arg
                if k == 0:
                    pe.wait_ge(pool_out, 1)
                    wait_out(pe, first["xq"])
                if k == 12 and lo == 12:
                    pe.wait_ge(rope_done, N_ROPE)
                    wait_out(pe, first["va"] + 1)
                    pe.wait_ge(ix_acc, 8)
                head(k, lo, end)
            elif step == "ffn":
                unit(G0)
                unit(G0 + 1)
                ffn_loop(pe, triple)
                unit(S2 + 3 * (NF - 1))
            elif step == "rope":
                r, u = arg
                wait_out(pe, u)
                if r >= 1:
                    pe.wait_ge(rope_done, r)
                n = T if r == 0 else 2 * T
                mm(ps[:, 7, 0:n], const("rotate"), prob_b[r % 2][:, 0:n], start=True, stop=True)\
                    .then_inc(rot_done, 1)
            elif step == "index":
                pe.wait_ge(rope_done, 3)
                for i in range(8):
                    p0 = DH * (i % 2)
                    q, kk, bank = qi[p0:p0 + DH, i // 2, :], ki[p0:p0 + DH, :], 4 + i % 2
                    if i >= 2:
                        pe.wait_ge(ix_relu, i - 1)
                    mm(ps[:, bank, 0:P], q[:, 0:P], kk[:, 0:P], start=True, stop=True)
                    mm(ps[:, bank, P:CAUSAL], q[:, P:T], kk, start=True, stop=True).then_inc(ix_z, 1)
            elif step in ("post", "topk", "select"):
                pass
            else:
                raise ValueError(step)

        pe.wait_ge(n3_ready, 1)
        for c in range(KC):
            for tb in range(TB):
                last = nc.tensor.transpose(ps[:, 2 + c // 2, T * (c % 2) + P * tb:T * (c % 2) + P * tb + P],
                                           n3[:, tb, c:D:KC], ident)
        last.then_inc(n3_T, 1)
        pe.wait_ge(n3_out, 1)
        pe.wait_ge(in_route, 64)
        for tb in range(TB):
            for c in range(KC):
                last = mm(ps[:, 0, 36 * tb:36 * tb + 36], n3T[:, c, P * tb:P * tb + P], w_route[:, c, :],
                          start=c == 0, stop=c == KC - 1)
        last.then_inc(logit_done, 1)
        pe.wait_ge(route_sel, 1)
        before = const("before")
        mm(ps[:, 1, 0:EXPERTS], before, chosen[:, 0, :], start=True, stop=True)
        mm(ps[:, 1, EXPERTS:2 * EXPERTS], before, chosen[:, 1, :], start=True, stop=False)
        mm(ps[:, 1, EXPERTS:2 * EXPERTS], ones[:, :], chosen[:, 0, :], start=False, stop=True)
        mm(ps[:, 1, 64:64 + EXPERTS], ones[:, :], chosen[:, 0, :], start=True, stop=False)
        mm(ps[:, 1, 64:64 + EXPERTS], ones[:, :], chosen[:, 1, :], start=False, stop=True).then_inc(rank_done, 1)
        pe.wait_ge(passes_ready, 1)
        n_pass = pe.value_load(passes_i[0:1, 0:1], min_val=1, max_val=T // SLOTS)
        with pe.Fori(0, n_pass) as pas:
            with pe.Fori(0, EXPERTS // QUAD) as i:
                quad = pe.snap(pas * (EXPERTS // QUAD) + i)
                e0 = pe.snap(quad * QUAD)
                pe.wait_ge(hot_ready, quad + 1)
                for c in range(KC):
                    for tb in range(TB):
                        last = mm(ps[:, 2 + c // 4, P * (c % 4):P * (c % 4) + P], n3[:, tb, c:D:KC],
                                  one_hot[:, tb, :], start=tb == 0, stop=tb == 1)
                last.then_inc(xg_done, 1)
                for tb in range(TB):
                    last = nc.tensor.transpose(ps[:, 0, P * tb:P * tb + P], gated_hot[:, tb, :], ident)
                last.then_inc(gt_done, 1)
                pe.wait_ge(xg_ready, quad + 1)
                for e in range(QUAD):
                    odd = e % 2
                    s1, s3, s2 = SLOT_OF[odd]
                    w1 = arena[:, s1:s1 + 2, :].rearrange("p s (c n) -> p (s c) n", c=4)
                    w3 = arena[:, s3:s3 + 2, :].rearrange("p s (c n) -> p (s c) n", c=4)
                    w2 = arena[:, s2:s2 + 2, :].rearrange("p s (c n) -> p (s c) n", c=2)
                    arrived = pe.snap(e0 * 8 + (e // 2 + 1) * 16)
                    done = pe.snap(e0 + e)
                    for n, (w, landing) in enumerate(((w1, w_up[odd]), (w3, w_gate3[odd]))):
                        pe.wait_ge(landing, arrived)
                        for c in range(KC):
                            for g in range(4):
                                last = mm(ps[SLOTS * g:SLOTS * g + SLOTS, 4 + odd, P * n:P * n + P],
                                          xg[:, c, SLOTS * e:SLOTS * e + SLOTS], w[:, c, P * g:P * g + P],
                                          start=c == 0, stop=c == KC - 1, tile_position=(0, SLOTS * g))
                    last.then_inc(e_up, 1)
                    pe.wait_ge(e_hid, done + 1)
                    nc.tensor.transpose(ps[:, 6, 0:P], hid[:, :], ident).then_inc(e_T, 1)
                    pe.wait_ge(w_down[odd], arrived)
                    pe.wait_ge(e_hidT, done + 1)
                    for b in range(4):
                        for g in range(4):
                            last = mm(ps[SLOTS * g:SLOTS * g + SLOTS, 7, 0:UC],
                                      hid_T[:, SLOTS * b:SLOTS * b + SLOTS], w2[:, b, UC * g:UC * g + UC],
                                      start=b == 0, stop=b == 3, tile_position=(0, SLOTS * g))
                    last.then_inc(e_y, 1)
                pe.wait_ge(gt_ready, quad + 1)
                pe.wait_ge(e_yA, e0 * 2 + 2 * QUAD)
                pe.wait_ge(e_yD, e0 * 2 + 2 * QUAD)
                for tb in range(TB):
                    for half in range(2):
                        last = mm(ps[:, 2 * tb + half, :], gate_T[:, P * tb:P * tb + P],
                                  y_quad[:, 512 * half:512 * half + 512], start=True, stop=True)
                last.then_inc(comb_done, 1)

    @block.scalar
    def _(act):
        chain = [0]
        fn = nc.scalar.activation

        def link(ins):
            chain[0] += 1
            ins.then_inc(act_chain, 1)
            act.wait_ge(act_chain, chain[0])

        act.dma_start(pool_w_sb[:, :, :], a["w_pool_mix"][0].rearrange("g c d -> c g d")).then_inc(in_mix, 16)

        def split(u):
            if u >= U:
                return
            x = units[u]
            n = x["kc"] * x["cols"]
            if u >= 3:
                act.wait_ge(unit_done, u - 2)
            act.wait_ge(landed[u % 3], landings(u))
            fn(w_hi[:, u % 3, 0:n], arena[:, u % 3, 0:n], ACT.Copy).then_inc(hi_ready, 1)

        def split_ffn(i, j):
            if isinstance(i, int):
                return split(S2 + 3 * (i - 1) + j + 2)
            s = (S2 + j + 2) % 3
            act.wait_ge(unit_done, i * 3 + (S2 - 3 + j))
            act.wait_ge(landed[s], i * 16 + (landings(S2 + 3 + j + 2) - 32))
            fn(w_hi[:, s, :], arena[:, s, :], ACT.Copy).then_inc(hi_ready, 1)

        copies = {"mk": mk, "q": q1, "k": k1, "xq": xq}
        tokens = {"mv": mv, "p": p_tok, "v": v1, "vb": vb, "va": va, "out": y_tok}

        def evacuate(u):
            x = units[u]
            name, j = x["name"], x.get("j", 0)
            full = ps[:, bank_of[u], :]
            act.wait_ge(unit_done, u + 1)
            if name in copies:
                scale = 0.125 if name in ("q", "xq") else 1.0
                dst = copies[name][:, 2 * j:2 * j + 2, :].rearrange("p a b -> p (a b)")
                fn(dst, full, ACT.Copy, scale=scale).then_inc(out_act, 1)
            elif name in tokens:
                fn(tokens[name][:, :, UC * j:UC * j + UC], full.rearrange("p (a b) -> p a b", a=2), ACT.Copy)\
                    .then_inc(out_act, 1)
            elif name in ("gate", "gate2"):
                g = gates if name == "gate" else gates2
                fn(g[:, 2 * j:2 * j + 2, :].rearrange("p a b -> p (a b)"), full, ACT.Sigmoid).then_inc(out_act, 1)
            elif name == "kiwi":
                link(fn(index_w[:, :, :].rearrange("p a b -> p (a b)"), full[:, T:T + 16], ACT.Copy,
                        scale=512.0 ** -0.5))
                fn(prob_b[0][:, 0:T], full[:, 0:T], ACT.Copy).then_inc(out_act, 1)
            elif name in ROPED:
                r = rope_of[u]
                if r >= 2:
                    act.wait_ge(rope_done, r - 1)
                fn(prob_b[r % 2][:, :], full, ACT.Copy).then_inc(out_act, 1)
            else:
                raise ValueError(name)

        def square(n, src, junk):
            for tb in range(TB):
                ins = fn(junk[:, tb, :], src[:, tb, :], ACT.Square, accum_out=stat[:, tb:tb + 1])
                link(ins) if tb == 0 else ins.then_inc(sq_done, 1)

        def root(n):
            act.wait_ge(mean_done, n + 1)
            fn(stat[:, 4:6], stat[:, 2:4], ACT.Sqrt).then_inc(root_done, 1)

        def head(k, lo, end):
            if k < end:
                s = k % 2
                if kind(k) == "sb":
                    act.wait_ge(z_done, k + 1)
                    if k >= 2:
                        act.wait_ge(mid_ready, k - 1)
                    link(fn(score_b[s][:, 0:CAUSAL], ps[:, 4 + s, 0:CAUSAL], ACT.Abs))
                    link(fn(score_b[s][:, 0:CAUSAL], score_b[s][:, 0:CAUSAL], ACT.Exp, scale=-1.0))
                    fn(score_b[s][:, 0:CAUSAL], score_b[s][:, 0:CAUSAL], ACT.Ln, bias=1.0).then_inc(exp_done, 1)
                else:
                    act.wait_ge(prep_done, k - 7)
                    scale = 1.0 if kind(k) == "x" else 0.125
                    c = (0, T, 2 * T) if kind(k) == "x" else (0, P, CAUSAL)
                    for tb in range(TB):
                        ins = fn(prob_b[s][:, c[tb]:c[tb + 1]], score_b[s][:, c[tb]:c[tb + 1]], ACT.Exp,
                                 bias=softmax[:, 8 * s + tb:8 * s + tb + 1], scale=scale,
                                 accum_out=softmax[:, 8 * s + 2 + tb:8 * s + 3 + tb])
                        link(ins) if tb == 0 else ins.then_inc(exp_done, 1)
            k -= 1
            if lo <= k < end and kind(k) == "sb":
                act.wait_ge(expo_ready, k + 1)
                fn(right_b[k % 2][:, 0:CAUSAL], expo_b[k % 2][:, 0:CAUSAL], ACT.Exp).then_inc(a_done, 1)

        norms = 0
        split(0)
        split(1)
        for step, *arg in plan:
            if step == "norm":
                n = arg[0]
                if n == 0:
                    act.wait_ge(in_mem, 16)
                    square(norms, mem_tok, normed)
                else:
                    if n == 1:
                        act.wait_ge(in_x, 16)
                    else:
                        act.wait_ge(gain_used, n - 1)
                    act.wait_ge(norm_T, 4 * n)
                    square(norms, h, normed2 if n == 3 else normed)
                root(norms)
                norms += 1
            elif step == "post":
                if arg[0] == 1:
                    act.wait_ge(unit_done, G0 + 3 * NF)
                    for tb in range(TB):
                        for half in range(2):
                            link(fn(y_tok[:, tb, 512 * half:512 * half + 512], ps[:, 4 + 2 * tb + half, :],
                                    ACT.Copy))
                else:
                    wait_out(act, first["out"] + 3)
                square(norms, y_tok, normed)
                root(norms)
                norms += 1
            elif step == "unit":
                split(arg[0] + 2)
                if units[arg[0]]["name"] not in BY_VECTOR:
                    evacuate(arg[0])
            elif step == "pool_window":
                act.wait_ge(pool_w, 1)
                for b in range(2):
                    ins = fn(mixed[:, 2 * b:2 * b + 2, :].rearrange("p a b -> p (a b)"), ps[:, 6 + b, :], ACT.Copy)
                    link(ins) if b == 0 else ins.then_inc(pool_mixed, 1)
            elif step == "head":
                head(*arg)
            elif step == "index":
                for i in range(8):
                    act.wait_ge(ix_z, i + 1)
                    if i >= 2:
                        act.wait_ge(ix_acc, i - 1)
                    fn(score_b[i % 2][:, 0:CAUSAL], ps[:, 4 + i % 2, 0:CAUSAL], ACT.Relu).then_inc(ix_relu, 1)
            elif step == "ffn":
                def gate(i, used):
                    act.wait_ge(unit_done, used)
                    fn(silu_g[:, :], ps[:, 0, :], ACT.Silu).then_inc(out_act, 1)

                def triple(i):
                    for j in range(3):
                        split_ffn(i, j)
                        if j == 0:
                            act.wait_ge(out_dve, i + outs(G0 - 1, True))
                            gate(i, i * 3 + (S2 - 3 + 1))

                for j in range(2):
                    split(G0 + j + 2)
                    if j == 0:
                        gate(0, G0 + 1)
                ffn_loop(act, triple)
                split(S2 + 3 * (NF - 1) + 2)
        act.wait_ge(out_dve, outs(U - 1, True))
        square(norms, h, n3)
        root(norms)
        norms += 1
        act.wait_ge(n3_T, 1)
        for b in range(4):
            ins = fn(n3T[:, 2 * b:2 * b + 2, :].rearrange("p a b -> p (a b)"), ps[:, 2 + b, :], ACT.Copy)
            link(ins) if b < 3 else ins.then_inc(n3_out, 1)
        act.wait_ge(route_in, 1)
        fn(exp_out[:, :, :].rearrange("p a b -> p (a b)"), exp_in[:, :, :].rearrange("p a b -> p (a b)"), ACT.Exp)\
            .then_inc(route_exp, 1)
        act.wait_ge(passes_ready, 1)
        n_pass = act.value_load(passes_i[0:1, 0:1], min_val=1, max_val=T // SLOTS)
        with act.Fori(0, n_pass) as pas:
            with act.Fori(0, EXPERTS // QUAD) as i:
                quad = act.snap(pas * (EXPERTS // QUAD) + i)
                e0 = act.snap(quad * QUAD)
                act.wait_ge(xg_done, quad + 1)
                fn(xg[:, 0:4, :].rearrange("p a b -> p (a b)"), ps[:, 2, :], ACT.Copy).then_inc(xg_part, 1)
                act.wait_ge(xg_part, quad + 1)
                fn(xg[:, 4:8, :].rearrange("p a b -> p (a b)"), ps[:, 3, :], ACT.Copy).then_inc(xg_ready, 1)
                act.wait_ge(gt_done, quad + 1)
                fn(gate_T[:, :], ps[:, 0, 0:T], ACT.Copy).then_inc(gt_ready, 1)
                for e in range(QUAD):
                    act.wait_ge(e_up, e0 + e + 1)
                    fn(silu_e[:, :], ps[:, 4 + e % 2, 0:P], ACT.Silu).then_inc(e_silu, 1)
                    act.wait_ge(e_y, e0 + e + 1)
                    for g in (0, 1):
                        fn(y_quad[SLOTS * e:SLOTS * e + SLOTS, UC * g:UC * g + UC],
                           ps[SLOTS * g:SLOTS * g + SLOTS, 7, 0:UC], ACT.Copy).then_inc(e_yA, 1)
        act.wait_ge(comb_added, n_pass * (EXPERTS // QUAD))
        square(norms, h, n3)
        root(norms)

    @block.vector
    def _(dve):
        chain = [0]
        v = nc.vector

        def link(ins):
            chain[0] += 1
            ins.then_inc(dve_chain, 1)
            dve.wait_ge(dve_chain, chain[0])

        def split(u):
            if u >= U:
                return
            n = units[u]["kc"] * units[u]["cols"]
            dve.wait_ge(hi_ready, u + 1)
            v.tensor_tensor(w_lo[:, u % 3, 0:n], arena[:, u % 3, 0:n], w_hi[:, u % 3, 0:n].bitcast(F32),
                            ALU.subtract).then_inc(lo_ready, 1)

        def split_ffn(i, j):
            if isinstance(i, int):
                return split(S2 + 3 * (i - 1) + j + 2)
            s = (S2 + j + 2) % 3
            dve.wait_ge(hi_ready, i * 3 + (S2 - 3 + j + 3))
            v.tensor_tensor(w_lo[:, s, :], arena[:, s, :], w_hi[:, s, :].bitcast(F32), ALU.subtract)\
                .then_inc(lo_ready, 1)

        def scale_of(n):
            dve.wait_ge(sq_done, n + 1)
            v.tensor_scalar(stat[:, 2:4], stat[:, 0:2], 1.0 / D, EPS, ALU.mult, ALU.add).then_inc(mean_done, 1)
            dve.wait_ge(root_done, n + 1)
            link(v.reciprocal(stat[:, 6:8], stat[:, 4:6]))

        def flat(x):
            return x.rearrange("p a b -> p (a b)")

        def norm(n, seen, used):
            src = (mem_tok, h, h, h)[n]
            dst = normed2 if n == 3 else normed
            scale_of(seen)
            for tb in range(TB):
                ins = v.tensor_scalar(dst[:, tb, :], src[:, tb, :], stat[:, 6 + tb:7 + tb], None, ALU.mult)
                link(ins) if tb == 0 else ins.then_inc(normed_done, 1)
            if used:
                dve.wait_ge(unit_done, used)
            g0 = (0, 8, 20, 28)[n]
            for c in range(KC):
                if c % 2 == 0:
                    dve.wait_ge(norm_T, 4 * n + c // 2 + 1)
                src = ps[:, 2 + c // 2, T * (c % 2):T * (c % 2) + T]
                g = vec[:, g0 + c:g0 + c + 1]
                link(v.tensor_scalar(x_hi[:, c, :], src, g, None, ALU.mult))
                ins = v.scalar_tensor_tensor(x_lo[:, c, :], src, g, x_hi[:, c, :].bitcast(F32), ALU.mult,
                                             ALU.subtract)
                link(ins) if c < KC - 1 else ins.then_inc(x_ready, 1)

        def post(n, seen):
            scale_of(seen)
            dve.wait_ge(in_gain, 16 * (n + 1))
            for tb in range(TB):
                link(v.scalar_tensor_tensor(y_tok[:, tb, :], y_tok[:, tb, :], stat[:, 6 + tb:7 + tb], gain_row[:, :],
                                            ALU.mult, ALU.mult))
                ins = v.tensor_tensor(h[:, tb, :], h[:, tb, :], y_tok[:, tb, :], ALU.add)
                link(ins) if tb == 0 else ins.then_inc(gain_used, 1)
            dve.wait_ge(gain_used, n + 1)

        def head(k, lo, end):
            k0, s = k, k % 2
            if k < end:
                kd, z = kind(k), ps[:, 4 + k % 2, :]
                dve.wait_ge(z_done, k + 1)
                if kd != "sb":
                    if kd == "x":
                        link(v.tensor_copy(score_b[s][:, :], z))
                        cut = (0, T, 2 * T)
                    else:
                        hide = const("hide") if kd == "moba" else score[:, :]
                        link(v.tensor_tensor(score_b[s][:, 0:CAUSAL], z[:, 0:CAUSAL], hide, ALU.add))
                        cut = (0, P, CAUSAL)
                    for tb in range(TB):
                        link(v.tensor_reduce(softmax[:, 8 * s + 4 + tb:8 * s + 5 + tb],
                                             score_b[s][:, cut[tb]:cut[tb + 1]], AX.X, ALU.max))
                    v.tensor_scalar(softmax[:, 8 * s:8 * s + 2], softmax[:, 8 * s + 4:8 * s + 6],
                                    -1.0 if kd == "x" else -0.125, None, ALU.mult).then_inc(prep_done, 1)
            k -= 1
            if lo <= k < end:
                m = ps[:, (6, 2)[k % 2], :]
                dve.wait_ge(mid_done, k + 1)
                if kind(k) == "sb":
                    v.tensor_tensor(expo_b[k % 2][:, 0:CAUSAL], expo_b[k % 2][:, 0:CAUSAL], m[:, 0:CAUSAL],
                                    ALU.subtract).then_inc(expo_ready, 1)
                else:
                    n = 2 * T if kind(k) == "x" else CAUSAL
                    v.tensor_copy(right_b[k % 2][:, 0:n], m[:, 0:n]).then_inc(right_ready, 1)
            k -= 1
            if lo <= k < end and k % 2:
                o, c = ps[:, (7, 3)[k // 2 % 2], 0:T], pair_slot(k)
                dve.wait_ge(o_done, k + 1)
                link(v.tensor_copy(o_hi[:, c, :], o))
                v.tensor_tensor(o_lo[:, c, :], o, o_hi[:, c, :].bitcast(F32), ALU.subtract).then_inc(pair_out, 1)
            k = k0
            if k < end:
                kd, z = kind(k), ps[:, 4 + k % 2, :]
                dve.wait_ge(exp_done, k + 1)
                if kd == "sb":
                    soft = prob_b[s][:, 0:CAUSAL]
                    link(v.scalar_tensor_tensor(soft, z[:, 0:CAUSAL], 0.0, score_b[s][:, 0:CAUSAL], ALU.max, ALU.add))
                    link(v.tensor_tensor(expo_b[s][:, 0:CAUSAL], z[:, 0:CAUSAL], soft, ALU.subtract))
                    v.tensor_tensor(soft, soft, const("keep"), ALU.mult).then_inc(mid_ready, 1)
                else:
                    cut = (0, T, 2 * T) if kd == "x" else (0, P, CAUSAL)
                    link(v.reciprocal(softmax[:, 8 * s + 6:8 * s + 8], softmax[:, 8 * s + 2:8 * s + 4]))
                    for tb in range(TB):
                        part = prob_b[s][:, cut[tb]:cut[tb + 1]]
                        ins = v.tensor_scalar(part, part, softmax[:, 8 * s + 6 + tb:8 * s + 7 + tb], None, ALU.mult)
                        link(ins) if tb == 0 else ins.then_inc(mid_ready, 1)
            k -= 1
            if lo <= k < end and kind(k) == "sb":
                dve.wait_ge(a_done, k + 1)
                right = right_b[k % 2][:, 0:CAUSAL]
                v.tensor_tensor(right, right, const("keep"), ALU.mult).then_inc(right_ready, 1)

        def merge(u):
            x = units[u]
            g, n = (gates, 8) if u < G0 else (gates2, 8)
            j, b = x["j"], x["b"]
            part = flat(g[:, n * b + 2 * j:n * b + 2 * j + 2, :])
            total = flat(g[:, 2 * j:2 * j + 2, :])
            v.tensor_tensor(part, part, ps[:, bank_of[u], :], ALU.mult).then_inc(out_dve, 1)
            dve.wait_ge(out_dve, outs(u, True))
            if b:
                link(v.tensor_tensor(total, total, part, ALU.add))
            if x["last"]:
                hi, lo = flat(x_hi[:, 2 * j:2 * j + 2, :]), flat(x_lo[:, 2 * j:2 * j + 2, :])
                link(v.tensor_copy(hi, total))
                v.tensor_tensor(lo, total, hi.bitcast(F32), ALU.subtract).then_inc(merged_ready, 1)

        roped = {"qi": qi, "kb": kb, "qb": qb, "ka": ka, "qa": qa}

        def rope(r, u):
            wait_out(dve, u)
            s, n = r % 2, T if r == 0 else 2 * T
            name = units[u]["name"]
            dst = ki[:, :] if r == 0 else flat(roped[name][:, 2 * units[u]["j"]:2 * units[u]["j"] + 2, :])
            link(v.tensor_tensor(expo_b[s][:, 0:n], prob_b[s][:, 0:n], const("cos")[:, 0:n], ALU.mult))
            dve.wait_ge(rot_done, r + 1)
            link(v.tensor_tensor(right_b[s][:, 0:n], ps[:, 7, 0:n], const("sin")[:, 0:n], ALU.mult))
            v.tensor_tensor(dst, expo_b[s][:, 0:n], right_b[s][:, 0:n], ALU.add).then_inc(rope_done, 1)

        columns = ((0, P), (P, CAUSAL))

        def ffn():
            def up(i, done):
                dve.wait_ge(unit_done, done)
                dve.wait_ge(out_act, i + (outs(G0 - 1, False) + 1))
                v.tensor_tensor(act_f[:, :], silu_g[:, :], ps[:, 1, :], ALU.mult).then_inc(out_dve, 1)
                dve.wait_ge(out_dve, i + (outs(G0 - 1, True) + 1))

            def parts(i):
                hi, lo = flat(o_hi[:, 0:2, :]), flat(o_lo[:, 0:2, :])
                v.tensor_copy(hi, act_f[:, :]).then_inc(act_hi, 1)
                dve.wait_ge(act_hi, i + 1)
                v.tensor_tensor(lo, act_f[:, :], hi.bitcast(F32), ALU.subtract).then_inc(act_ready, 1)
                dve.wait_ge(act_ready, i + 1)

            def triple(i):
                for j in range(3):
                    split_ffn(i, j)
                    if j == 1:
                        up(i, i * 3 + (S2 - 3 + 2))
                    elif j == 2:
                        dve.wait_ge(unit_done, i * 3 + (S2 - 3 + 3))
                        parts(i)

            split(G0 + 2)
            split(G0 + 3)
            up(0, G0 + 2)
            parts(0)
            ffn_loop(dve, triple)
            split(S2 + 3 * (NF - 1) + 2)

        v.memset(ones[:, :], 1.0).then_inc(dve_chain, 1)
        chain[0] += 1
        split(0)
        split(1)
        seen = 0
        used = 0
        for step, *arg in plan:
            if step == "vectors":
                dve.wait_ge(vec_T, 1)
                link(v.tensor_copy(vec[:, :], ps[:, 7, 0:36]))
            elif step == "norm":
                norm(arg[0], seen, used)
                seen += 1
            elif step == "post":
                post(arg[0], seen)
                seen += 1
            elif step == "unit":
                u = arg[0]
                split(u + 2)
                used = u + 1
                if units[u]["name"] == "merge":
                    dve.wait_ge(unit_done, u + 1)
                    merge(u)
                elif units[u]["name"] == "out2":
                    dve.wait_ge(unit_done, u + 1)
                    part = h[:, :, UC * units[u]["j"]:UC * units[u]["j"] + UC]
                    v.tensor_tensor(part, part, ps[:, bank_of[u], :].rearrange("p (a b) -> p a b", a=TB), ALU.add)\
                        .then_inc(out_dve, 1)
                    dve.wait_ge(out_dve, outs(u, True))
            elif step == "pool_mix":
                dve.wait_ge(pool_p, 1)
                for g in range(4):
                    src = ps[:, 6 + g // 2, T * (g % 2):T * (g % 2) + T]
                    gain = vec[:, 16 + g:17 + g]
                    link(v.tensor_scalar(o_hi[:, g, :], src, gain, None, ALU.mult))
                    ins = v.scalar_tensor_tensor(o_lo[:, g, :], src, gain, o_hi[:, g, :].bitcast(F32), ALU.mult,
                                                 ALU.subtract)
                    link(ins) if g < 3 else ins.then_inc(pool_out, 1)
            elif step == "head":
                head(*arg)
            elif step == "ffn":
                ffn()
                used = G0 + 3 * NF
            elif step == "rope":
                rope(*arg)
            elif step == "index":
                for i in range(8):
                    dve.wait_ge(ix_relu, i + 1)
                    for tb, (c0, c1) in enumerate(columns):
                        w, src = index_w[:, tb, i:i + 1], score_b[i % 2][:, c0:c1]
                        if i == 0:
                            ins = v.tensor_scalar(score[:, c0:c1], src, w, None, ALU.mult)
                        else:
                            ins = v.scalar_tensor_tensor(score[:, c0:c1], src, w, score[:, c0:c1], ALU.mult, ALU.add)
                        link(ins) if tb == 0 else ins.then_inc(ix_acc, 1)
                    dve.wait_ge(ix_acc, i + 1)
                link(v.tensor_tensor(work[:, :], score[:, :], const("hide"), ALU.add))
            elif step == "topk":
                for tb, (c0, c1) in enumerate(columns):
                    link(v.max(best8[:, tb, :], work[:, c0:c1]))
                    link(v.match_replace(work[:, c0:c1], best8[:, tb, :], work[:, c0:c1], TAKEN))
            elif step == "select":
                link(v.tensor_scalar(score[:, :], work[:, :], TAKEN / 2, NEG, ALU.is_gt, ALU.mult))
                link(v.tensor_tensor(score[:, :], score[:, :], const("hide"), ALU.add))

        scale_of(seen)
        dve.wait_ge(in_gain, 48)
        for tb in range(TB):
            ins = v.scalar_tensor_tensor(n3[:, tb, :], h[:, tb, :], stat[:, 6 + tb:7 + tb], gain_row[:, :], ALU.mult,
                                         ALU.mult)
            link(ins) if tb == 0 else ins.then_inc(n3_ready, 1)
        dve.wait_ge(logit_done, 1)
        dve.wait_ge(in_route, 64)

        def wide(x, n):
            return x.unsqueeze(2).to_broadcast([P, TB, n])

        def per_token(x, n):
            return x.unsqueeze(1).to_broadcast([P, TB, n])

        def tt(dst, a_, b_, op):
            link(v.tensor_tensor(dst, a_, b_, op))

        def biggest(dst, src, n):
            link(v.tensor_reduce(dst, src, AX.X, ALU.max))

        def first_of(dst, src, top, rev, n, scratch, place):
            tt(dst, src, wide(top, n), ALU.is_equal)
            tt(dst, dst, per_token(rev, n), ALU.mult)
            biggest(place, dst, n)
            tt(dst, dst, wide(place, n), ALU.is_equal)

        gmax, place, gsum, best, second, total, share = (r_s[:, i, :] for i in range(7))
        tt(logits[:, :, :], ps[:, 0, 0:72].rearrange("p (a b) -> p a b", a=TB), per_token(b_route[:, :], 36), ALU.add)
        lg, le = logits[:, :, 0:GROUPS], logits[:, :, GROUPS:36]
        biggest(gmax, lg, GROUPS)
        tt(exp_in[:, :, 0:GROUPS], lg, wide(gmax, GROUPS), ALU.subtract)
        first_of(pick_g[:, :, :], lg, gmax, const("revg"), GROUPS, None, place)
        for tb in range(TB):
            own = pick_g[:, tb, :].unsqueeze(2).to_broadcast([P, GROUPS, PER_GROUP])
            dst = masked_e[:, tb, :].rearrange("p (g e) -> p g e", g=GROUPS)
            tt(dst, le[:, tb, :].rearrange("p (g e) -> p g e", g=GROUPS), own, ALU.mult)
            hidden = pick[:, tb, :].rearrange("p (g e) -> p g e", g=GROUPS)
            link(v.tensor_scalar(hidden, own, 1.0, -NEG, ALU.subtract, ALU.mult))
            tt(dst, dst, hidden, ALU.add)
        biggest(best, masked_e[:, :, :], EXPERTS)
        v.tensor_tensor(exp_in[:, :, GROUPS:36], masked_e[:, :, :], wide(best, EXPERTS), ALU.subtract)\
            .then_inc(route_in, 1)
        first_of(chosen[:, :, :], masked_e[:, :, :], best, const("rev"), EXPERTS, None, place)
        link(v.tensor_scalar(pick[:, :, :], chosen[:, :, :], 2 * NEG, None, ALU.mult))
        tt(masked_e[:, :, :], masked_e[:, :, :], pick[:, :, :], ALU.add)
        biggest(second, masked_e[:, :, :], EXPERTS)
        first_of(pick_one[:, :, :], masked_e[:, :, :], second, const("rev"), EXPERTS, None, place)
        v.tensor_tensor(chosen[:, :, :], chosen[:, :, :], pick_one[:, :, :], ALU.add).then_inc(route_sel, 1)
        dve.wait_ge(route_sel, 1)
        dve.wait_ge(route_exp, 1)
        link(v.tensor_reduce(gsum, exp_out[:, :, 0:GROUPS], AX.X, ALU.add))
        link(v.reciprocal(gsum, gsum))
        link(v.tensor_reduce(total, exp_out[:, :, GROUPS:36], AX.X, ALU.add))
        link(v.reciprocal(total, total))
        tt(gate_e[:, :, :], exp_out[:, :, GROUPS:36], wide(total, EXPERTS), ALU.mult)
        tt(gate_e[:, :, :], gate_e[:, :, :], chosen[:, :, :], ALU.mult)
        link(v.tensor_reduce(share, gate_e[:, :, :], AX.X, ALU.add))
        link(v.reciprocal(share, share))
        tt(share, share, gsum, ALU.mult)
        tt(gate_e[:, :, :], gate_e[:, :, :], wide(share, EXPERTS), ALU.mult)
        dve.wait_ge(rank_done, 1)
        link(v.tensor_copy(slot_no[:, :], const("slot")))
        link(v.scalar_tensor_tensor(flat(rank[:, :, :]), ps[:, 1, 0:2 * EXPERTS], 1.0, flat(chosen[:, :, :]), ALU.add,
                                    ALU.mult))
        link(v.tensor_scalar(rank[:, :, :], rank[:, :, :], -1.0, None, ALU.add))
        link(v.tensor_reduce(r_s[:, 8, 0:1], ps[:, 1, 64:64 + EXPERTS], AX.X, ALU.max))
        link(v.tensor_scalar(exp_in[:, 0, 0:8], const("steps"), r_s[:, 8, 0:1], None, ALU.is_lt))
        link(v.tensor_reduce(r_s[:, 8, 1:2], exp_in[:, 0, 0:8], AX.X, ALU.add))
        v.tensor_copy(passes_i[:, :], r_s[:, 8, 1:2]).then_inc(passes_ready, 1)
        dve.wait_ge(passes_ready, 1)
        n_pass = dve.value_load(passes_i[0:1, 0:1], min_val=1, max_val=T // SLOTS)
        with dve.Fori(0, n_pass) as pas:
            with dve.Fori(0, EXPERTS // QUAD) as i:
                quad = dve.snap(pas * (EXPERTS // QUAD) + i)
                e0 = dve.snap(quad * QUAD)
                at_e = dve.snap(i * QUAD)
                slots = slot_no[:, :].unsqueeze(1).to_broadcast([P, QUAD, SLOTS])
                for tb in range(TB):
                    mine = rank[:, tb, bass.ds(at_e, QUAD)].unsqueeze(2).to_broadcast([P, QUAD, SLOTS])
                    hot = one_hot[:, tb, :].rearrange("p (e s) -> p e s", e=QUAD)
                    v.tensor_tensor(hot, slots, mine, ALU.is_equal).then_inc(hot_part, 1)
                    dve.wait_ge(hot_part, quad * 2 + (tb + 1))
                for tb in range(TB):
                    hot = one_hot[:, tb, :].rearrange("p (e s) -> p e s", e=QUAD)
                    gate = gate_e[:, tb, bass.ds(at_e, QUAD)].unsqueeze(2).to_broadcast([P, QUAD, SLOTS])
                    ins = v.tensor_tensor(gated_hot[:, tb, :].rearrange("p (e s) -> p e s", e=QUAD), hot, gate, ALU.mult)
                ins.then_inc(hot_ready, 1)
                for e in range(QUAD):
                    done = dve.snap(e0 + (e + 1))
                    dve.wait_ge(e_silu, done)
                    v.tensor_tensor(hid[:, :], silu_e[:, :], ps[:, 4 + e % 2, P:2 * P], ALU.mult).then_inc(e_hid, 1)
                    dve.wait_ge(e_T, done)
                    v.tensor_copy(hid_T[:, :], ps[:, 6, 0:P]).then_inc(e_hidT, 1)
                    dve.wait_ge(e_y, done)
                    for g in (2, 3):
                        v.tensor_copy(y_quad[SLOTS * e:SLOTS * e + SLOTS, UC * g:UC * g + UC],
                                      ps[SLOTS * g:SLOTS * g + SLOTS, 7, 0:UC]).then_inc(e_yD, 1)
                dve.wait_ge(comb_done, quad + 1)
                for tb in range(TB):
                    for half in range(2):
                        part = h[:, tb, 512 * half:512 * half + 512]
                        ins = v.tensor_tensor(part, part, ps[:, 2 * tb + half, :], ALU.add)
                ins.then_inc(comb_added, 1)
                dve.wait_ge(comb_added, quad + 1)
            v.tensor_scalar(slot_no[:, :], slot_no[:, :], float(SLOTS), None, ALU.add).then_inc(slot_moved, 1)
            dve.wait_ge(slot_moved, pas + 1)
        scale_of(seen + 1)
        dve.wait_ge(in_gain, 64)
        for tb in range(TB):
            ins = v.scalar_tensor_tensor(n3[:, tb, :], h[:, tb, :], stat[:, 6 + tb:7 + tb], gain_row[:, :], ALU.mult,
                                         ALU.mult)
            link(ins) if tb == 0 else ins.then_inc(fin_ready, 1)

    block_cm.__exit__(None, None, None)


_INS = ["x", "mem", "norm_mix_pre", "w_in", "w_pool_mix", "pool_scale", "w_pool_o", "w_sb_o", "norm_mem", "w_mem_kv",
        "w_x_o", "w_out", "norm_mix_post", "norm_ffn_pre", "w_ffn_in", "w_ffn_out", "norm_ffn_post", "g_mix_2",
        "w_in_2", "w_proj_a_2", "w_proj_b_2", "w_out_2", "g_ffn_2", "w_group_2", "b_group_2", "w_expert_2",
        "b_expert_2", "w1_2", "w3_2", "w2_2", "g_final_2"]


def kernel(**inputs):
    import concourse.bacc as bacc
    from concourse.bass_utils import run_bass_kernel_spmd

    nc = bacc.Bacc("TRN2", target_bir_lowering=False, num_devices=1)
    arrays, aps = {}, {}
    for name in _INS:
        x = np.ascontiguousarray(inputs[name])
        arrays[f"in_{name}"] = x
        aps[name] = nc.dram_tensor(f"in_{name}", x.shape, mybir.dt.from_np(x.dtype), kind="ExternalInput").ap()
    for name, x in (("table", make_table()), ("windows", make_windows())):
        arrays[f"in_{name}"] = x
        aps[name] = nc.dram_tensor(f"in_{name}", x.shape, F32, kind="ExternalInput").ap()
    out = nc.dram_tensor("out", (1, T, D), F32, kind="ExternalOutput").ap()
    layers_kernel(nc, aps, aps["table"], aps["windows"], out)
    r = run_bass_kernel_spmd(nc, [arrays], core_ids=[0])
    return r.results[0]["out"]
```

```python
import numpy as np
import concourse.bass as bass
from concourse import mybir

F32 = mybir.dt.float32
F32R = mybir.dt.float32r
I32 = mybir.dt.int32
ACT = mybir.ActivationFunctionType
ALU = mybir.AluOpType
AX = mybir.AxisListType

P = 128
T = 256
TB = T // P
D = 1024
KC = D // P
DH = 64
HEADS = 8
X_HEADS = 4
FF = 2816
UNIT = 2048
UC = 256
EPS = 1e-6
NEG = -1e30
TAKEN = -3e38
TOPK = T // 4
GROUPS, PER_GROUP = 4, 8
EXPERTS = GROUPS * PER_GROUP
EFF = 512
SLOTS = 32
QUAD = 4
WINDOWS = (2, 4, 8, 16)
CAUSAL = P + T

TABLE = {}
_at = 0
for _name, _n in (("ident", P), ("later", P), ("before", P), ("rotate", P), ("keep", CAUSAL), ("hide", CAUSAL),
                  ("cos", 2 * T), ("sin", 2 * T), ("slot", SLOTS), ("rev", EXPERTS), ("revg", GROUPS), ("steps", 8)):
    TABLE[_name] = (_at, _at + _n)
    _at += _n
TABLE_W = _at


def make_table():
    t = np.zeros((P, TABLE_W), np.float32)

    def put(name, value):
        a, b = TABLE[name]
        t[:, a:b] = value

    i, j = np.arange(P)[:, None], np.arange(P)[None, :]
    put("ident", i == j)
    put("later", i > j)
    put("before", i < j)
    rot = np.zeros((P, P), np.float32)
    for p in range(P):
        if p % DH < DH // 2:
            rot[p + DH // 2, p] = -1.0
        else:
            rot[p - DH // 2, p] = 1.0
    put("rotate", rot)
    put("keep", np.concatenate([i < j, np.ones((P, P)), i < j], 1))
    put("hide", np.where(np.concatenate([j <= i, np.ones((P, P), bool), j <= i], 1), 0.0, NEG))
    inv = np.power(np.float32(10000.0), -np.arange(0, DH, 2, dtype=np.float32) / np.float32(DH))
    ang = (np.arange(T, dtype=np.float32)[None, :] * inv[np.arange(P) % (DH // 2)][:, None]).astype(np.float32)
    put("cos", np.tile(np.cos(ang), (1, 2)))
    put("sin", np.tile(np.sin(ang), (1, 2)))
    put("slot", np.arange(SLOTS)[None, :])
    put("rev", EXPERTS - np.arange(EXPERTS)[None, :])
    put("revg", GROUPS - np.arange(GROUPS)[None, :])
    put("steps", SLOTS * np.arange(8)[None, :])
    return t


def make_windows():
    b = np.zeros((P, len(WINDOWS), CAUSAL), np.float32)
    for g, w in enumerate(WINDOWS):
        full = np.zeros((T, T), np.float32)
        for t in range(T):
            lo = max(t + 1 - w, 0)
            full[lo:t + 1, t] = np.float32(1.0) / np.float32(t + 1 - lo)
            full[t, t] -= 1.0
        b[:, g, 0:T] = full[0:P, :]
        b[:, g, T:CAUSAL] = full[P:T, P:T]
    return b


def unit_plan(a):
    units = []

    def add(name, w, c0, kc=KC, cols=UC, k0=0, **more):
        src = w[k0 * P:(k0 + kc) * P, c0:c0 + cols].rearrange("(c p) n -> p c n", p=P)
        units.append(dict(name=name, src=[(0, cols, src)], kc=kc, cols=cols, **more))

    kv, w_in = a["w_mem_kv"][0], a["w_in"][0]
    for name, c0, n, f in (("p", 0, 2, "A"), ("q", 512, 2, "B"), ("k", 1024, 2, "B"), ("v", 1536, 2, "A"),
                           ("xq", 2048, 1, "B")):
        for j in range(n):
            add(name, w_in, c0 + UC * j, form=f, j=j)
    add("mk", kv, 0, form="B")
    add("mv", kv, UC, form="A")
    for j in range(12):
        add("gate", w_in, 2304 + UC * j, form="B", j=j)
    branches = (("w_pool_o", 4, 0), ("w_sb_o", 4, 4), ("w_x_o", 2, 8))
    for b, j in [(0, j) for j in range(4)] + [(b, j) for j in range(4) for b in (1, 2)]:
        w, kc, o0 = branches[b]
        add("merge", a[w][0], UC * j, kc=kc, form="B", j=j, b=b, o0=o0, last=b == 2)
    for j in range(4):
        add("out", a["w_out"][0], UC * j, form="A", j=j)
    up, down = a["w_ffn_in"][0], a["w_ffn_out"][0]

    def add_down(i):
        src = down[i * UC:(i + 1) * UC, :].rearrange("(c p) n -> p c n", p=P)
        units.append(dict(name="down", src=[(0, D, src)], kc=2, cols=D, form="F", i=i))

    for i in range(FF // UC):
        add("g", up, UC * i, form="B", i=i)
        add("u", up, FF + UC * i, form="B", i=i)
        if i:
            add_down(i - 1)
    add_down(FF // UC - 1)
    w2 = a["w_in_2"][0]
    src = w2.rearrange("(c p) n -> p c n", p=P)
    units.append(dict(name="kiwi", kc=KC, cols=136, form="K",
                      src=[(0, DH, src[:, :, 3584:3584 + DH]), (DH, 136, src[:, :, 3584:3656])]))
    for name, c0, f in (("qi", 3072, "B"), ("kb", 2048, "B"), ("qb", 1536, "B"), ("vb", 2560, "A"),
                        ("ka", 512, "B"), ("qa", 0, "B"), ("va", 1024, "A")):
        for j in range(2):
            add(name, w2, c0 + UC * j, form=f, j=j)
    for j in range(8):
        add("gate2", w2, 3656 + UC * j, form="B", j=j)
    for b, (w, o0) in enumerate((("w_proj_a_2", 0), ("w_proj_b_2", 4))):
        for j in range(4):
            add("merge", a[w][0], UC * j, kc=4, form="B", j=j, b=b, o0=o0, last=b == 1)
    for j in range(4):
        add("out2", a["w_out_2"][0], UC * j, form="A", j=j)
    return units


ROPED = ("kiwi", "qi", "kb", "qb", "ka", "qa")
BY_VECTOR = ("merge", "u", "out", "out2")


def step_plan(units):
    first = {}
    for u, unit in enumerate(units):
        first.setdefault(unit["name"], u)
    plan = []
    ropes = 0

    def unit(u):
        plan.append(("unit", u))

    plan.append(("vectors",))
    plan.append(("norm", 0))
    unit(0)
    unit(1)
    plan.append(("norm", 1))
    for u in range(2, 11):
        unit(u)
        if u == 4:
            plan.append(("pool_window",))
    plan.append(("pool_mix",))
    for k in range(12):
        unit(first["gate"] + k)
        plan.append(("heads", *([x] if 0 <= x < 12 else [] for x in (k, k - 1, k - 2))))
    plan.append(("sigmoid", 0, 12))
    unit(first["merge"])
    plan.append(("heads", [], [11], [10]))
    unit(first["merge"] + 1)
    plan.append(("heads", [], [], [11]))
    for u in range(first["merge"] + 2, first["merge"] + 12):
        unit(u)
    for u in range(first["out"], first["out"] + 4):
        unit(u)
    plan.append(("post", 0))
    plan.append(("norm", 2))
    plan.append(("ffn",))
    plan.append(("post", 1))
    plan.append(("norm", 3))
    waiting = []
    for u in range(first["kiwi"], first["gate2"]):
        unit(u)
        n = u - first["kiwi"]
        if waiting:
            plan.append(("rope", *waiting.pop()))
        if units[u]["name"] in ROPED:
            waiting.append((ropes, u))
            ropes += 1
        if 4 <= n < 8:
            plan.append(("index", 2 * (n - 4)))
        if n >= 8:
            plan.append(("topk", n - 8))
    assert not waiting
    for k in range(8):
        unit(first["gate2"] + k)
        if k == 0:
            plan.append(("topk", 7))
            plan.append(("select",))
        pairs = ([12 + 2 * x, 13 + 2 * x] if 0 <= x < 8 else [] for x in (k, k - 1, k - 2))
        plan.append(("heads", *pairs))
    plan.append(("sigmoid", 12, 20))
    start = first["gate2"] + 8
    unit(start)
    plan.append(("heads", [], [26, 27], [24, 25]))
    unit(start + 1)
    plan.append(("heads", [], [], [26, 27]))
    for u in range(start + 2, start + 12):
        unit(u)
        if u > start + 8:
            plan.append(("route", u - start - 9))
    plan.append(("route", 3))
    return plan


def layers_kernel(nc, a, table, windows, out):
    units = unit_plan(a)
    plan = step_plan(units)
    U = len(units)
    G0 = next(u for u, x in enumerate(units) if x["name"] == "g")
    NF = FF // UC
    assert all(x["form"] != "F" or len(x["src"]) == 1 for x in units)

    base = -(-nc.sbuf_base // 64) * 64
    at = base

    def put(name, shape, dt, where=None):
        nonlocal at
        size = 4 * int(np.prod(shape[1:]))
        t = nc.alloc_sbuf_tensor_at(name, shape, dt, offset=at if where is None else where)
        if where is None:
            at += -(-size // 32) * 32
        return t

    SLOT_B = 4 * UNIT
    arena_at = at
    arena = put("arena", [P, 12, UNIT], F32)
    split_at = at
    w_hi = put("w_hi", [P, 3, UNIT], F32R)
    w_lo = put("w_lo", [P, 3, UNIT], F32R)
    split_end = at
    x_at = at
    x_hi = put("x_hi", [P, KC, T], F32R)
    x_lo = put("x_lo", [P, KC, T], F32R)
    o_at = at
    o_hi = put("o_hi", [P, 10, T], F32R)
    o_lo = put("o_lo", [P, 10, T], F32R)
    o_end = at
    h = put("h", [P, TB, D], F32)
    gain_rows = [put(f"gain_row{i}", [P, D], F32) for i in range(2)]
    tab = put("tab", [P, TABLE_W], F32)
    vec = put("vec", [P, 36], F32)
    ones = put("ones", [P, P], F32)
    stat = put("stat", [P, 8, 8], F32)
    sq_part = put("sq_part", [P, TB, 4], F32)
    minus_half = put("minus_half", [P, TB], F32)
    w_route = put("w_route", [P, KC, 36], F32)
    b_route = put("b_route", [P, 36], F32)
    softmax = put("softmax", [P, 16], F32)
    index_w = put("index_w", [P, TB, 8], F32)
    best8 = put("best8", [P, TB, 8], F32)
    passes_i = put("passes_i", [P, 1], I32)
    assert at <= nc.sbuf_usable_end, (at, nc.sbuf_usable_end)

    def const(name):
        lo, hi = TABLE[name]
        return tab[:, lo:hi]

    ident = const("ident")

    temp_at = arena_at + 3 * SLOT_B
    temp_end = arena_at + 12 * SLOT_B
    where = temp_at

    def temp(name, shape, dt=F32, at_=None):
        nonlocal where
        if at_ is None:
            at_ = where
            where += 4 * int(np.prod(shape[1:]))
            assert where <= temp_end, name
        return nc.alloc_sbuf_tensor_at(name, shape, dt, offset=at_)

    hw = [[temp(f"head_{n}{i}", [P, 2 * T]) for i in range(2)] for n in ("score", "prob", "expo", "right")]
    score_b, prob_b, expo_b, right_b = hw
    heads_end = where
    p_tok = temp("p_tok", [P, TB, 512])
    q1 = temp("q1", [P, 4, T])
    k1 = temp("k1", [P, 4, T])
    v1 = temp("v1", [P, TB, 512])
    xq = temp("xq", [P, 2, T])
    mk = temp("mk", [P, 2, T])
    mv = temp("mv", [P, TB, T])
    gates_at = where
    gates = temp("gates", [P, 24, T])
    win = temp("win", [P, 4, CAUSAL])
    pool_w_sb = temp("pool_w_sb", [P, 4, P])
    mixed = temp("mixed", [P, 4, T], at_=gates_at + 16384 + 1024)
    x_f = temp("x_f", [P, KC, T], at_=gates_at)
    rstd_row = temp("rstd_row", [P, T], at_=gates_at + 16384)
    junk = temp("junk", [P, D], at_=temp_at)
    mem_tok = temp("mem_tok", [P, TB, D], at_=gates_at + 8192)
    rows = temp("rows", [36, P], at_=gates_at + 16384 + 5120)
    y_tok = temp("y_tok", [P, TB, D], at_=gates_at + 8192)
    silu_g = temp("silu_g", [P, 2 * T], at_=heads_end)
    act_f = temp("act_f", [P, 2 * T], at_=heads_end + 2048)
    where = heads_end
    qi, kb, qb, ka, qa = (temp(n, [P, 4, T]) for n in ("qi", "kb", "qb", "ka", "qa"))
    vb, va = (temp(n, [P, TB, 512]) for n in ("vb", "va"))
    ki = temp("ki", [P, T])
    score = temp("score", [P, CAUSAL])
    work = temp("work", [P, CAUSAL])
    gates2_at = arena_at + 10 * SLOT_B
    assert where <= gates2_at
    where = gates2_at
    gates2 = temp("gates2", [P, 16, T])
    x_f2 = temp("x_f2", [P, KC, T], at_=gates2_at)

    third = [nc.alloc_sbuf_tensor_at(f"third_w{n}", [P, 2, UNIT], F32, offset=o)
             for n, o in ((1, x_at), (3, split_at), (2, split_at + 2 * SLOT_B))]
    n3 = nc.alloc_sbuf_tensor_at("n3", [P, TB, D], F32, offset=o_at)
    n3T = nc.alloc_sbuf_tensor_at("n3T", [P, KC, T], F32, offset=o_at + 8192)
    mo = split_at + 4 * SLOT_B

    def moe(name, shape, dt=F32, where=None):
        nonlocal mo
        size = -(-4 * int(np.prod(shape[1:])) // 32) * 32
        if where is None:
            where = mo
            mo += size
        assert mo <= split_end, name
        return nc.alloc_sbuf_tensor_at(name, shape, dt, offset=where)

    assert o_end - o_at >= 16384 + 4096
    y_quad = moe("y_quad", [P, D], where=o_at + 16384)
    logits = moe("logits", [P, TB, 36])
    exp_in = moe("exp_in", [P, TB, 36])
    exp_out = moe("exp_out", [P, TB, 36])
    masked_e = moe("masked_e", [P, TB, EXPERTS])
    pick = moe("pick", [P, TB, EXPERTS])
    pick_one = moe("pick_one", [P, TB, EXPERTS])
    pick_g = moe("pick_g", [P, TB, GROUPS])
    r_s = moe("r_s", [P, 16, TB])
    chosen = moe("chosen", [P, TB, EXPERTS])
    gate_e = moe("gate_e", [P, TB, EXPERTS])
    rank = moe("rank", [P, TB, EXPERTS])
    slot_no = moe("slot_no", [P, SLOTS])
    one_hot = moe("one_hot", [P, TB, P])
    gated_hot = moe("gated_hot", [P, TB, P])
    gate_T = moe("gate_T", [P, T])
    xg = moe("xg", [P, KC, P])
    silu_e = moe("silu_e", [P, P])
    hid = moe("hid", [P, P])
    hid_T = moe("hid_T", [P, P])

    ps = nc.alloc_psum_tensor("ps", [P, 8, 512], F32)

    bank_of, bank_before = {}, {}
    turn, last_in = 0, {}
    for u, x in enumerate(units):
        if x["form"] == "F":
            continue
        bank = {"g": 0, "u": 1}.get(x["name"], turn % 2)
        turn = bank + 1
        bank_of[u], bank_before[u] = bank, last_in.get(bank)
        last_in[bank] = u
    rope_of = {u: r for r, u in enumerate(u for u, x in enumerate(units) if x["name"] in ROPED)}
    SLOT_OF = ((10, 0, 2), (4, 6, 8))

    def slots(first, blocks):
        return arena[:, first:first + 2, :].rearrange("p s (c n) -> p (s c) n", c=blocks // 2)

    even_w, odd_w = ([slots(s, b) for s, b in zip(at3, (KC, KC, 4))] for at3 in SLOT_OF)
    third_w = [t[:, :, :].rearrange("p s (c n) -> p (s c) n", c=b // 2) for t, b in zip(third, (KC, KC, 4))]

    def sem(name):
        return nc.alloc_semaphore(name)

    landed = [sem(f"unit_landed{i}") for i in range(3)]
    hi_ready, lo_ready = sem("w_hi_ready"), sem("w_lo_ready")
    unit_done = sem("unit_done")
    out_act, out_dve = sem("unit_out_act"), sem("unit_out_dve")
    in_mem, in_rows, in_ident, in_table, in_win, in_mix = (
        sem(f"in_{n}") for n in ("mem", "rows", "ident", "table", "windows", "mix"))
    in_x = [sem("in_x0"), sem("in_x1")]
    in_gain = [sem("in_gain0"), sem("in_gain1")]
    h_ready, sq_ready, y_half, sq_half = sem("h_ready"), sem("sq_part_ready"), sem("ffn_y_half"), sem("ffn_sq_half")
    row_done, f_ready, xh_ready, x_ready = sem("rstd_row_done"), sem("x_f_ready"), sem("x_hi_ready"), sem("x_ready")
    half_ready, sig_ready = sem("minus_half_ready"), sem("gate_sigmoid")
    hg_ready, route_T, route_out = sem("hg_ready"), sem("route_T"), sem("route_out")
    vec_T, vec_ready = sem("vec_T"), sem("vec_ready")
    sq_done, mean_done, root_done, norm_T = (sem(n) for n in ("sq_done", "mean_done", "rstd_done", "norm_T"))
    pool_w, pool_mixed, pool_p, pool_out = (sem(n) for n in ("pool_w", "pool_mixed", "pool_p", "pool_out"))
    z_done, prep_done, exp_done, mid_ready, mid_done, expo_ready, a_done, right_ready, o_done, pair_out = (
        sem(n) for n in ("z_done", "prep_done", "exp_done", "mid_ready", "mid_done", "expo_ready", "a_done",
                         "right_ready", "o_done", "pair_out"))
    merged_ready = sem("merged_ready")
    act_hi, act_ready = sem("ffn_act_hi"), sem("ffn_act_ready")
    rot_done, rope_done, wi_T = sem("rot_done"), sem("rope_done"), sem("wi_out")
    ix_z, ix_relu, ix_acc = sem("index_z"), sem("index_relu"), sem("index_acc")
    select_done = sem("select_done")
    act_chain, dve_chain = sem("act_chain"), sem("dve_chain")
    in_route, n3_ready = sem("in_route"), sem("n3_ready")
    logit_done, route_sel, rank_done, passes_ready = (sem(n) for n in ("logit_done", "route_sel", "rank_done",
                                                                       "passes_ready"))
    landed_w = [[sem(f"{parity}_w{n}") for n in (1, 3, 2)] for parity in ("even", "odd")]
    in_third3 = [sem(f"third_w{n}_in") for n in (1, 3, 2)]
    route_in, route_exp = sem("route_in"), sem("route_exp")
    xg_part, hot_part, slot_moved = sem("xg_part"), sem("hot_part"), sem("slot_moved")
    hot_ready, xg_done, xg_ready, gt_done, gt_ready = (sem(n) for n in ("hot_ready", "xg_done", "xg_ready",
                                                                        "gt_done", "gt_ready"))
    e_up, e_silu, e_hid, e_T, e_hidT, e_y, e_yA, e_yD = (sem(n) for n in (
        "e_up", "e_silu", "e_hid", "e_T", "e_hidT", "e_y", "e_y_act", "e_y_dve"))
    comb_done, comb_added = sem("comb_done"), sem("comb_added")
    fin_ready, fin_out = sem("final_ready"), sem("final_out")

    def landings(u):
        return 16 * sum(len(units[v]["src"]) for v in range(u % 3, u + 1, 3))

    def outs(u, vector):
        return sum((x["name"] in BY_VECTOR) == vector for x in units[:u + 1] if x["form"] != "F")

    def wait_out(eng, u):
        if units[u]["name"] in BY_VECTOR:
            eng.wait_ge(out_dve, outs(u, True))
        else:
            eng.wait_ge(out_act, outs(u, False))

    def kind(k):
        return "sb" if k < 8 else "x" if k < 12 else "moba" if k < 20 else "dsa"

    def pair_slot(k):
        return 4 + k // 2 if k < 12 else (k - 12) // 2

    def head_in(k):
        kd = kind(k)
        j = {"sb": k, "x": k - 8, "moba": k - 12, "dsa": k - 20}[kd]
        q, kk, v = {"sb": (q1, k1, v1), "x": (xq, mk, mv), "moba": (qa, ka, va), "dsa": (qb, kb, vb)}[kd]
        p0 = DH * (j % 2)
        return q[p0:p0 + DH, j // 2, :], kk[p0:p0 + DH, j // 2, :], v[:, :, DH * j:DH * j + DH], p0

    first = {}
    for u, x in enumerate(units):
        first.setdefault(x["name"], u)
    second_merge = first["gate2"] + 8
    N_ROPE = len(rope_of)
    norm_event, post_event, moe_event, last_event = (0, 1, 3, 5), (2, 4), 6, 7
    out0, out20 = first["out"], first["out2"]
    S2 = G0 + 2

    def ffn_loop(eng, triple):
        triple(1)
        with eng.Fori(2, NF - 1) as i:
            triple(i)
        triple(NF - 1)

    block_cm = nc.Block()
    block = block_cm.__enter__()

    @block.sync
    def _(sp):
        def load(u):
            if u >= 3:
                sp.wait_ge(lo_ready, u - 2)
            kc, cols = units[u]["kc"], units[u]["cols"]
            dst = arena[:, u % 3, 0:kc * cols].rearrange("p (c n) -> p c n", c=kc)
            for c0, c1, src in units[u]["src"]:
                sp.dma_start(dst[:, :, c0:c1], src).then_inc(landed[u % 3], 16)

        load(0)
        load(1)
        sp.dma_start(mem_tok[:, :, :], a["mem"][0].rearrange("(b p) n -> p b n", p=P)).then_inc(in_mem, 16)
        for u in range(2, S2 + 3):
            load(u)
        up_v = a["w_ffn_in"][0].rearrange("(c p) n -> p c n", p=P)
        down_v = a["w_ffn_out"][0].rearrange("(c p) n -> p c n", p=P)
        with sp.Fori(2, NF - 1) as i:
            addresses = [sp.snap(i * UC), sp.snap(i * UC + FF), sp.snap(i * 2 - 2)]
            freed = [sp.snap(i * 3 + (S2 - 3 + j - 2)) for j in range(3)]
            for j in range(3):
                s = (S2 + j) % 3
                sp.wait_ge(lo_ready, freed[j])
                if j < 2:
                    dst = arena[:, s, :].rearrange("p (c n) -> p c n", c=KC)
                    src = up_v[:, :, bass.ds(addresses[j], UC)]
                else:
                    dst = arena[:, s, :].rearrange("p (c n) -> p c n", c=2)
                    src = down_v[:, bass.ds(addresses[j], 2), :]
                sp.dma_start(dst, src).then_inc(landed[s], 16)
        w1, w3, w2 = a["w1_2"][0], a["w3_2"][0], a["w2_2"][0]
        sources = (w1.rearrange("e (p c) f -> p e c f", c=KC), w3.rearrange("e (p c) f -> p e c f", c=KC),
                   w2.rearrange("e (c p) n -> p e c n", p=P))

        def expert_load(e, places, which, landing):
            src = sources[which][:, bass.ds(e, 1), :, :].rearrange("p e c n -> p (e c) n")
            sp.dma_start(places[which], src).then_inc(landing, 16)

        for u in range(S2 + 3 * (NF - 2), U):
            if u == second_merge + 7:
                sp.wait_ge(o_done, 28)
                for which in range(3):
                    expert_load(0, odd_w, which, landed_w[1][which])
            if u == U - 1:
                sp.wait_ge(merged_ready, 8)
                expert_load(1, even_w, 0, landed_w[0][0])
            load(u)
        sp.wait_ge(lo_ready, U)
        expert_load(1, even_w, 1, landed_w[0][1])
        expert_load(1, even_w, 2, landed_w[0][2])
        sp.wait_ge(unit_done, U)
        for which in range(3):
            expert_load(2, third_w, which, in_third3[which])
        for which in range(3):
            sp.wait_ge(e_y if which == 2 else e_up, 1)
            expert_load(3, odd_w, which, landed_w[1][which])

        def stream(pass_, lo_pair):
            with sp.Fori(lo_pair, EXPERTS // 2) as i:
                for odd in range(2):
                    e = sp.snap(i * 2 + odd)
                    used = sp.snap(i * 2 + (pass_ * EXPERTS + odd - 1))
                    for which in range(3):
                        sp.wait_ge(e_y if which == 2 else e_up, used)
                        expert_load(e, (even_w, odd_w)[odd], which, landed_w[odd][which])

        stream(0, 2)
        sp.wait_ge(passes_ready, 1)
        n_pass = sp.value_load(passes_i[0:1, 0:1], min_val=1, max_val=T // SLOTS)
        with sp.If(n_pass > 1):
            with sp.Fori(1, n_pass) as again:
                stream(again, 0)
            sp.nop()
        for tb in range(TB):
            sp.wait_ge(fin_ready, tb + 1)
            sp.dma_start(out[0, P * tb:P * tb + P, :], n3[:, tb, :]).then_inc(fin_out, 16)
        sp.wait_ge(fin_out, 32)

    @block.gpsimd
    def _(pool):
        nc.gpsimd.memset(minus_half[:, :], -0.5).then_inc(half_ready, 1)
        pool.wait_ge(half_ready, 1)

        def row_load(i, v):
            pool.dma_start(gain_rows[i][:, :], v.partition_broadcast(P)).then_inc(in_gain[i], 16)

        def inverse_root(n):
            pool.wait_ge(mean_done, n + 1)
            nc.gpsimd.tensor_tensor(stat[:, n, 6:8], stat[:, n, 2:4], minus_half[:, :], ALU.pow).then_inc(root_done, 1)

        rest = TABLE["ident"][1]
        pool.dma_start(tab[:, rest:], table[:, rest:]).then_inc(in_table, 16)
        pool.dma_start(win[:, :, :], windows).then_inc(in_win, 16)
        inverse_root(0)
        inverse_root(1)
        row_load(0, a["norm_mix_post"][0])
        row_load(1, a["norm_ffn_post"][0])
        for c0, n, w, b in ((0, GROUPS, "w_group_2", "b_group_2"), (GROUPS, EXPERTS, "w_expert_2", "b_expert_2")):
            pool.dma_start(w_route[:, :, c0:c0 + n], a[w][0].rearrange("(c p) n -> p c n", p=P))\
                .then_inc(in_route, 16)
            pool.dma_start(b_route[:, c0:c0 + n], a[b][0].partition_broadcast(P)).then_inc(in_route, 16)
        inverse_root(2)
        row_load(0, a["g_ffn_2"][0])
        inverse_root(3)
        inverse_root(4)
        row_load(1, a["g_final_2"])
        inverse_root(5)
        inverse_root(6)
        inverse_root(7)

    @block.tensor
    def _(pe):
        mm = nc.tensor.matmul

        def three(dst, l_hi, l_lo, r_hi, r_lo, start, stop):
            mm(dst, l_hi, r_hi, start=start, stop=False)
            mm(dst, l_hi, r_lo, start=False, stop=False)
            return mm(dst, l_lo, r_hi, start=False, stop=stop)

        def unit(u):
            x = units[u]
            kc, cols, s = x["kc"], x["cols"], u % 3
            hi = w_hi[:, s, 0:kc * cols].rearrange("p (c n) -> p c n", c=kc)
            lo = w_lo[:, s, 0:kc * cols].rearrange("p (c n) -> p c n", c=kc)
            pe.wait_ge(lo_ready, u + 1)
            if x["form"] == "F":
                return down(x["i"], hi, lo)
            if bank_before[u] is not None:
                wait_out(pe, bank_before[u])
            part_ready = None
            if u in after_norm:
                n = after_norm.index(u)
                part_ready = lambda c: pe.wait_ge(x_ready, 4 * n + c // 2 + 1)
            elif u in (out0, out20):
                n = 4 if u == out20 else 0
                part_ready = lambda c: pe.wait_ge(merged_ready, n + c // 2 + 1)
            dense(x, bank_of[u], hi, lo, part_ready).then_inc(unit_done, 1)

        def dense(x, bank, hi, lo, part_ready=None):
            kc, cols = x["kc"], x["cols"]
            a_hi, a_lo, o = x_hi, x_lo, 0
            if x["name"] in ("merge", "mk", "mv"):
                a_hi, a_lo, o = o_hi, o_lo, x.get("o0", 0)
            if x["form"] == "A":
                for tb in range(TB):
                    for c in range(kc):
                        if part_ready and tb == 0 and c % 2 == 0:
                            part_ready(c)
                        tok = slice(P * tb, P * tb + P)
                        last = three(ps[:, bank, cols * tb:cols * tb + cols], a_hi[:, o + c, tok],
                                     a_lo[:, o + c, tok], hi[:, c, :], lo[:, c, :], c == 0, c == kc - 1)
            elif x["form"] == "B":
                for nb in range(cols // P):
                    for c in range(kc):
                        if part_ready and nb == 0 and c % 2 == 0:
                            part_ready(c)
                        col = slice(P * nb, P * nb + P)
                        last = three(ps[:, bank, T * nb:T * nb + T], hi[:, c, col], lo[:, c, col],
                                     a_hi[:, o + c, :], a_lo[:, o + c, :], c == 0, c == kc - 1)
            else:
                for c in range(kc):
                    if c % 2 == 0:
                        part_ready(c)
                    three(ps[:, bank, 0:T], hi[:, c, 0:P], lo[:, c, 0:P], a_hi[:, c, :], a_lo[:, c, :],
                          c == 0, c == kc - 1)
                for tb in range(TB):
                    for c in range(kc):
                        tok = slice(P * tb, P * tb + P)
                        last = three(ps[:, bank, T + 8 * tb:T + 8 * tb + 8], a_hi[:, c, tok], a_lo[:, c, tok],
                                     hi[:, c, P:P + 8], lo[:, c, P:P + 8], c == 0, c == kc - 1)
            return last

        def down(i, hi, lo):
            first, end = isinstance(i, int) and i == 0, isinstance(i, int) and i == NF - 1
            pe.wait_ge(act_ready, i + 1)
            for c in range(2):
                for tb in range(TB):
                    for half in range(2):
                        tok, col = slice(P * tb, P * tb + P), slice(512 * half, 512 * half + 512)
                        last = three(ps[:, 4 + 2 * tb + half, :], o_hi[:, c, tok], o_lo[:, c, tok],
                                     hi[:, c, col], lo[:, c, col], first and c == 0, end and c == 1)
            last.then_inc(unit_done, 1)

        def triple(i):
            for j in range(3):
                x, s = units[S2 + j], (S2 + j) % 3
                pe.wait_ge(lo_ready, i * 3 + (S2 - 3 + j + 1))
                shape = dict(c=x["kc"])
                hi = w_hi[:, s, :].rearrange("p (c n) -> p c n", **shape)
                lo = w_lo[:, s, :].rearrange("p (c n) -> p c n", **shape)
                if j == 2:
                    down(i - 1, hi, lo)
                    continue
                if j == 0:
                    pe.wait_ge(out_act, i + outs(G0 - 1, False))
                else:
                    pe.wait_ge(out_dve, i + outs(G0 - 1, True))
                dense(x, j, hi, lo).then_inc(unit_done, 1)

        after_norm = (first["p"], first["mk"], first["g"], first["kiwi"])

        def norm(n):
            src = (h, mem_tok, h, h)[n]
            if n == 1:
                pe.wait_ge(in_mem, 16)
                pe.wait_ge(f_ready, 4)
            for tb in range(TB):
                if n == 0:
                    pe.wait_ge(in_x[tb], 16)
                elif n >= 2:
                    pe.wait_ge(h_ready, TB * (n - 2) + tb + 1)
                for c in range(KC):
                    last = nc.tensor.transpose(ps[:, 2 + c // 2, T * (c % 2) + P * tb:T * (c % 2) + P * tb + P],
                                               src[:, tb, P * c:P * c + P], ident)
                    if tb and c % 2:
                        last.then_inc(norm_T, 1)
            pe.wait_ge(root_done, norm_event[n] + 1)
            for tb in range(TB):
                scale = stat[:, norm_event[n], 6 + tb:7 + tb].to_broadcast([P, P])
                last = mm(ps[:, 6, P * tb:P * tb + P], scale, ident, start=True, stop=True)
            last.then_inc(row_done, 1)

        def scores(k, lo):
                q, kk, v, p0 = head_in(k)
                if k >= lo + 2:
                    pe.wait_ge(mid_ready, k - 1)
                bank = 4 + k % 2
                if kind(k) == "sb":
                    mm(ps[:, bank, 0:T], kk[:, 0:P], q, start=True, stop=True)
                    last = mm(ps[:, bank, T:CAUSAL], kk[:, P:T], q[:, P:T], start=True, stop=True)
                elif kind(k) == "x":
                    for tb in range(TB):
                        last = mm(ps[:, bank, T * tb:T * tb + T], q[:, P * tb:P * tb + P], kk, start=True,
                                  stop=True)
                else:
                    mm(ps[:, bank, 0:P], q[:, 0:P], kk[:, 0:P], start=True, stop=True)
                    last = mm(ps[:, bank, P:CAUSAL], q[:, P:T], kk, start=True, stop=True)
                last.then_inc(z_done, 1)

        def middle(k, lo):
                pe.wait_ge(mid_ready, k + 1)
                if k >= lo + 2:
                    pe.wait_ge(right_ready, k - 1)
                m, src = ps[:, (6, 2)[k % 2], :], prob_b[k % 2]
                if kind(k) == "sb":
                    later = const("later")
                    mm(m[:, 0:T], later, src[:, 0:T], start=True, stop=False)
                    mm(m[:, P:T], ones[:, :], src[:, T:CAUSAL], start=False, stop=True)
                    last = mm(m[:, T:CAUSAL], later, src[:, T:CAUSAL], start=True, stop=True)
                elif kind(k) == "x":
                    for tb in range(TB):
                        for mb in range(TB):
                            last = nc.tensor.transpose(m[:, T * mb + P * tb:T * mb + P * tb + P],
                                                       src[:, T * tb + P * mb:T * tb + P * mb + P], ident)
                else:
                    for t in range(3):
                        last = nc.tensor.transpose(m[:, P * t:P * t + P], src[:, P * t:P * t + P], ident)
                last.then_inc(mid_done, 1)

        def values(k, lo):
                q, kk, v, p0 = head_in(k)
                pe.wait_ge(right_ready, k + 1)
                if k % 2 == 0 and k >= lo + 4:
                    pe.wait_ge(pair_out, k // 2 - 1)
                o = ps[p0:p0 + DH, (7, 3)[k // 2 % 2], :]
                r = right_b[k % 2]
                mm(o[:, 0:T], v[:, 0, :], r[:, 0:T], start=True, stop=False)
                if kind(k) == "x":
                    last = mm(o[:, 0:T], v[:, 1, :], r[:, T:2 * T], start=False, stop=True)
                else:
                    last = mm(o[:, P:T], v[:, 1, :], r[:, T:CAUSAL], start=False, stop=True)
                last.then_inc(o_done, 1)

        def route_logits(r):
            pe.wait_ge(route_out, r + 1)
            if r == 0:
                pe.wait_ge(in_route, 64)
            for tb in range(TB):
                for c in (2 * r, 2 * r + 1):
                    last = mm(ps[:, 6 + tb, 0:36], n3T[:, c, P * tb:P * tb + P], w_route[:, c, :], start=c == 0,
                              stop=c == KC - 1)
            if r == 3:
                last.then_inc(logit_done, 1)

        for step, *arg in plan:
            if step == "vectors":
                pe.wait_ge(in_rows, 80)
                pe.wait_ge(in_ident, 16)
                nc.tensor.transpose(ps[:, 7, 0:36], rows[:, :], ident[0:36, 0:36]).then_inc(vec_T, 1)
            elif step == "norm":
                norm(arg[0])
            elif step == "unit":
                u = arg[0]
                if units[u]["name"] == "merge" and units[u]["j"] == 0:
                    if units[u]["b"] == 0:
                        pe.wait_ge(*((pool_out, 1) if u < G0 else (pair_out, 10)))
                    else:
                        pe.wait_ge(pair_out, 6 if u < G0 else 14)
                unit(u)
            elif step == "pool_window":
                wait_out(pe, first["p"] + 1)
                pe.wait_ge(in_win, 16)
                pe.wait_ge(f_ready, 5)
                for g in range(4):
                    dst = ps[:, 6, T * g:T * g + T] if g < 2 else ps[:, 7, T * (g - 2):T * (g - 2) + T]
                    col = slice(P * g, P * g + P)
                    mm(dst, p_tok[:, 0, col], win[:, g, 0:T], start=True, stop=False)
                    last = mm(dst[:, P:T], p_tok[:, 1, col], win[:, g, T:CAUSAL], start=False, stop=True)
                last.then_inc(pool_w, 1)
            elif step == "pool_mix":
                pe.wait_ge(pool_mixed, 1)
                pe.wait_ge(in_mix, 16)
                for g in range(4):
                    dst = ps[:, 6, T * g:T * g + T] if g < 2 else ps[:, 7, T * (g - 2):T * (g - 2) + T]
                    last = mm(dst, pool_w_sb[:, g, :], mixed[:, g, :], start=True, stop=True)
                last.then_inc(pool_p, 1)
            elif step == "heads":
                s_, m_, v_ = arg
                lo = 0 if max(s_ + m_ + v_) < 12 else 12
                if s_ == [0]:
                    wait_out(pe, first["xq"])
                if s_ == [1]:
                    pe.wait_ge(pool_out, 1)
                if s_ == [8]:
                    wait_out(pe, first["mv"])
                if 12 in s_:
                    pe.wait_ge(rope_done, N_ROPE)
                    wait_out(pe, first["va"] + 1)
                    pe.wait_ge(ix_acc, 8)
                if lo == 0:
                    for part, ks in ((scores, s_), (middle, m_), (values, v_)):
                        for k in ks:
                            part(k, lo)
                else:
                    for part, ks in ((values, v_), (middle, m_), (scores, s_)):
                        for k in ks:
                            part(k, lo)
            elif step == "ffn":
                unit(G0)
                unit(G0 + 1)
                ffn_loop(pe, triple)
                unit(S2 + 3 * (NF - 1))
            elif step == "rope":
                r, u = arg
                wait_out(pe, u)
                if r >= 1:
                    pe.wait_ge(rope_done, r)
                n = T if r == 0 else 2 * T
                mm(ps[:, 7, 0:n], const("rotate"), prob_b[r % 2][:, 0:n], start=True, stop=True)\
                    .then_inc(rot_done, 1)
            elif step == "index":
                pe.wait_ge(rope_done, 3)
                for i in (arg[0], arg[0] + 1):
                    p0 = DH * (i % 2)
                    q, kk, bank = qi[p0:p0 + DH, i // 2, :], ki[p0:p0 + DH, :], 4 + i % 2
                    if i >= 2:
                        pe.wait_ge(ix_relu, i - 1)
                    mm(ps[:, bank, 0:P], q[:, 0:P], kk[:, 0:P], start=True, stop=True)
                    mm(ps[:, bank, P:CAUSAL], q[:, P:T], kk, start=True, stop=True).then_inc(ix_z, 1)
            elif step == "route":
                r = arg[0]
                if r:
                    route_logits(r - 1)
                pe.wait_ge(hg_ready, r + 1)
                for tb in range(TB):
                    for c in range(2):
                        last = nc.tensor.transpose(ps[:, 2 + r, T * c + P * tb:T * c + P * tb + P],
                                                   n3[:, tb, UC * r + P * c:UC * r + P * c + P], ident)
                last.then_inc(route_T, 1)
            elif step in ("post", "topk", "select", "sigmoid"):
                pass
            else:
                raise ValueError(step)

        route_logits(3)
        pe.wait_ge(route_sel, 1)
        before = const("before")
        mm(ps[:, 1, 0:EXPERTS], before, chosen[:, 0, :], start=True, stop=True)
        mm(ps[:, 1, EXPERTS:2 * EXPERTS], before, chosen[:, 1, :], start=True, stop=False)
        mm(ps[:, 1, EXPERTS:2 * EXPERTS], ones[:, :], chosen[:, 0, :], start=False, stop=True)
        mm(ps[:, 1, 64:64 + EXPERTS], ones[:, :], chosen[:, 0, :], start=True, stop=False)
        mm(ps[:, 1, 64:64 + EXPERTS], ones[:, :], chosen[:, 1, :], start=False, stop=True).then_inc(rank_done, 1)

        def quad_body(q):
            looped = not isinstance(q, int)
            e0 = pe.snap(q * QUAD) if looped else 0
            pe.wait_ge(hot_ready, q + 1)
            for c in range(KC):
                for tb in range(TB):
                    last = mm(ps[:, 2 + c // 4, P * (c % 4):P * (c % 4) + P], n3[:, tb, c:D:KC],
                              one_hot[:, tb, :], start=tb == 0, stop=tb == 1)
            last.then_inc(xg_done, 1)
            for tb in range(TB):
                last = nc.tensor.transpose(ps[:, 0, P * tb:P * tb + P], gated_hot[:, tb, :], ident)
            last.then_inc(gt_done, 1)
            pe.wait_ge(xg_ready, q + 1)
            for e in range(QUAD):
                if looped:
                    places, landing = (even_w, odd_w)[e % 2], landed_w[e % 2]
                    arrived = pe.snap(q * 32 + 8 * (e + e % 2))
                else:
                    places = (odd_w, even_w, third_w, odd_w)[e]
                    landing = (landed_w[1], landed_w[0], in_third3, landed_w[1])[e]
                    arrived = (16, 16, 16, 32)[e]
                done = pe.snap(e0 + e) if looped else e
                for n in range(2):
                    pe.wait_ge(landing[n], arrived)
                    for c in range(KC):
                        for g in range(4):
                            last = mm(ps[SLOTS * g:SLOTS * g + SLOTS, 4 + e % 2, P * n:P * n + P],
                                      xg[:, c, SLOTS * e:SLOTS * e + SLOTS], places[n][:, c, P * g:P * g + P],
                                      start=c == 0, stop=c == KC - 1, tile_position=(0, SLOTS * g))
                last.then_inc(e_up, 1)
                pe.wait_ge(e_hid, done + 1)
                nc.tensor.transpose(ps[:, 6, 0:P], hid[:, :], ident).then_inc(e_T, 1)
                pe.wait_ge(landing[2], arrived)
                pe.wait_ge(e_hidT, done + 1)
                for b in range(4):
                    for g in range(4):
                        last = mm(ps[SLOTS * g:SLOTS * g + SLOTS, 7, 0:UC],
                                  hid_T[:, SLOTS * b:SLOTS * b + SLOTS], places[2][:, b, UC * g:UC * g + UC],
                                  start=b == 0, stop=b == 3, tile_position=(0, SLOTS * g))
                last.then_inc(e_y, 1)
            pe.wait_ge(gt_ready, q + 1)
            pe.wait_ge(e_yA, e0 * 2 + 2 * QUAD)
            pe.wait_ge(e_yD, e0 * 2 + 2 * QUAD)
            for tb in range(TB):
                for half in range(2):
                    last = mm(ps[:, 2 * tb + half, :], gate_T[:, P * tb:P * tb + P],
                              y_quad[:, 512 * half:512 * half + 512], start=True, stop=True)
            last.then_inc(comb_done, 1)

        quad_body(0)
        pe.wait_ge(passes_ready, 1)
        n_pass = pe.value_load(passes_i[0:1, 0:1], min_val=1, max_val=T // SLOTS)
        with pe.Fori(1, n_pass * (EXPERTS // QUAD)) as q:
            quad_body(q)

    @block.scalar
    def _(act):
        chain = [0]
        fn = nc.scalar.activation

        def link(ins):
            chain[0] += 1
            ins.then_inc(act_chain, 1)
            act.wait_ge(act_chain, chain[0])

        for tb in range(TB):
            act.dma_start(h[:, tb, :], a["x"][0, P * tb:P * tb + P, :]).then_inc(in_x[tb], 16)
        act.dma_start(ident, table[:, 0:P]).then_inc(in_ident, 16)
        r = 0
        for name, n in (("norm_mem", 8), ("norm_mix_pre", 8), ("pool_scale", 4), ("norm_ffn_pre", 8),
                        ("g_mix_2", 8)):
            act.dma_start(rows[r:r + n, :], a[name][0].rearrange("(r n) -> r n", n=P)).then_inc(in_rows, 16)
            r += n
        act.dma_start(pool_w_sb[:, :, :], a["w_pool_mix"][0].rearrange("g c d -> c g d")).then_inc(in_mix, 16)

        def split(u):
            if u >= U:
                return
            x = units[u]
            n = x["kc"] * x["cols"]
            if u >= 3:
                act.wait_ge(unit_done, u - 2)
            act.wait_ge(landed[u % 3], landings(u))
            fn(w_hi[:, u % 3, 0:n], arena[:, u % 3, 0:n], ACT.Copy).then_inc(hi_ready, 1)

        def split_ffn(i, j):
            if isinstance(i, int):
                return split(S2 + 3 * (i - 1) + j + 2)
            s = (S2 + j + 2) % 3
            act.wait_ge(unit_done, i * 3 + (S2 - 3 + j))
            act.wait_ge(landed[s], i * 16 + (landings(S2 + 3 + j + 2) - 32))
            fn(w_hi[:, s, :], arena[:, s, :], ACT.Copy).then_inc(hi_ready, 1)

        copies = {"mk": mk, "q": q1, "k": k1, "xq": xq}
        tokens = {"mv": mv, "p": p_tok, "v": v1, "vb": vb, "va": va}

        def evacuate(u):
            x = units[u]
            name, j = x["name"], x.get("j", 0)
            full = ps[:, bank_of[u], :]
            act.wait_ge(unit_done, u + 1)
            if name in copies:
                scale = 0.125 if name in ("q", "xq") else 1.0
                dst = copies[name][:, 2 * j:2 * j + 2, :].rearrange("p a b -> p (a b)")
                fn(dst, full, ACT.Copy, scale=scale).then_inc(out_act, 1)
            elif name in tokens:
                fn(tokens[name][:, :, UC * j:UC * j + UC], full.rearrange("p (a b) -> p a b", a=2), ACT.Copy)\
                    .then_inc(out_act, 1)
            elif name in ("gate", "gate2"):
                g = gates if name == "gate" else gates2
                fn(g[:, 2 * j:2 * j + 2, :].rearrange("p a b -> p (a b)"), full, ACT.Copy).then_inc(out_act, 1)
            elif name == "kiwi":
                link(fn(index_w[:, :, :].rearrange("p a b -> p (a b)"), full[:, T:T + 16], ACT.Copy,
                        scale=512.0 ** -0.5))
                fn(prob_b[0][:, 0:T], full[:, 0:T], ACT.Copy).then_inc(out_act, 1)
            elif name in ROPED:
                r = rope_of[u]
                if r >= 2:
                    act.wait_ge(rope_done, r - 1)
                fn(prob_b[r % 2][:, :], full, ACT.Copy).then_inc(out_act, 1)
            else:
                raise ValueError(name)

        def squares(event, src, ready, junk=junk):
            for tb in range(TB):
                ready(tb)
                ins = fn(junk[:, :], src[:, tb, :], ACT.Square, accum_out=stat[:, event, tb:tb + 1])
                link(ins) if tb == 0 else ins.then_inc(sq_done, 1)

        def norm(n, used):
            if n == 0:
                squares(norm_event[n], h, lambda tb: act.wait_ge(in_x[tb], 16))
            elif n == 1:
                act.wait_ge(in_mem, 16)
                squares(norm_event[n], mem_tok, lambda tb: None)
            else:
                squares(norm_event[n], h, lambda tb: act.wait_ge(h_ready, TB * (n - 2) + tb + 1))
            if used:
                act.wait_ge(unit_done, used)
            src, dst = x_f2 if n == 3 else x_f, o_hi if n == 1 else x_hi
            for g in range(4):
                act.wait_ge(f_ready, 4 * n + g + 1)
                fn(dst[:, 2 * g:2 * g + 2, :].rearrange("p a b -> p (a b)"),
                   src[:, 2 * g:2 * g + 2, :].rearrange("p a b -> p (a b)"), ACT.Copy).then_inc(xh_ready, 1)

        def column_squares(src, j, count, junk=junk):
            for tb in range(TB):
                ins = fn(junk[:, 0:UC], src(tb), ACT.Square, accum_out=sq_part[:, tb, j:j + 1])
                link(ins) if tb == 0 else ins.then_inc(sq_ready, 1)
            act.wait_ge(sq_ready, count)

        def scores(k):
                s = k % 2
                if kind(k) == "sb":
                    act.wait_ge(z_done, k + 1)
                    if k >= 2:
                        act.wait_ge(mid_ready, k - 1)
                    link(fn(score_b[s][:, 0:CAUSAL], ps[:, 4 + s, 0:CAUSAL], ACT.Abs))
                    link(fn(score_b[s][:, 0:CAUSAL], score_b[s][:, 0:CAUSAL], ACT.Exp, scale=-1.0))
                    fn(score_b[s][:, 0:CAUSAL], score_b[s][:, 0:CAUSAL], ACT.Ln, bias=1.0).then_inc(exp_done, 1)
                else:
                    act.wait_ge(prep_done, k - 7)
                    scale = 1.0 if kind(k) == "x" else 0.125
                    c = (0, T, 2 * T) if kind(k) == "x" else (0, P, CAUSAL)
                    src = ps[:, 4 + s, :] if kind(k) == "x" else score_b[s]
                    for tb in range(TB):
                        ins = fn(prob_b[s][:, c[tb]:c[tb + 1]], src[:, c[tb]:c[tb + 1]], ACT.Exp,
                                 bias=softmax[:, 8 * s + tb:8 * s + tb + 1], scale=scale,
                                 accum_out=softmax[:, 8 * s + 2 + tb:8 * s + 3 + tb])
                        link(ins) if tb == 0 else ins.then_inc(exp_done, 1)

        def middle(k):
            if kind(k) == "sb":
                act.wait_ge(expo_ready, k + 1)
                fn(right_b[k % 2][:, 0:CAUSAL], expo_b[k % 2][:, 0:CAUSAL], ACT.Exp).then_inc(a_done, 1)

        split(0)
        split(1)
        used = 0
        for step, *arg in plan:
            if step == "vectors":
                pass
            elif step == "norm":
                norm(arg[0], used if arg[0] != 1 else 0)
            elif step == "post":
                if arg[0] == 1:
                    act.wait_ge(unit_done, G0 + 3 * NF)
                    for tb in range(TB):
                        if tb:
                            act.wait_ge(y_half, 2)
                        for half in range(2):
                            fn(junk[:, 0:512], ps[:, 4 + 2 * tb + half, :], ACT.Square,
                               accum_out=sq_part[:, tb, half:half + 1]).then_inc(sq_half, 1)
                            act.wait_ge(sq_half, 2 * tb + half + 1)
            elif step == "unit":
                u = arg[0]
                used = u + 1
                split(u + 2)
                if units[u]["name"] == "out":
                    j = units[u]["j"]
                    act.wait_ge(unit_done, u + 1)
                    column_squares(lambda tb: ps[:, bank_of[u], UC * tb:UC * tb + UC], j, j + 1)
                elif units[u]["name"] not in BY_VECTOR:
                    evacuate(u)
            elif step == "route":
                r = arg[0]
                act.wait_ge(hg_ready, r + 1)
                column_squares(lambda tb: h[:, tb, UC * r:UC * r + UC], r, 4 + r + 1,
                               y_quad)
                act.wait_ge(route_T, r + 1)
                fn(n3T[:, 2 * r:2 * r + 2, :].rearrange("p a b -> p (a b)"), ps[:, 2 + r, :], ACT.Copy)\
                    .then_inc(route_out, 1)
            elif step == "sigmoid":
                last_gate = first["merge"] - 1 if arg[0] == 0 else second_merge - 1
                wait_out(act, last_gate)
                g = gates if arg[0] == 0 else gates2
                rest = (1, 2) if arg[0] == 0 else (1,)
                order = [(0, j) for j in range(4)] + [(b, j) for j in range(4) for b in rest]
                for b, j in order:
                    part = g[:, 8 * b + 2 * j:8 * b + 2 * j + 2, :].rearrange("p a b -> p (a b)")
                    fn(part, part, ACT.Sigmoid).then_inc(sig_ready, 1)
            elif step == "pool_window":
                act.wait_ge(pool_w, 1)
                for b in range(2):
                    ins = fn(mixed[:, 2 * b:2 * b + 2, :].rearrange("p a b -> p (a b)"), ps[:, 6 + b, :], ACT.Copy)
                    link(ins) if b == 0 else ins.then_inc(pool_mixed, 1)
            elif step == "heads":
                for k in arg[1]:
                    middle(k)
                for k in arg[0]:
                    scores(k)
            elif step == "index":
                for i in (arg[0], arg[0] + 1):
                    act.wait_ge(ix_z, i + 1)
                    if i >= 2:
                        act.wait_ge(ix_acc, i - 1)
                    fn(score_b[i % 2][:, 0:CAUSAL], ps[:, 4 + i % 2, 0:CAUSAL], ACT.Relu).then_inc(ix_relu, 1)
            elif step == "ffn":
                def gate(i, used):
                    act.wait_ge(unit_done, used)
                    fn(silu_g[:, :], ps[:, 0, :], ACT.Silu).then_inc(out_act, 1)

                def triple(i):
                    for j in range(3):
                        split_ffn(i, j)
                        if j == 0:
                            act.wait_ge(out_dve, i + outs(G0 - 1, True))
                            gate(i, i * 3 + (S2 - 3 + 1))

                for j in range(2):
                    split(G0 + j + 2)
                    if j == 0:
                        gate(0, G0 + 1)
                ffn_loop(act, triple)
                split(S2 + 3 * (NF - 1) + 2)
                used = G0 + 3 * NF

        act.wait_ge(route_in, 1)
        fn(exp_out[:, :, :].rearrange("p a b -> p (a b)"), exp_in[:, :, :].rearrange("p a b -> p (a b)"), ACT.Exp)\
            .then_inc(route_exp, 1)

        def quad_body(q):
            e0 = act.snap(q * QUAD) if not isinstance(q, int) else 0
            act.wait_ge(xg_done, q + 1)
            fn(xg[:, 0:4, :].rearrange("p a b -> p (a b)"), ps[:, 2, :], ACT.Copy).then_inc(xg_part, 1)
            act.wait_ge(xg_part, q + 1)
            fn(xg[:, 4:8, :].rearrange("p a b -> p (a b)"), ps[:, 3, :], ACT.Copy).then_inc(xg_ready, 1)
            act.wait_ge(gt_done, q + 1)
            fn(gate_T[:, :], ps[:, 0, 0:T], ACT.Copy).then_inc(gt_ready, 1)
            for e in range(QUAD):
                act.wait_ge(e_up, e0 + (e + 1))
                fn(silu_e[:, :], ps[:, 4 + e % 2, 0:P], ACT.Silu).then_inc(e_silu, 1)
                act.wait_ge(e_y, e0 + (e + 1))
                for g in (0, 1):
                    fn(y_quad[SLOTS * e:SLOTS * e + SLOTS, UC * g:UC * g + UC],
                       ps[SLOTS * g:SLOTS * g + SLOTS, 7, 0:UC], ACT.Copy).then_inc(e_yA, 1)

        quad_body(0)
        act.wait_ge(passes_ready, 1)
        n_pass = act.value_load(passes_i[0:1, 0:1], min_val=1, max_val=T // SLOTS)
        with act.Fori(1, n_pass * (EXPERTS // QUAD)) as q:
            quad_body(q)
        act.wait_ge(comb_added, n_pass * (EXPERTS // QUAD))
        squares(last_event, h, lambda tb: None, y_quad)

    @block.vector
    def _(dve):
        chain = [0]
        v = nc.vector

        def link(ins):
            chain[0] += 1
            ins.then_inc(dve_chain, 1)
            dve.wait_ge(dve_chain, chain[0])

        def split(u):
            if u >= U:
                return
            n = units[u]["kc"] * units[u]["cols"]
            dve.wait_ge(hi_ready, u + 1)
            v.tensor_tensor(w_lo[:, u % 3, 0:n], arena[:, u % 3, 0:n], w_hi[:, u % 3, 0:n].bitcast(F32),
                            ALU.subtract).then_inc(lo_ready, 1)

        def split_ffn(i, j):
            if isinstance(i, int):
                return split(S2 + 3 * (i - 1) + j + 2)
            s = (S2 + j + 2) % 3
            dve.wait_ge(hi_ready, i * 3 + (S2 - 3 + j + 3))
            v.tensor_tensor(w_lo[:, s, :], arena[:, s, :], w_hi[:, s, :].bitcast(F32), ALU.subtract)\
                .then_inc(lo_ready, 1)

        def flat(x):
            return x.rearrange("p a b -> p (a b)")

        def mean_square(event):
            v.tensor_scalar(stat[:, event, 2:4], stat[:, event, 0:2], 1.0 / D, EPS, ALU.mult, ALU.add)\
                .then_inc(mean_done, 1)
            dve.wait_ge(root_done, event + 1)

        def gather_squares(event, n):
            link(v.tensor_reduce(stat[:, event, 0:2], sq_part[:, :, 0:n], AX.X, ALU.add))
            mean_square(event)

        def norm(n, used):
            dve.wait_ge(sq_done, n + 1)
            mean_square(norm_event[n])
            dve.wait_ge(row_done, n + 1)
            link(v.tensor_copy(rstd_row[:, :], ps[:, 6, 0:T]))
            if used:
                dve.wait_ge(unit_done, used)
            x = x_f2 if n == 3 else x_f
            hi, lo = (o_hi, o_lo) if n == 1 else (x_hi, x_lo)
            g0 = (8, 0, 20, 28)[n]

            def low(g):
                dve.wait_ge(xh_ready, 4 * n + g + 1)
                v.tensor_tensor(flat(lo[:, 2 * g:2 * g + 2, :]), flat(x[:, 2 * g:2 * g + 2, :]),
                                flat(hi[:, 2 * g:2 * g + 2, :]).bitcast(F32), ALU.subtract).then_inc(x_ready, 1)

            for g in range(4):
                dve.wait_ge(norm_T, 4 * n + g + 1)
                for c in (2 * g, 2 * g + 1):
                    ins = v.scalar_tensor_tensor(x[:, c, :], ps[:, 2 + g, T * (c % 2):T * (c % 2) + T],
                                                 vec[:, g0 + c:g0 + c + 1], rstd_row[:, :], ALU.mult, ALU.mult)
                    link(ins) if c % 2 == 0 else ins.then_inc(f_ready, 1)
                if g:
                    low(g - 1)
            low(3)

        def post(n):
            if n == 0:
                dve.wait_ge(out_dve, outs(out0 + 3, True))
                gather_squares(post_event[0], 4)
            else:
                dve.wait_ge(unit_done, G0 + 3 * NF)
                dve.wait_ge(in_gain[1], 16)
                for i, tb in enumerate((1, 0)):
                    if i:
                        dve.wait_ge(sq_half, 2)
                    for half in range(2):
                        v.tensor_tensor(y_tok[:, tb, 512 * half:512 * half + 512], ps[:, 4 + 2 * tb + half, :],
                                        gain_rows[1][:, 512 * half:512 * half + 512], ALU.mult).then_inc(y_half, 1)
                dve.wait_ge(y_half, 4)
                dve.wait_ge(sq_half, 4)
                gather_squares(post_event[1], 2)
            for tb in range(TB):
                v.scalar_tensor_tensor(h[:, tb, :], y_tok[:, tb, :], stat[:, post_event[n], 6 + tb:7 + tb],
                                       h[:, tb, :], ALU.mult, ALU.add).then_inc(h_ready, 1)

        columns = ((0, P), (P, CAUSAL))

        def maxima(k):
                kd, z, s = kind(k), ps[:, 4 + k % 2, :], k % 2
                dve.wait_ge(z_done, k + 1)
                if kd != "sb":
                    if kd == "x":
                        link(v.tensor_reduce(softmax[:, 8 * s + 4:8 * s + 6], z.rearrange("p (a b) -> p a b", a=TB),
                                             AX.X, ALU.max))
                    else:
                        hide = const("hide") if kd == "moba" else score[:, :]
                        for tb, (c0, c1) in enumerate(columns):
                            link(v.tensor_tensor_reduce(out=score_b[s][:, c0:c1], in0=z[:, c0:c1],
                                                        in1=hide[:, c0:c1], scale=1.0, scalar=-3e38, op0=ALU.add,
                                                        op1=ALU.max,
                                                        accum_out=softmax[:, 8 * s + 4 + tb:8 * s + 5 + tb]))
                    v.tensor_scalar(softmax[:, 8 * s:8 * s + 2], softmax[:, 8 * s + 4:8 * s + 6],
                                    -1.0 if kd == "x" else -0.125, None, ALU.mult).then_inc(prep_done, 1)

        def take_middle(k):
                m = ps[:, (6, 2)[k % 2], :]
                dve.wait_ge(mid_done, k + 1)
                if kind(k) == "sb":
                    v.tensor_tensor(expo_b[k % 2][:, 0:CAUSAL], expo_b[k % 2][:, 0:CAUSAL], m[:, 0:CAUSAL],
                                    ALU.subtract).then_inc(expo_ready, 1)
                else:
                    n = 2 * T if kind(k) == "x" else CAUSAL
                    v.tensor_copy(right_b[k % 2][:, 0:n], m[:, 0:n]).then_inc(right_ready, 1)

        def take_pair(k):
            if k % 2:
                o, c = ps[:, (7, 3)[k // 2 % 2], 0:T], pair_slot(k)
                dve.wait_ge(o_done, k + 1)
                link(v.tensor_copy(o_hi[:, c, :], o))
                v.tensor_tensor(o_lo[:, c, :], o, o_hi[:, c, :].bitcast(F32), ALU.subtract).then_inc(pair_out, 1)

        def weights(k):
                kd, z, s = kind(k), ps[:, 4 + k % 2, :], k % 2
                dve.wait_ge(exp_done, k + 1)
                if kd == "sb":
                    soft = prob_b[s][:, 0:CAUSAL]
                    link(v.scalar_tensor_tensor(soft, z[:, 0:CAUSAL], 0.0, score_b[s][:, 0:CAUSAL], ALU.max, ALU.add))
                    link(v.tensor_tensor(expo_b[s][:, 0:CAUSAL], z[:, 0:CAUSAL], soft, ALU.subtract))
                    v.tensor_tensor(soft, soft, const("keep"), ALU.mult).then_inc(mid_ready, 1)
                else:
                    cut = (0, T, 2 * T) if kd == "x" else (0, P, CAUSAL)
                    link(v.reciprocal(softmax[:, 8 * s + 6:8 * s + 8], softmax[:, 8 * s + 2:8 * s + 4]))
                    for tb in range(TB):
                        part = prob_b[s][:, cut[tb]:cut[tb + 1]]
                        ins = v.tensor_scalar(part, part, softmax[:, 8 * s + 6 + tb:8 * s + 7 + tb], None, ALU.mult)
                        link(ins) if tb == 0 else ins.then_inc(mid_ready, 1)

        def keep_past(k):
            if kind(k) == "sb":
                dve.wait_ge(a_done, k + 1)
                right = right_b[k % 2][:, 0:CAUSAL]
                v.tensor_tensor(right, right, const("keep"), ALU.mult).then_inc(right_ready, 1)

        def merge(u):
            x = units[u]
            g, n = (gates, 8) if u < G0 else (gates2, 8)
            j, b = x["j"], x["b"]
            dve.wait_ge(sig_ready, (j + 1 if b == 0 else 4 + 2 * j + b) if u < G0 else 12 + 4 * b + j + 1)
            part = flat(g[:, n * b + 2 * j:n * b + 2 * j + 2, :])
            total = flat(g[:, 2 * j:2 * j + 2, :])
            v.tensor_tensor(part, part, ps[:, bank_of[u], :], ALU.mult).then_inc(out_dve, 1)
            dve.wait_ge(out_dve, outs(u, True))
            if b:
                link(v.tensor_tensor(total, total, part, ALU.add))
            if x["last"]:
                hi, lo = flat(x_hi[:, 2 * j:2 * j + 2, :]), flat(x_lo[:, 2 * j:2 * j + 2, :])
                link(v.tensor_copy(hi, total))
                v.tensor_tensor(lo, total, hi.bitcast(F32), ALU.subtract).then_inc(merged_ready, 1)

        roped = {"qi": qi, "kb": kb, "qb": qb, "ka": ka, "qa": qa}

        def rope(r, u):
            wait_out(dve, u)
            s, n = r % 2, T if r == 0 else 2 * T
            name = units[u]["name"]
            dst = ki[:, :] if r == 0 else flat(roped[name][:, 2 * units[u]["j"]:2 * units[u]["j"] + 2, :])
            link(v.tensor_tensor(expo_b[s][:, 0:n], prob_b[s][:, 0:n], const("cos")[:, 0:n], ALU.mult))
            dve.wait_ge(rot_done, r + 1)
            link(v.tensor_tensor(right_b[s][:, 0:n], ps[:, 7, 0:n], const("sin")[:, 0:n], ALU.mult))
            v.tensor_tensor(dst, expo_b[s][:, 0:n], right_b[s][:, 0:n], ALU.add).then_inc(rope_done, 1)

        def ffn():
            def up(i, done):
                dve.wait_ge(unit_done, done)
                dve.wait_ge(out_act, i + (outs(G0 - 1, False) + 1))
                v.tensor_tensor(act_f[:, :], silu_g[:, :], ps[:, 1, :], ALU.mult).then_inc(out_dve, 1)
                dve.wait_ge(out_dve, i + (outs(G0 - 1, True) + 1))

            def parts(i):
                hi, lo = flat(o_hi[:, 0:2, :]), flat(o_lo[:, 0:2, :])
                v.tensor_copy(hi, act_f[:, :]).then_inc(act_hi, 1)
                dve.wait_ge(act_hi, i + 1)
                v.tensor_tensor(lo, act_f[:, :], hi.bitcast(F32), ALU.subtract).then_inc(act_ready, 1)
                dve.wait_ge(act_ready, i + 1)

            def triple(i):
                for j in range(3):
                    split_ffn(i, j)
                    if j == 1:
                        up(i, i * 3 + (S2 - 3 + 2))
                    elif j == 2:
                        dve.wait_ge(unit_done, i * 3 + (S2 - 3 + 3))
                        parts(i)

            split(G0 + 2)
            split(G0 + 3)
            up(0, G0 + 2)
            parts(0)
            ffn_loop(dve, triple)
            split(S2 + 3 * (NF - 1) + 2)

        v.memset(ones[:, :], 1.0).then_inc(dve_chain, 1)
        chain[0] += 1
        split(0)
        split(1)
        used = 0
        for step, *arg in plan:
            if step == "vectors":
                dve.wait_ge(vec_T, 1)
                link(v.tensor_copy(vec[:, :], ps[:, 7, 0:36]))
            elif step == "norm":
                norm(arg[0], used if arg[0] != 1 else 0)
            elif step == "post":
                post(arg[0])
            elif step == "unit":
                u = arg[0]
                split(u + 2)
                used = u + 1
                if units[u]["name"] == "merge":
                    dve.wait_ge(unit_done, u + 1)
                    merge(u)
                elif units[u]["name"] == "out":
                    j = units[u]["j"]
                    if j == 0:
                        dve.wait_ge(in_gain[0], 16)
                    dve.wait_ge(sq_ready, j + 1)
                    gain = gain_rows[0][:, UC * j:UC * j + UC].unsqueeze(1).to_broadcast([P, TB, UC])
                    v.tensor_tensor(y_tok[:, :, UC * j:UC * j + UC],
                                    ps[:, bank_of[u], :].rearrange("p (a b) -> p a b", a=TB), gain, ALU.mult)\
                        .then_inc(out_dve, 1)
                elif units[u]["name"] == "out2":
                    j = units[u]["j"]
                    dve.wait_ge(unit_done, u + 1)
                    part = h[:, :, UC * j:UC * j + UC]
                    v.tensor_tensor(part, part, ps[:, bank_of[u], :].rearrange("p (a b) -> p a b", a=TB), ALU.add)\
                        .then_inc(out_dve, 1)
                    dve.wait_ge(out_dve, outs(u, True))
                    if j == 0:
                        dve.wait_ge(in_gain[0], 32)
                    gain = gain_rows[0][:, UC * j:UC * j + UC].unsqueeze(1).to_broadcast([P, TB, UC])
                    v.tensor_tensor(n3[:, :, UC * j:UC * j + UC], part, gain, ALU.mult).then_inc(hg_ready, 1)
            elif step == "pool_mix":
                dve.wait_ge(pool_p, 1)
                for g in range(4):
                    src = ps[:, 6 + g // 2, T * (g % 2):T * (g % 2) + T]
                    gain = vec[:, 16 + g:17 + g]
                    link(v.tensor_scalar(o_hi[:, g, :], src, gain, None, ALU.mult))
                    ins = v.scalar_tensor_tensor(o_lo[:, g, :], src, gain, o_hi[:, g, :].bitcast(F32), ALU.mult,
                                                 ALU.subtract)
                    link(ins) if g < 3 else ins.then_inc(pool_out, 1)
            elif step == "heads":
                if any(kind(k) == "sb" for k in arg[0] + arg[1]) or max(sum(arg, [])) < 12:
                    for k in arg[0]:
                        if kind(k) != "sb":
                            maxima(k)
                    for part, ks in ((take_middle, arg[1]), (take_pair, arg[2]), (keep_past, arg[1]),
                                     (weights, arg[0])):
                        for k in ks:
                            part(k)
                else:
                    for part, ks in ((take_pair, arg[2]), (take_middle, arg[1]), (maxima, arg[0]),
                                     (weights, arg[0])):
                        for k in ks:
                            part(k)
            elif step == "ffn":
                ffn()
                used = G0 + 3 * NF
            elif step == "rope":
                rope(*arg)
            elif step == "index":
                for i in (arg[0], arg[0] + 1):
                    dve.wait_ge(ix_relu, i + 1)
                    for tb, (c0, c1) in enumerate(columns):
                        w, src = index_w[:, tb, i:i + 1], score_b[i % 2][:, c0:c1]
                        if i == 0:
                            ins = v.tensor_scalar(score[:, c0:c1], src, w, None, ALU.mult)
                        else:
                            ins = v.scalar_tensor_tensor(score[:, c0:c1], src, w, score[:, c0:c1], ALU.mult, ALU.add)
                        link(ins) if tb == 0 else ins.then_inc(ix_acc, 1)
                    dve.wait_ge(ix_acc, i + 1)
                if arg[0] == 6:
                    link(v.tensor_tensor(work[:, :], score[:, :], const("hide"), ALU.add))
            elif step == "topk":
                for tb, (c0, c1) in enumerate(columns):
                    link(v.max(best8[:, tb, :], work[:, c0:c1]))
                    link(v.match_replace(work[:, c0:c1], best8[:, tb, :], work[:, c0:c1], TAKEN))
            elif step == "select":
                link(v.tensor_scalar(score[:, :], work[:, :], TAKEN / 2, NEG, ALU.is_gt, ALU.mult))
                link(v.tensor_tensor(score[:, :], score[:, :], const("hide"), ALU.add))

        dve.wait_ge(hg_ready, 4)
        dve.wait_ge(sq_ready, 8)
        gather_squares(moe_event, 4)
        dve.wait_ge(logit_done, 1)
        dve.wait_ge(in_route, 64)
        for tb in range(TB):
            link(v.scalar_tensor_tensor(logits[:, tb, :], ps[:, 6 + tb, 0:36], stat[:, moe_event, 6 + tb:7 + tb],
                                        b_route[:, :], ALU.mult, ALU.add))

        def wide(x, n):
            return x.unsqueeze(2).to_broadcast([P, TB, n])

        def per_token(x, n):
            return x.unsqueeze(1).to_broadcast([P, TB, n])

        def tt(dst, a_, b_, op):
            link(v.tensor_tensor(dst, a_, b_, op))

        def biggest(dst, src, n):
            link(v.tensor_reduce(dst, src, AX.X, ALU.max))

        def first_of(dst, src, top, rev, n, scratch, place):
            tt(dst, src, wide(top, n), ALU.is_equal)
            tt(dst, dst, per_token(rev, n), ALU.mult)
            biggest(place, dst, n)
            tt(dst, dst, wide(place, n), ALU.is_equal)

        gmax, place, gsum, best, second, total, share = (r_s[:, i, :] for i in range(7))
        lg, le = logits[:, :, 0:GROUPS], logits[:, :, GROUPS:36]
        biggest(gmax, lg, GROUPS)
        tt(exp_in[:, :, 0:GROUPS], lg, wide(gmax, GROUPS), ALU.subtract)
        first_of(pick_g[:, :, :], lg, gmax, const("revg"), GROUPS, None, place)
        for tb in range(TB):
            own = pick_g[:, tb, :].unsqueeze(2).to_broadcast([P, GROUPS, PER_GROUP])
            dst = masked_e[:, tb, :].rearrange("p (g e) -> p g e", g=GROUPS)
            tt(dst, le[:, tb, :].rearrange("p (g e) -> p g e", g=GROUPS), own, ALU.mult)
            hidden = pick[:, tb, :].rearrange("p (g e) -> p g e", g=GROUPS)
            link(v.tensor_scalar(hidden, own, 1.0, -NEG, ALU.subtract, ALU.mult))
            tt(dst, dst, hidden, ALU.add)
        biggest(best, masked_e[:, :, :], EXPERTS)
        v.tensor_tensor(exp_in[:, :, GROUPS:36], masked_e[:, :, :], wide(best, EXPERTS), ALU.subtract)\
            .then_inc(route_in, 1)
        first_of(chosen[:, :, :], masked_e[:, :, :], best, const("rev"), EXPERTS, None, place)
        link(v.tensor_scalar(pick[:, :, :], chosen[:, :, :], 2 * NEG, None, ALU.mult))
        tt(masked_e[:, :, :], masked_e[:, :, :], pick[:, :, :], ALU.add)
        biggest(second, masked_e[:, :, :], EXPERTS)
        first_of(pick_one[:, :, :], masked_e[:, :, :], second, const("rev"), EXPERTS, None, place)
        v.tensor_tensor(chosen[:, :, :], chosen[:, :, :], pick_one[:, :, :], ALU.add).then_inc(route_sel, 1)
        dve.wait_ge(route_sel, 1)
        for tb in range(TB):
            link(v.tensor_scalar(n3[:, tb, :], n3[:, tb, :], stat[:, moe_event, 6 + tb:7 + tb], None, ALU.mult))
        dve.wait_ge(route_exp, 1)
        link(v.tensor_reduce(gsum, exp_out[:, :, 0:GROUPS], AX.X, ALU.add))
        link(v.reciprocal(gsum, gsum))
        link(v.tensor_reduce(total, exp_out[:, :, GROUPS:36], AX.X, ALU.add))
        link(v.reciprocal(total, total))
        tt(gate_e[:, :, :], exp_out[:, :, GROUPS:36], wide(total, EXPERTS), ALU.mult)
        tt(gate_e[:, :, :], gate_e[:, :, :], chosen[:, :, :], ALU.mult)
        link(v.tensor_reduce(share, gate_e[:, :, :], AX.X, ALU.add))
        link(v.reciprocal(share, share))
        tt(share, share, gsum, ALU.mult)
        tt(gate_e[:, :, :], gate_e[:, :, :], wide(share, EXPERTS), ALU.mult)
        dve.wait_ge(rank_done, 1)
        link(v.tensor_copy(slot_no[:, :], const("slot")))
        link(v.scalar_tensor_tensor(flat(rank[:, :, :]), ps[:, 1, 0:2 * EXPERTS], 1.0, flat(chosen[:, :, :]), ALU.add,
                                    ALU.mult))
        link(v.tensor_scalar(rank[:, :, :], rank[:, :, :], -1.0, None, ALU.add))
        link(v.tensor_reduce(r_s[:, 8, 0:1], ps[:, 1, 64:64 + EXPERTS], AX.X, ALU.max))
        link(v.tensor_scalar(exp_in[:, 0, 0:8], const("steps"), r_s[:, 8, 0:1], None, ALU.is_lt))
        link(v.tensor_reduce(r_s[:, 8, 1:2], exp_in[:, 0, 0:8], AX.X, ALU.add))
        v.tensor_copy(passes_i[:, :], r_s[:, 8, 1:2]).then_inc(passes_ready, 1)
        dve.wait_ge(passes_ready, 1)

        def quad_body(q, i, again=None):
            looped = not isinstance(q, int)
            e0 = dve.snap(q * QUAD) if looped else 0
            at_e = dve.snap(i * QUAD) if looped else i * QUAD
            slots = slot_no[:, :].unsqueeze(1).to_broadcast([P, QUAD, SLOTS])
            if again is not None:
                dve.wait_ge(slot_moved, again)
            for tb in range(TB):
                mine = rank[:, tb, bass.ds(at_e, QUAD)].unsqueeze(2).to_broadcast([P, QUAD, SLOTS])
                hot = one_hot[:, tb, :].rearrange("p (e s) -> p e s", e=QUAD)
                v.tensor_tensor(hot, slots, mine, ALU.is_equal).then_inc(hot_part, 1)
                dve.wait_ge(hot_part, q * 2 + (tb + 1))
            for tb in range(TB):
                hot = one_hot[:, tb, :].rearrange("p (e s) -> p e s", e=QUAD)
                gate = gate_e[:, tb, bass.ds(at_e, QUAD)].unsqueeze(2).to_broadcast([P, QUAD, SLOTS])
                ins = v.tensor_tensor(gated_hot[:, tb, :].rearrange("p (e s) -> p e s", e=QUAD), hot, gate, ALU.mult)
            ins.then_inc(hot_ready, 1)
            for e in range(QUAD):
                done = dve.snap(e0 + (e + 1)) if looped else e + 1
                dve.wait_ge(e_silu, done)
                v.tensor_tensor(hid[:, :], silu_e[:, :], ps[:, 4 + e % 2, P:2 * P], ALU.mult).then_inc(e_hid, 1)
                dve.wait_ge(e_T, done)
                v.tensor_copy(hid_T[:, :], ps[:, 6, 0:P]).then_inc(e_hidT, 1)
                dve.wait_ge(e_y, done)
                for g in (2, 3):
                    v.tensor_copy(y_quad[SLOTS * e:SLOTS * e + SLOTS, UC * g:UC * g + UC],
                                  ps[SLOTS * g:SLOTS * g + SLOTS, 7, 0:UC]).then_inc(e_yD, 1)
            dve.wait_ge(comb_done, q + 1)
            for tb in range(TB):
                for half in range(2):
                    part = h[:, tb, 512 * half:512 * half + 512]
                    ins = v.tensor_tensor(part, part, ps[:, 2 * tb + half, :], ALU.add)
            ins.then_inc(comb_added, 1)
            dve.wait_ge(comb_added, q + 1)

        quad_body(0, 0)
        with dve.Fori(1, EXPERTS // QUAD) as i:
            quad_body(i, i)
        n_pass = dve.value_load(passes_i[0:1, 0:1], min_val=1, max_val=T // SLOTS)
        with dve.If(n_pass > 1):
            with dve.Fori(1, n_pass) as again:
                v.tensor_scalar(slot_no[:, :], slot_no[:, :], float(SLOTS), None, ALU.add).then_inc(slot_moved, 1)
                with dve.Fori(0, EXPERTS // QUAD) as i:
                    quad_body(dve.snap(again * (EXPERTS // QUAD) + i), i, again)
            dve.nop()
        dve.wait_ge(sq_done, 5)
        mean_square(last_event)
        dve.wait_ge(in_gain[1], 32)
        for tb in range(TB):
            v.scalar_tensor_tensor(n3[:, tb, :], h[:, tb, :], stat[:, last_event, 6 + tb:7 + tb], gain_rows[1][:, :],
                                   ALU.mult, ALU.mult).then_inc(fin_ready, 1)

    block_cm.__exit__(None, None, None)


_INS = ["x", "mem", "norm_mix_pre", "w_in", "w_pool_mix", "pool_scale", "w_pool_o", "w_sb_o", "norm_mem", "w_mem_kv",
        "w_x_o", "w_out", "norm_mix_post", "norm_ffn_pre", "w_ffn_in", "w_ffn_out", "norm_ffn_post", "g_mix_2",
        "w_in_2", "w_proj_a_2", "w_proj_b_2", "w_out_2", "g_ffn_2", "w_group_2", "b_group_2", "w_expert_2",
        "b_expert_2", "w1_2", "w3_2", "w2_2", "g_final_2"]


def kernel(**inputs):
    import concourse.bacc as bacc
    from concourse.bass_utils import run_bass_kernel_spmd

    nc = bacc.Bacc("TRN2", target_bir_lowering=False, num_devices=1)
    arrays, aps = {}, {}
    for name in _INS:
        x = np.ascontiguousarray(inputs[name])
        arrays[f"in_{name}"] = x
        aps[name] = nc.dram_tensor(f"in_{name}", x.shape, mybir.dt.from_np(x.dtype), kind="ExternalInput").ap()
    for name, x in (("table", make_table()), ("windows", make_windows())):
        arrays[f"in_{name}"] = x
        aps[name] = nc.dram_tensor(f"in_{name}", x.shape, F32, kind="ExternalInput").ap()
    out = nc.dram_tensor("out", (1, T, D), F32, kind="ExternalOutput").ap()
    layers_kernel(nc, aps, aps["table"], aps["windows"], out)
    r = run_bass_kernel_spmd(nc, [arrays], core_ids=[0])
    return r.results[0]["out"]
```

```python
import numpy as np
import concourse.bass as bass
from concourse import mybir

F32 = mybir.dt.float32
F32R = mybir.dt.float32r
I32 = mybir.dt.int32
ACT = mybir.ActivationFunctionType
ALU = mybir.AluOpType
AX = mybir.AxisListType

P = 128
T = 256
TB = T // P
D = 1024
KC = D // P
DH = 64
HEADS = 8
X_HEADS = 4
FF = 2816
UNIT = 2048
UC = 256
EPS = 1e-6
NEG = -1e30
TAKEN = -3e38
TOPK = T // 4
GROUPS, PER_GROUP = 4, 8
EXPERTS = GROUPS * PER_GROUP
EFF = 512
SLOTS = 32
QUAD = 4
WINDOWS = (2, 4, 8, 16)
CAUSAL = P + T

TABLE = {}
_at = 0
for _name, _n in (("ident", P), ("later", P), ("before", P), ("rotate", P), ("keep", CAUSAL), ("hide", CAUSAL),
                  ("cos", 2 * T), ("sin", 2 * T), ("slot", SLOTS), ("rev", EXPERTS), ("revg", GROUPS), ("steps", 8)):
    TABLE[_name] = (_at, _at + _n)
    _at += _n
TABLE_W = _at


def make_table():
    t = np.zeros((P, TABLE_W), np.float32)

    def put(name, value):
        a, b = TABLE[name]
        t[:, a:b] = value

    i, j = np.arange(P)[:, None], np.arange(P)[None, :]
    put("ident", i == j)
    put("later", i > j)
    put("before", i < j)
    rot = np.zeros((P, P), np.float32)
    for p in range(P):
        if p % DH < DH // 2:
            rot[p + DH // 2, p] = -1.0
        else:
            rot[p - DH // 2, p] = 1.0
    put("rotate", rot)
    put("keep", np.concatenate([i < j, np.ones((P, P)), i < j], 1))
    put("hide", np.where(np.concatenate([j <= i, np.ones((P, P), bool), j <= i], 1), 0.0, NEG))
    inv = np.power(np.float32(10000.0), -np.arange(0, DH, 2, dtype=np.float32) / np.float32(DH))
    ang = (np.arange(T, dtype=np.float32)[None, :] * inv[np.arange(P) % (DH // 2)][:, None]).astype(np.float32)
    put("cos", np.tile(np.cos(ang), (1, 2)))
    put("sin", np.tile(np.sin(ang), (1, 2)))
    put("slot", np.arange(SLOTS)[None, :])
    put("rev", EXPERTS - np.arange(EXPERTS)[None, :])
    put("revg", GROUPS - np.arange(GROUPS)[None, :])
    put("steps", SLOTS * np.arange(8)[None, :])
    return t


def make_windows():
    b = np.zeros((P, len(WINDOWS), CAUSAL), np.float32)
    for g, w in enumerate(WINDOWS):
        full = np.zeros((T, T), np.float32)
        for t in range(T):
            lo = max(t + 1 - w, 0)
            full[lo:t + 1, t] = np.float32(1.0) / np.float32(t + 1 - lo)
            full[t, t] -= 1.0
        b[:, g, 0:T] = full[0:P, :]
        b[:, g, T:CAUSAL] = full[P:T, P:T]
    return b


def unit_plan(a):
    units = []

    def add(name, w, c0, kc=KC, cols=UC, k0=0, **more):
        src = w[k0 * P:(k0 + kc) * P, c0:c0 + cols].rearrange("(c p) n -> p c n", p=P)
        units.append(dict(name=name, src=[(0, cols, src)], kc=kc, cols=cols, **more))

    kv, w_in = a["w_mem_kv"][0], a["w_in"][0]
    for name, c0, n, f in (("p", 0, 2, "A"), ("q", 512, 2, "B"), ("k", 1024, 2, "B"), ("v", 1536, 2, "A"),
                           ("xq", 2048, 1, "B")):
        for j in range(n):
            add(name, w_in, c0 + UC * j, form=f, j=j)
    add("mk", kv, 0, form="B")
    add("mv", kv, UC, form="A")
    for j in range(12):
        add("gate", w_in, 2304 + UC * j, form="B", j=j)
    branches = (("w_pool_o", 4, 0), ("w_sb_o", 4, 4), ("w_x_o", 2, 8))
    for b, j in [(0, j) for j in range(4)] + [(b, j) for j in range(4) for b in (1, 2)]:
        w, kc, o0 = branches[b]
        add("merge", a[w][0], UC * j, kc=kc, form="B", j=j, b=b, o0=o0, last=b == 2)
    for j in range(4):
        add("out", a["w_out"][0], UC * j, form="A", j=j)
    up, down = a["w_ffn_in"][0], a["w_ffn_out"][0]

    def add_down(i):
        src = down[i * UC:(i + 1) * UC, :].rearrange("(c p) n -> p c n", p=P)
        units.append(dict(name="down", src=[(0, D, src)], kc=2, cols=D, form="F", i=i))

    for i in range(FF // UC):
        add("g", up, UC * i, form="B", i=i)
        add("u", up, FF + UC * i, form="B", i=i)
        if i:
            add_down(i - 1)
    add_down(FF // UC - 1)
    w2 = a["w_in_2"][0]
    src = w2.rearrange("(c p) n -> p c n", p=P)
    units.append(dict(name="kiwi", kc=KC, cols=136, form="K",
                      src=[(0, DH, src[:, :, 3584:3584 + DH]), (DH, 136, src[:, :, 3584:3656])]))
    for name, c0, f in (("qi", 3072, "B"), ("kb", 2048, "B"), ("qb", 1536, "B"), ("vb", 2560, "A"),
                        ("ka", 512, "B"), ("qa", 0, "B"), ("va", 1024, "A")):
        for j in range(2):
            add(name, w2, c0 + UC * j, form=f, j=j)
    for j in range(8):
        add("gate2", w2, 3656 + UC * j, form="B", j=j)
    for b, (w, o0) in enumerate((("w_proj_a_2", 0), ("w_proj_b_2", 4))):
        for j in range(4):
            add("merge", a[w][0], UC * j, kc=4, form="B", j=j, b=b, o0=o0, last=b == 1)
    for j in range(4):
        add("out2", a["w_out_2"][0], UC * j, form="A", j=j)
    return units


ROPED = ("kiwi", "qi", "kb", "qb", "ka", "qa")
EXP_AND_LN = 6
BY_VECTOR = ("merge", "u", "out", "out2")


def step_plan(units):
    first = {}
    for u, unit in enumerate(units):
        first.setdefault(unit["name"], u)
    plan = []
    ropes = 0

    def unit(u):
        plan.append(("unit", u))

    plan.append(("norm", 0))
    unit(0)
    unit(1)
    plan.append(("norm", 1))
    for u in range(2, 11):
        unit(u)
        if u < 7:
            plan.append(("memory", u - 3))
        if u == 4:
            plan.append(("pool_window",))
    plan.append(("pool_mix",))
    for k in range(12):
        unit(first["gate"] + k)
        plan.append(("heads", [k], [k - 1] if k else [], [k - 3, k - 2] if k > 2 and k % 2 else []))
    plan.append(("sigmoid", 0, [(0, j) for j in range(4)]))
    start = first["merge"]
    for n in range(12):
        unit(start + n)
        if n == 0:
            plan.append(("heads", [], [11], []))
        elif n == 1:
            plan.append(("heads", [], [], [10, 11]))
        if n < 4:
            plan.append(("sigmoid", 0, [(1, n), (2, n)]))
        if n in (6, 8):
            plan.append(("finish", n // 2 - 3))
    plan += [("finish", 2), ("finish", 3)]
    for u in range(first["out"], first["out"] + 4):
        unit(u)
    plan.append(("residual", 0))
    plan.append(("ffn",))
    plan.append(("residual", 1))
    waiting = []
    for u in range(first["kiwi"], first["gate2"]):
        unit(u)
        n = u - first["kiwi"]
        if n == 1:
            plan.append(("row", 3))
        if waiting:
            plan.append(("rope", *waiting.pop()))
        if units[u]["name"] in ROPED:
            waiting.append((ropes, u))
            ropes += 1
        if 4 <= n < 8:
            plan.append(("index", 2 * (n - 4)))
        if n >= 8:
            plan.append(("topk", n - 8))
    assert not waiting
    for k in range(8):
        unit(first["gate2"] + k)
        if k == 0:
            plan.append(("topk", 7))
            plan.append(("select",))
        pairs = ([12 + 2 * x, 13 + 2 * x] if 0 <= x < 8 else [] for x in (k, k - 1, k - 2))
        plan.append(("heads", *pairs))
    plan.append(("sigmoid", 1, [(0, j) for j in range(4)]))
    start = first["gate2"] + 8
    unit(start)
    plan.append(("heads", [], [26, 27], [24, 25]))
    plan.append(("sigmoid", 1, [(1, 0)]))
    unit(start + 1)
    plan.append(("heads", [], [], [26, 27]))
    plan.append(("sigmoid", 1, [(1, 1)]))
    for u in range(start + 2, start + 12):
        unit(u)
        if u < start + 4:
            plan.append(("sigmoid", 1, [(1, u - start)]))
        if start + 5 < u < start + 8:
            plan.append(("finish", u - start - 6))
        if u == start + 7:
            plan += [("finish", 2), ("finish", 3)]
        if u > start + 8:
            plan.append(("route", u - start - 9))
    plan.append(("route", 3))
    return plan


def layers_kernel(nc, a, table, windows, out):
    units = unit_plan(a)
    plan = step_plan(units)
    U = len(units)
    G0 = next(u for u, x in enumerate(units) if x["name"] == "g")
    NF = FF // UC

    base = -(-nc.sbuf_base // 64) * 64
    at = base

    def put(name, shape, dt):
        nonlocal at
        t = nc.alloc_sbuf_tensor_at(name, shape, dt, offset=at)
        at += -(-4 * int(np.prod(shape[1:])) // 32) * 32
        return t

    SLOT_B = 4 * UNIT
    arena_at = at
    arena = put("arena", [P, 12, UNIT], F32)
    ring = arena[:, 1:4, :]
    split_at = at
    w_hi = put("w_hi", [P, 3, UNIT], F32R)
    w_lo = put("w_lo", [P, 3, UNIT], F32R)
    split_end = at
    x_at = at
    x_hi = put("x_hi", [P, KC, T], F32R)
    x_lo = put("x_lo", [P, KC, T], F32R)
    o_at = at
    o_hi = put("o_hi", [P, 10, T], F32R)
    o_lo = put("o_lo", [P, 10, T], F32R)
    o_end = at
    h = put("h", [P, TB, D], F32)
    gain_rows = [put(f"gain_row{i}", [P, D], F32) for i in range(2)]
    tab = put("tab", [P, TABLE_W], F32)
    vec = put("vec", [P, 36], F32)
    ones = put("ones", [P, P], F32)
    stat = put("stat", [P, 8, 8], F32)
    sq_part = put("sq_part", [P, TB, 4], F32)
    minus_half = put("minus_half", [P, TB], F32)
    w_route = put("w_route", [P, KC, 36], F32)
    b_route = put("b_route", [P, 36], F32)
    softmax = put("softmax", [P, 16], F32)
    index_w = put("index_w", [P, TB, 8], F32)
    best8 = put("best8", [P, TB, 8], F32)
    passes_i = put("passes_i", [P, 1], I32)
    assert at <= nc.sbuf_usable_end, (at, nc.sbuf_usable_end)

    def const(name):
        lo, hi = TABLE[name]
        return tab[:, lo:hi]

    ident = const("ident")

    temp_at = arena_at + 4 * SLOT_B
    temp_end = arena_at + 12 * SLOT_B
    where = temp_at

    def temp(name, shape, dt=F32, at_=None):
        nonlocal where
        if at_ is None:
            at_ = where
            where += 4 * int(np.prod(shape[1:]))
            assert where <= temp_end, name
        return nc.alloc_sbuf_tensor_at(name, shape, dt, offset=at_)

    hw = [[temp(f"head_{n}{i}", [P, 2 * T]) for i in range(2)] for n in ("score", "prob", "expo", "right")]
    score_b, prob_b, expo_b, right_b = hw
    heads_end = where
    p_tok = temp("p_tok", [P, TB, 512])
    q1 = temp("q1", [P, 4, T])
    k1 = temp("k1", [P, 4, T])
    v1 = temp("v1", [P, TB, 512])
    xq = temp("xq", [P, 2, T])
    mk = temp("mk", [P, 2, T])
    mv = temp("mv", [P, TB, T])
    gates_at = where
    gates = temp("gates", [P, 24, T])
    win = temp("win", [P, 4, CAUSAL], at_=arena_at)
    pool_w_sb = temp("pool_w_sb", [P, 4, P])
    mixed = temp("mixed", [P, 4, T], at_=gates_at + 16384 + 1024)
    x_f = temp("x_f", [P, KC, T], at_=gates_at)
    rstd_row = temp("rstd_row", [P, T], at_=arena_at + 6144)
    junk = temp("junk", [P, D], at_=temp_at)
    mem_tok = temp("mem_tok", [P, TB, D], at_=gates_at + 8192)
    rows = temp("rows", [36, P], at_=gates_at + 16384 + 5120)
    y_tok = temp("y_tok", [P, TB, D], at_=gates_at + 8192)
    silu_g = temp("silu_g", [P, 2 * T], at_=heads_end)
    act_f = temp("act_f", [P, 2 * T], at_=heads_end + 2048)
    where = heads_end
    kb, qb = (temp(n, [P, 4, T]) for n in ("kb", "qb"))
    vb = temp("vb", [P, TB, 512])
    ki = temp("ki", [P, T])
    score = temp("score", [P, CAUSAL])
    work = temp("work", [P, CAUSAL])
    qi, ka, qa = (temp(n, [P, 4, T]) for n in ("qi", "ka", "qa"))
    va = temp("va", [P, TB, 512])
    assert where == arena_at + 10 * SLOT_B
    gates2 = temp("gates2", [P, 16, T])

    third = [nc.alloc_sbuf_tensor_at(f"third_w{n}", [P, 2, UNIT], F32, offset=o)
             for n, o in ((1, x_at), (3, split_at), (2, split_at + 2 * SLOT_B))]
    n3 = nc.alloc_sbuf_tensor_at("n3", [P, TB, D], F32, offset=o_at)
    n3T = nc.alloc_sbuf_tensor_at("n3T", [P, KC, T], F32, offset=o_at + 8192)
    mo = split_at + 4 * SLOT_B

    def moe(name, shape, dt=F32, where=None):
        nonlocal mo
        size = -(-4 * int(np.prod(shape[1:])) // 32) * 32
        if where is None:
            where = mo
            mo += size
        assert mo <= split_end, name
        return nc.alloc_sbuf_tensor_at(name, shape, dt, offset=where)

    assert o_end - o_at >= 16384 + 4096
    y_quad = moe("y_quad", [P, D], where=o_at + 16384)
    logits = moe("logits", [P, TB, 36])
    exp_in = moe("exp_in", [P, TB, 36])
    exp_out = moe("exp_out", [P, TB, 36])
    masked_e = moe("masked_e", [P, TB, EXPERTS])
    pick = moe("pick", [P, TB, EXPERTS])
    pick_one = moe("pick_one", [P, TB, EXPERTS])
    pick_g = moe("pick_g", [P, TB, GROUPS])
    r_s = moe("r_s", [P, 16, TB])
    chosen = moe("chosen", [P, TB, EXPERTS])
    gate_e = moe("gate_e", [P, TB, EXPERTS])
    rank = moe("rank", [P, TB, EXPERTS])
    slot_no = moe("slot_no", [P, SLOTS])
    one_hot = moe("one_hot", [P, TB, P])
    gated_hot = moe("gated_hot", [P, TB, P])
    gate_T = moe("gate_T", [P, T])
    xg = moe("xg", [P, KC, P])
    silu_e = moe("silu_e", [P, P])
    hid = moe("hid", [P, P])
    hid_T = moe("hid_T", [P, P])

    ps = nc.alloc_psum_tensor("ps", [P, 8, 512], F32)

    bank_of, bank_before = {}, {}
    turn, last_in = 0, {}
    for u, x in enumerate(units):
        if x["form"] == "F":
            continue
        bank = {"g": 0, "u": 1}.get(x["name"], turn % 2)
        turn = bank + 1
        bank_of[u], bank_before[u] = bank, last_in.get(bank)
        last_in[bank] = u
    rope_of = {u: r for r, u in enumerate(u for u, x in enumerate(units) if x["name"] in ROPED)}
    SLOT_OF = ((10, 0, 2), (8, 6, 4))

    def slots(first, blocks):
        return arena[:, first:first + 2, :].rearrange("p s (c n) -> p (s c) n", c=blocks // 2)

    even_w, odd_w = ([slots(s, b) for s, b in zip(at3, (KC, KC, 4))] for at3 in SLOT_OF)
    third_w = [t[:, :, :].rearrange("p s (c n) -> p (s c) n", c=b // 2) for t, b in zip(third, (KC, KC, 4))]

    def sem(name):
        return nc.alloc_semaphore(name)

    landed = [sem(f"unit_landed{i}") for i in range(3)]
    hi_ready, lo_ready = sem("w_hi_ready"), sem("w_lo_ready")
    unit_done = sem("unit_done")
    out_act, out_dve = sem("unit_out_act"), sem("unit_out_dve")
    in_mem, in_rows, in_ident, in_table, in_win, in_mix = (
        sem(f"in_{n}") for n in ("mem", "rows", "ident", "table", "windows", "mix"))
    in_x = [sem("in_x0"), sem("in_x1")]
    in_gain = [sem("in_gain0"), sem("in_gain1")]
    h_ready, sq_ready, y_half, sq_half = sem("h_ready"), sem("sq_part_ready"), sem("ffn_y_half"), sem("ffn_sq_half")
    row_done, f_ready, xh_ready, x_ready = sem("rstd_row_done"), sem("x_f_ready"), sem("x_hi_ready"), sem("x_ready")
    half_ready, sig_ready = sem("minus_half_ready"), sem("gate_sigmoid")
    row_kept, gate2_scaled = sem("row_kept"), sem("gate2_scaled")
    gate_out, up_out = sem("ffn_gate_out"), sem("ffn_up_out")
    sum_ready, sum_hi, n3_ready = sem("merge_sum_ready"), sem("merge_hi"), sem("n3_ready")
    hg_ready, route_T, route_out = sem("hg_ready"), sem("route_T"), sem("route_out")
    vec_T = sem("vec_T")
    sq_done, mean_done, root_done, norm_T = (sem(n) for n in ("sq_done", "mean_done", "rstd_done", "norm_T"))
    pool_w, pool_mixed, pool_p, pool_out = (sem(n) for n in ("pool_w", "pool_mixed", "pool_p", "pool_out"))
    z_done, prep_done, exp_done, mid_ready, mid_done, expo_ready, a_done, right_ready, o_done, pair_out = (
        sem(n) for n in ("z_done", "prep_done", "exp_done", "mid_ready", "mid_done", "expo_ready", "a_done",
                         "right_ready", "o_done", "pair_out"))
    merged_ready = sem("merged_ready")
    act_hi, act_ready = sem("ffn_act_hi"), sem("ffn_act_ready")
    rot_done, rope_done, wi_T = sem("rot_done"), sem("rope_done"), sem("wi_out")
    ix_z, ix_relu, ix_acc = sem("index_z"), sem("index_relu"), sem("index_acc")
    act_chain, dve_chain = sem("act_chain"), sem("dve_chain")
    in_route = sem("in_route")
    logit_done, route_sel, rank_done, passes_ready = (sem(n) for n in ("logit_done", "route_sel", "rank_done",
                                                                       "passes_ready"))
    landed_w = [[sem(f"{parity}_w{n}") for n in (1, 3, 2)] for parity in ("even", "odd")]
    in_third3 = [sem(f"third_w{n}_in") for n in (1, 3, 2)]
    route_in, route_exp = sem("route_in"), sem("route_exp")
    xg_part, hot_part, slot_moved = sem("xg_part"), sem("hot_part"), sem("slot_moved")
    hot_ready, xg_done, xg_ready, gt_done, gt_ready = (sem(n) for n in ("hot_ready", "xg_done", "xg_ready",
                                                                        "gt_done", "gt_ready"))
    e_w1 = sem("e_w1")
    e_up, e_silu, e_hid, e_T, e_hidT, e_y, e_yA, e_yD = (sem(n) for n in (
        "e_up", "e_silu", "e_hid", "e_T", "e_hidT", "e_y", "e_y_act", "e_y_dve"))
    comb_done, comb_added = sem("comb_done"), [sem("comb_added0"), sem("comb_added1")]
    fin_ready, fin_out = sem("final_ready"), sem("final_out")

    def landings(u):
        return 16 * sum(len(units[v]["src"]) for v in range(u % 3, u + 1, 3))

    def outs(u, vector):
        return sum((x["name"] in BY_VECTOR) == vector for x in units[:u + 1] if x["form"] != "F")

    def wait_out(eng, u):
        if units[u]["name"] in BY_VECTOR:
            eng.wait_ge(out_dve, outs(u, True))
        else:
            eng.wait_ge(out_act, outs(u, False))

    def kind(k):
        return "sb" if k < 8 else "x" if k < 12 else "moba" if k < 20 else "dsa"

    def pair_slot(k):
        return 4 + k // 2 if k < 12 else (k - 12) // 2

    def head_in(k):
        kd = kind(k)
        j = {"sb": k, "x": k - 8, "moba": k - 12, "dsa": k - 20}[kd]
        q, kk, v = {"sb": (q1, k1, v1), "x": (xq, mk, mv), "moba": (qa, ka, va), "dsa": (qb, kb, vb)}[kd]
        p0 = DH * (j % 2)
        return q[p0:p0 + DH, j // 2, :], kk[p0:p0 + DH, j // 2, :], v[:, :, DH * j:DH * j + DH], p0

    first = {}
    for u, x in enumerate(units):
        first.setdefault(x["name"], u)
    second_merge = first["gate2"] + 8
    N_ROPE = len(rope_of)
    gain_at = (8, 0, 20, 28)
    norm_event, post_event, moe_event, last_event = (0, 1, 3, 5), (2, 4), 6, 7
    out0, out20 = first["out"], first["out2"]
    S2 = G0 + 2

    def ffn_loop(eng, triple):
        triple(1)
        with eng.Fori(2, NF - 1) as i:
            triple(i)
        triple(NF - 1)

    block_cm = nc.Block()
    block = block_cm.__enter__()

    @block.sync
    def _(sp):
        def load(u):
            if u >= 3:
                sp.wait_ge(lo_ready, u - 2)
            kc, cols = units[u]["kc"], units[u]["cols"]
            dst = ring[:, u % 3, 0:kc * cols].rearrange("p (c n) -> p c n", c=kc)
            for c0, c1, src in units[u]["src"]:
                sp.dma_start(dst[:, :, c0:c1], src).then_inc(landed[u % 3], 16)

        for tb in range(TB):
            sp.dma_start(h[:, tb, :], a["x"][0, P * tb:P * tb + P, :]).then_inc(in_x[tb], 16)
        load(0)
        sp.wait_ge(in_rows, 80)
        load(1)
        sp.dma_start(mem_tok[:, :, :], a["mem"][0].rearrange("(b p) n -> p b n", p=P)).then_inc(in_mem, 16)
        for u in range(2, S2 + 3):
            load(u)
        up_v = a["w_ffn_in"][0].rearrange("(c p) n -> p c n", p=P)
        down_v = a["w_ffn_out"][0].rearrange("(c p) n -> p c n", p=P)
        with sp.Fori(2, NF - 1) as i:
            addresses = [sp.snap(i * UC), sp.snap(i * UC + FF), sp.snap(i * 2 - 2)]
            freed = [sp.snap(i * 3 + (S2 - 3 + j - 2)) for j in range(3)]
            for j in range(3):
                s = (S2 + j) % 3
                sp.wait_ge(lo_ready, freed[j])
                if j < 2:
                    dst = ring[:, s, :].rearrange("p (c n) -> p c n", c=KC)
                    src = up_v[:, :, bass.ds(addresses[j], UC)]
                else:
                    dst = ring[:, s, :].rearrange("p (c n) -> p c n", c=2)
                    src = down_v[:, bass.ds(addresses[j], 2), :]
                sp.dma_start(dst, src).then_inc(landed[s], 16)
        w1, w3, w2 = a["w1_2"][0], a["w3_2"][0], a["w2_2"][0]
        sources = (w1.rearrange("e (p c) f -> p e c f", c=KC), w3.rearrange("e (p c) f -> p e c f", c=KC),
                   w2.rearrange("e (c p) n -> p e c n", p=P))

        def expert_load(e, places, which, landing):
            src = sources[which][:, bass.ds(e, 1), :, :].rearrange("p e c n -> p (e c) n")
            sp.dma_start(places[which], src).then_inc(landing, 16)

        for u in range(S2 + 3 * (NF - 2), U):
            if u == second_merge + 2:
                sp.wait_ge(o_done, 20)
                expert_load(0, odd_w, 0, landed_w[1][0])
            elif u in (second_merge + 5, second_merge + 7):
                if u == second_merge + 5:
                    sp.wait_ge(o_done, 28)
                which = (u - second_merge - 3) // 2
                expert_load(0, odd_w, which, landed_w[1][which])
            load(u)
        sp.wait_ge(merged_ready, 8)
        expert_load(1, even_w, 0, landed_w[0][0])
        sp.wait_ge(lo_ready, U)
        expert_load(1, even_w, 1, landed_w[0][1])
        expert_load(1, even_w, 2, landed_w[0][2])
        sp.wait_ge(unit_done, U)
        for which in range(3):
            expert_load(2, third_w, which, in_third3[which])
        for which in range(3):
            sp.wait_ge((e_w1, e_up, e_y)[which], 1)
            expert_load(3, odd_w, which, landed_w[1][which])

        def stream(pass_, lo_pair):
            with sp.Fori(lo_pair, EXPERTS // 2) as i:
                for odd in range(2):
                    e = sp.snap(i * 2 + odd)
                    used = sp.snap(i * 2 + (pass_ * EXPERTS + odd - 1))
                    for which in range(3):
                        sp.wait_ge((e_w1, e_up, e_y)[which], used)
                        expert_load(e, (even_w, odd_w)[odd], which, landed_w[odd][which])

        stream(0, 2)
        sp.wait_ge(passes_ready, 1)
        n_pass = sp.value_load(passes_i[0:1, 0:1], min_val=1, max_val=T // SLOTS)
        with sp.If(n_pass > 1):
            with sp.Fori(1, n_pass) as again:
                stream(again, 0)
            sp.nop()
        for tb in range(TB):
            sp.wait_ge(fin_ready, tb + 1)
            sp.dma_start(out[0, P * tb:P * tb + P, :], n3[:, tb, :]).then_inc(fin_out, 16)
        sp.wait_ge(fin_out, 32)

    @block.gpsimd
    def _(pool):
        nc.gpsimd.memset(minus_half[:, :], -0.5).then_inc(half_ready, 1)
        pool.wait_ge(half_ready, 1)

        def row_load(i, v):
            pool.dma_start(gain_rows[i][:, :], v.partition_broadcast(P)).then_inc(in_gain[i], 16)

        def inverse_root(n):
            pool.wait_ge(mean_done, n + 1)
            nc.gpsimd.tensor_tensor(stat[:, n, 6:8], stat[:, n, 2:4], minus_half[:, :], ALU.pow)\
                .then_inc(root_done, 1)

        rest = TABLE["ident"][1]
        pool.wait_ge(in_rows, 80)
        pool.dma_start(tab[:, rest:], table[:, rest:]).then_inc(in_table, 16)
        pool.dma_start(win[:, :, :], windows).then_inc(in_win, 16)
        inverse_root(0)
        inverse_root(1)

        def add_up(layer):
            g, n, u0 = ((gates, 8, first["merge"]), (gates2, 8, second_merge))[layer]
            for j in range(4):
                for b in (1, 2)[:2 - layer]:
                    u = u0 + (4 + 2 * j + b - 1 if layer == 0 else 4 + j)
                    total = g[:, 2 * j:2 * j + 2, :].rearrange("p a b -> p (a b)")
                    part = g[:, n * b + 2 * j:n * b + 2 * j + 2, :].rearrange("p a b -> p (a b)")
                    pool.wait_ge(out_dve, outs(u, True))
                    done = (2 * j + b if layer == 0 else 8 + j + 1)
                    nc.gpsimd.tensor_tensor(total, total, part, ALU.add).then_inc(sum_ready, 1)
                    pool.wait_ge(sum_ready, done)

        row_load(0, a["norm_mix_post"][0])
        row_load(1, a["norm_ffn_post"][0])
        for c0, n, w, b in ((0, GROUPS, "w_group_2", "b_group_2"), (GROUPS, EXPERTS, "w_expert_2", "b_expert_2")):
            pool.dma_start(w_route[:, :, c0:c0 + n], a[w][0].rearrange("(c p) n -> p c n", p=P))\
                .then_inc(in_route, 16)
            pool.dma_start(b_route[:, c0:c0 + n], a[b][0].partition_broadcast(P)).then_inc(in_route, 16)
        add_up(0)
        inverse_root(2)
        row_load(0, a["g_ffn_2"][0])
        inverse_root(3)
        inverse_root(4)
        row_load(1, a["g_final_2"])
        inverse_root(5)
        for j in range(8):
            u = first["gate2"] + j
            wait_out(pool, u)
            pool.wait_ge(row_kept, 1)
            part = gates2[:, 2 * j:2 * j + 2, :]
            nc.gpsimd.tensor_tensor(part, part, rstd_row[:, :].unsqueeze(1).to_broadcast([P, 2, T]), ALU.mult)\
                .then_inc(gate2_scaled, 1)
        add_up(1)
        inverse_root(6)
        inverse_root(7)

    @block.tensor
    def _(pe):
        mm = nc.tensor.matmul

        def three(dst, l_hi, l_lo, r_hi, r_lo, start, stop):
            mm(dst, l_hi, r_hi, start=start, stop=False)
            mm(dst, l_hi, r_lo, start=False, stop=False)
            return mm(dst, l_lo, r_hi, start=False, stop=stop)

        def unit(u):
            x = units[u]
            kc, cols, s = x["kc"], x["cols"], u % 3
            hi = w_hi[:, s, 0:kc * cols].rearrange("p (c n) -> p c n", c=kc)
            lo = w_lo[:, s, 0:kc * cols].rearrange("p (c n) -> p c n", c=kc)
            pe.wait_ge(lo_ready, u + 1)
            if x["form"] == "F":
                return down(x["i"], hi, lo)
            if bank_before[u] is not None:
                wait_out(pe, bank_before[u])
            part_ready = None
            if u in after_norm:
                n = after_norm.index(u)
                part_ready = lambda c: pe.wait_ge(x_ready, 4 * n + c // 2 + 1)
            elif u in (out0, out20):
                n = 4 if u == out20 else 0
                part_ready = lambda c: pe.wait_ge(merged_ready, n + c // 2 + 1)
            dense(x, bank_of[u], hi, lo, part_ready).then_inc(unit_done, 1)

        def dense(x, bank, hi, lo, part_ready=None):
            kc, cols = x["kc"], x["cols"]
            a_hi, a_lo, o = x_hi, x_lo, 0
            if x["name"] in ("merge", "mk", "mv"):
                a_hi, a_lo, o = o_hi, o_lo, x.get("o0", 0)
            if x["form"] == "A":
                for tb in range(TB):
                    for c in range(kc):
                        if part_ready and tb == 0 and c % 2 == 0:
                            part_ready(c)
                        tok = slice(P * tb, P * tb + P)
                        last = three(ps[:, bank, cols * tb:cols * tb + cols], a_hi[:, o + c, tok],
                                     a_lo[:, o + c, tok], hi[:, c, :], lo[:, c, :], c == 0, c == kc - 1)
            elif x["form"] == "B":
                for nb in range(cols // P):
                    for c in range(kc):
                        if part_ready and nb == 0 and c % 2 == 0:
                            part_ready(c)
                        col = slice(P * nb, P * nb + P)
                        last = three(ps[:, bank, T * nb:T * nb + T], hi[:, c, col], lo[:, c, col],
                                     a_hi[:, o + c, :], a_lo[:, o + c, :], c == 0, c == kc - 1)
            else:
                for c in range(kc):
                    if c % 2 == 0:
                        part_ready(c)
                    three(ps[:, bank, 0:T], hi[:, c, 0:P], lo[:, c, 0:P], a_hi[:, c, :], a_lo[:, c, :],
                          c == 0, c == kc - 1)
                for c in range(kc):
                    last = three(ps[0:8, bank, T:2 * T], hi[:, c, P:P + 8], lo[:, c, P:P + 8], a_hi[:, c, :],
                                 a_lo[:, c, :], c == 0, c == kc - 1)
            return last

        def down(i, hi, lo):
            first, end = isinstance(i, int) and i == 0, isinstance(i, int) and i == NF - 1
            pe.wait_ge(act_ready, i + 1)
            for c in range(2):
                for tb in range(TB):
                    for half in range(2):
                        tok, col = slice(P * tb, P * tb + P), slice(512 * half, 512 * half + 512)
                        last = three(ps[:, 4 + 2 * tb + half, :], o_hi[:, c, tok], o_lo[:, c, tok],
                                     hi[:, c, col], lo[:, c, col], first and c == 0, end and c == 1)
            last.then_inc(unit_done, 1)

        def triple(i):
            for j in range(3):
                x, s = units[S2 + j], (S2 + j) % 3
                pe.wait_ge(lo_ready, i * 3 + (S2 - 3 + j + 1))
                shape = dict(c=x["kc"])
                hi = w_hi[:, s, :].rearrange("p (c n) -> p c n", **shape)
                lo = w_lo[:, s, :].rearrange("p (c n) -> p c n", **shape)
                if j == 2:
                    down(i - 1, hi, lo)
                    continue
                if j == 0:
                    pe.wait_ge(gate_out, i)
                else:
                    pe.wait_ge(out_dve, i + outs(G0 - 1, True))
                dense(x, j, hi, lo).then_inc(unit_done, 1)

        after_norm = (first["p"], first["mk"], first["g"], first["kiwi"])

        def row(n):
            pe.wait_ge(root_done, norm_event[n] + 1)
            for tb in range(TB):
                scale = stat[:, norm_event[n], 6 + tb:7 + tb].to_broadcast([P, P])
                last = mm(ps[:, 6 if n < 2 else 2, P * tb:P * tb + P], scale, ident, start=True, stop=True)
            last.then_inc(row_done, 1)

        def turn_over(src, g):
            for tb in range(TB):
                for c in (2 * g, 2 * g + 1):
                    last = nc.tensor.transpose(ps[:, 2 + g, T * (c % 2) + P * tb:T * (c % 2) + P * tb + P],
                                               src[:, tb, P * c:P * c + P], ident)
            last.then_inc(norm_T, 1)

        def norm(n):
            if n == 0:
                pe.wait_ge(in_ident, 16)
                for tb in range(TB):
                    pe.wait_ge(in_x[tb], 16)
            else:
                pe.wait_ge(in_mem, 16)
                pe.wait_ge(f_ready, 4)
            for g in range(4):
                turn_over((h, mem_tok)[n], g)
            if n == 0:
                pe.wait_ge(in_rows, 80)
                nc.tensor.transpose(ps[:, 7, 0:36], rows[:, :], ident[0:36, 0:36]).then_inc(vec_T, 1)
                row(0)

        def scores(k, lo):
            q, kk, v, p0 = head_in(k)
            if k >= lo + 2:
                pe.wait_ge(mid_ready, k - 1)
            bank = 4 + k % 2
            if kind(k) == "sb":
                mm(ps[:, bank, 0:T], kk[:, 0:P], q, start=True, stop=True)
                last = mm(ps[:, bank, T:CAUSAL], kk[:, P:T], q[:, P:T], start=True, stop=True)
            elif kind(k) == "x":
                for tb in range(TB):
                    last = mm(ps[:, bank, T * tb:T * tb + T], q[:, P * tb:P * tb + P], kk, start=True,
                              stop=True)
            else:
                mm(ps[:, bank, 0:P], q[:, 0:P], kk[:, 0:P], start=True, stop=True)
                last = mm(ps[:, bank, P:CAUSAL], q[:, P:T], kk, start=True, stop=True)
            last.then_inc(z_done, 1)

        def middle(k, lo):
            pe.wait_ge(mid_ready, k + 1)
            if k >= lo + 2:
                pe.wait_ge(right_ready, k - 1)
            m, src = ps[:, (6, 2)[k % 2], :], prob_b[k % 2]
            if kind(k) == "sb":
                later = const("later")
                mm(m[:, 0:T], later, src[:, 0:T], start=True, stop=False)
                mm(m[:, P:T], ones[:, :], src[:, T:CAUSAL], start=False, stop=True)
                last = mm(m[:, T:CAUSAL], later, src[:, T:CAUSAL], start=True, stop=True)
            elif kind(k) == "x":
                for tb in range(TB):
                    for mb in range(TB):
                        last = nc.tensor.transpose(m[:, T * mb + P * tb:T * mb + P * tb + P],
                                                   src[:, T * tb + P * mb:T * tb + P * mb + P], ident)
            else:
                for t in range(3):
                    last = nc.tensor.transpose(m[:, P * t:P * t + P], src[:, P * t:P * t + P], ident)
            last.then_inc(mid_done, 1)

        def values(pair, lo):
            k = pair[1]
            pe.wait_ge(right_ready, k + 1)
            if k >= lo + 4:
                pe.wait_ge(pair_out, k // 2 - 1)
            both = [(head_in(x), ps[DH * (x % 2):DH * (x % 2) + DH, (7, 3)[x // 2 % 2], :], right_b[x % 2])
                    for x in pair]
            for (_, _, v, _), o, r in both:
                mm(o[:, 0:T], v[:, 0, :], r[:, 0:T], start=True, stop=False)
            for (_, _, v, _), o, r in both:
                if kind(k) == "x":
                    last = mm(o[:, 0:T], v[:, 1, :], r[:, T:2 * T], start=False, stop=True)
                else:
                    last = mm(o[:, P:T], v[:, 1, :], r[:, T:CAUSAL], start=False, stop=True)
                last.then_inc(o_done, 1)

        def route_logits(r):
            pe.wait_ge(route_out, r + 1)
            if r == 0:
                pe.wait_ge(in_route, 64)
            for tb in range(TB):
                for c in (2 * r, 2 * r + 1):
                    last = mm(ps[:, 6 + tb, 0:36], n3T[:, c, P * tb:P * tb + P], w_route[:, c, :], start=c == 0,
                              stop=c == KC - 1)
            if r == 3:
                last.then_inc(logit_done, 1)

        for step, *arg in plan:
            if step == "norm":
                norm(arg[0])
            elif step == "residual":
                for g in range(4):
                    pe.wait_ge(h_ready, 8 * arg[0] + 2 * (g + 1))
                    turn_over(h, g)
            elif step == "row":
                row(arg[0])
                wait_out(pe, first["kiwi"])
                for tb in range(TB):
                    last = nc.tensor.transpose(ps[:, 3, 8 * tb:8 * tb + 8], score_b[0][0:8, P * tb:P * tb + P],
                                               ident[0:8, 0:8])
                last.then_inc(wi_T, 1)
            elif step == "unit":
                u = arg[0]
                if units[u]["name"] == "merge" and units[u]["j"] == 0:
                    if units[u]["b"] == 0:
                        pe.wait_ge(*((pool_out, 1) if u < G0 else (pair_out, 10)))
                    else:
                        pe.wait_ge(pair_out, 6 if u < G0 else 14)
                unit(u)
            elif step == "pool_window":
                wait_out(pe, first["p"] + 1)
                pe.wait_ge(in_win, 16)
                pe.wait_ge(f_ready, 5)
                for g in range(4):
                    dst = ps[:, 6, T * g:T * g + T] if g < 2 else ps[:, 7, T * (g - 2):T * (g - 2) + T]
                    col = slice(P * g, P * g + P)
                    mm(dst, p_tok[:, 0, col], win[:, g, 0:T], start=True, stop=False)
                    last = mm(dst[:, P:T], p_tok[:, 1, col], win[:, g, T:CAUSAL], start=False, stop=True)
                last.then_inc(pool_w, 1)
            elif step == "pool_mix":
                pe.wait_ge(pool_mixed, 1)
                pe.wait_ge(in_mix, 16)
                for g in range(4):
                    dst = ps[:, 6, T * g:T * g + T] if g < 2 else ps[:, 7, T * (g - 2):T * (g - 2) + T]
                    last = mm(dst, pool_w_sb[:, g, :], mixed[:, g, :], start=True, stop=True)
                last.then_inc(pool_p, 1)
            elif step == "heads":
                s_, m_, v_ = arg
                lo = 0 if max(s_ + m_ + v_) < 12 else 12
                if s_ == [0]:
                    wait_out(pe, first["xq"])
                if s_ == [1]:
                    pe.wait_ge(pool_out, 1)
                if s_ == [8]:
                    wait_out(pe, first["mv"])
                if 12 in s_:
                    pe.wait_ge(rope_done, N_ROPE)
                    wait_out(pe, first["va"] + 1)
                    pe.wait_ge(ix_acc, 8)
                if v_:
                    values(v_, lo)
                for k in m_:
                    middle(k, lo)
                for k in s_:
                    scores(k, lo)
            elif step == "ffn":
                unit(G0)
                row(2)
                unit(G0 + 1)
                ffn_loop(pe, triple)
                unit(S2 + 3 * (NF - 1))
            elif step == "rope":
                r, u = arg
                wait_out(pe, u)
                if r >= 1:
                    pe.wait_ge(rope_done, r)
                n = T if r == 0 else 2 * T
                mm(ps[:, 7, 0:n], const("rotate"), prob_b[r % 2][:, 0:n], start=True, stop=True)\
                    .then_inc(rot_done, 1)
            elif step == "index":
                pe.wait_ge(rope_done, 3)
                for i in (arg[0], arg[0] + 1):
                    p0 = DH * (i % 2)
                    q, kk, bank = qi[p0:p0 + DH, i // 2, :], ki[p0:p0 + DH, :], 4 + i % 2
                    if i >= 2:
                        pe.wait_ge(ix_relu, i - 1)
                    mm(ps[:, bank, 0:P], q[:, 0:P], kk[:, 0:P], start=True, stop=True)
                    mm(ps[:, bank, P:CAUSAL], q[:, P:T], kk, start=True, stop=True).then_inc(ix_z, 1)
            elif step == "route":
                r = arg[0]
                if r:
                    route_logits(r - 1)
                pe.wait_ge(hg_ready, r + 1)
                for tb in range(TB):
                    for c in range(2):
                        last = nc.tensor.transpose(ps[:, 2 + r, T * c + P * tb:T * c + P * tb + P],
                                                   n3[:, tb, UC * r + P * c:UC * r + P * c + P], ident)
                last.then_inc(route_T, 1)
            elif step == "memory":
                if arg[0] == 0:
                    row(1)
            elif step in ("finish", "topk", "select", "sigmoid"):
                pass
            else:
                raise ValueError(step)

        route_logits(3)
        pe.wait_ge(route_sel, 1)
        before = const("before")
        mm(ps[:, 1, 0:EXPERTS], before, chosen[:, 0, :], start=True, stop=True)
        mm(ps[:, 1, EXPERTS:2 * EXPERTS], before, chosen[:, 1, :], start=True, stop=False)
        mm(ps[:, 1, EXPERTS:2 * EXPERTS], ones[:, :], chosen[:, 0, :], start=False, stop=True)
        mm(ps[:, 1, 64:64 + EXPERTS], ones[:, :], chosen[:, 0, :], start=True, stop=False)
        mm(ps[:, 1, 64:64 + EXPERTS], ones[:, :], chosen[:, 1, :], start=False, stop=True).then_inc(rank_done, 1)

        def quad_body(q):
            looped = not isinstance(q, int)
            e0 = pe.snap(q * QUAD) if looped else 0
            if not looped:
                pe.wait_ge(n3_ready, 2)
            pe.wait_ge(hot_part, q * 2 + 2)
            for c in range(KC):
                for tb in range(TB):
                    last = mm(ps[:, 2 + c // 4, P * (c % 4):P * (c % 4) + P], n3[:, tb, c:D:KC],
                              one_hot[:, tb, :], start=tb == 0, stop=tb == 1)
            last.then_inc(xg_done, 1)
            pe.wait_ge(hot_ready, q + 1)
            for tb in range(TB):
                last = nc.tensor.transpose(ps[:, 0, P * tb:P * tb + P], gated_hot[:, tb, :], ident)
            last.then_inc(gt_done, 1)
            pe.wait_ge(xg_part, q + 1)
            pe.wait_ge(xg_ready, q + 1)
            for e in range(QUAD):
                if looped:
                    places, landing = (even_w, odd_w)[e % 2], landed_w[e % 2]
                    arrived = pe.snap(q * 32 + 8 * (e + e % 2))
                else:
                    places = (odd_w, even_w, third_w, odd_w)[e]
                    landing = (landed_w[1], landed_w[0], in_third3, landed_w[1])[e]
                    arrived = (16, 16, 16, 32)[e]
                done = pe.snap(e0 + e) if looped else e
                for n in range(2):
                    pe.wait_ge(landing[n], arrived)
                    for c in range(KC):
                        for g in range(4):
                            last = mm(ps[SLOTS * g:SLOTS * g + SLOTS, 4 + e % 2, P * n:P * n + P],
                                      xg[:, c, SLOTS * e:SLOTS * e + SLOTS], places[n][:, c, P * g:P * g + P],
                                      start=c == 0, stop=c == KC - 1, tile_position=(0, SLOTS * g))
                    last.then_inc((e_w1, e_up)[n], 1)
                pe.wait_ge(e_hid, done + 1)
                nc.tensor.transpose(ps[:, 6, 0:P], hid[:, :], ident).then_inc(e_T, 1)
                pe.wait_ge(landing[2], arrived)
                pe.wait_ge(e_hidT, done + 1)
                for b in range(4):
                    for g in range(4):
                        last = mm(ps[SLOTS * g:SLOTS * g + SLOTS, 7, 0:UC],
                                  hid_T[:, SLOTS * b:SLOTS * b + SLOTS], places[2][:, b, UC * g:UC * g + UC],
                                  start=b == 0, stop=b == 3, tile_position=(0, SLOTS * g))
                last.then_inc(e_y, 1)
            pe.wait_ge(gt_ready, q + 1)
            pe.wait_ge(e_yA, e0 * 2 + 2 * QUAD)
            pe.wait_ge(e_yD, e0 * 2 + 2 * QUAD)
            for tb in range(TB):
                for half in range(2):
                    last = mm(ps[:, 2 * tb + half, :], gate_T[:, P * tb:P * tb + P],
                              y_quad[:, 512 * half:512 * half + 512], start=True, stop=True)
                last.then_inc(comb_done, 1)

        quad_body(0)
        pe.wait_ge(passes_ready, 1)
        n_pass = pe.value_load(passes_i[0:1, 0:1], min_val=1, max_val=T // SLOTS)
        with pe.Fori(1, n_pass * (EXPERTS // QUAD)) as q:
            quad_body(q)

    @block.scalar
    def _(act):
        chain = [0]
        fn = nc.scalar.activation

        def link(ins):
            chain[0] += 1
            ins.then_inc(act_chain, 1)
            act.wait_ge(act_chain, chain[0])

        nc.scalar.add_instruction(mybir.InstLoadActFuncSet(act_func_set_id=EXP_AND_LN, ins=[], outs=[],
                                                           name=nc.get_next_instruction_name()))
        act.dma_start(ident, table[:, 0:P]).then_inc(in_ident, 16)
        r = 0
        for name, n in (("norm_mem", 8), ("norm_mix_pre", 8), ("pool_scale", 4), ("norm_ffn_pre", 8),
                        ("g_mix_2", 8)):
            act.dma_start(rows[r:r + n, :], a[name][0].rearrange("(r n) -> r n", n=P)).then_inc(in_rows, 16)
            r += n
        act.dma_start(pool_w_sb[:, :, :], a["w_pool_mix"][0].rearrange("g c d -> c g d")).then_inc(in_mix, 16)

        next_split = [0]

        def split(u):
            while next_split[0] <= min(u, U - 1):
                split_one(next_split[0])
                next_split[0] += 1

        def split_one(u):
            x = units[u]
            n = x["kc"] * x["cols"]
            if u >= 3:
                act.wait_ge(unit_done, u - 2)
            act.wait_ge(landed[u % 3], landings(u))
            fn(w_hi[:, u % 3, 0:n], ring[:, u % 3, 0:n], ACT.Copy).then_inc(hi_ready, 1)

        def split_ffn(i, j):
            if isinstance(i, int):
                next_split[0] = S2 + 3 * (i - 1) + j + 2
                return split(S2 + 3 * (i - 1) + j + 2)
            s = (S2 + j + 2) % 3
            act.wait_ge(unit_done, i * 3 + (S2 - 3 + j))
            act.wait_ge(landed[s], i * 16 + (landings(S2 + 3 + j + 2) - 32))
            fn(w_hi[:, s, :], ring[:, s, :], ACT.Copy).then_inc(hi_ready, 1)

        copies = {"mk": mk, "q": q1, "k": k1, "xq": xq}
        tokens = {"mv": mv, "p": p_tok, "v": v1, "vb": vb, "va": va}

        def evacuate(u):
            x = units[u]
            name, j = x["name"], x.get("j", 0)
            full = ps[:, bank_of[u], :]
            act.wait_ge(unit_done, u + 1)
            if name in copies:
                scale = 0.125 if name in ("q", "xq") else 1.0
                dst = copies[name][:, 2 * j:2 * j + 2, :].rearrange("p a b -> p (a b)")
                fn(dst, full, ACT.Copy, scale=scale).then_inc(out_act, 1)
            elif name in tokens:
                dst = tokens[name]
                if u < G0:
                    fn(dst[:, :, UC * j:UC * j + UC], full.rearrange("p (a b) -> p a b", a=2), ACT.Copy)\
                        .then_inc(out_act, 1)
                else:
                    for tb in range(TB):
                        ins = fn(dst[:, tb, UC * j:UC * j + UC], full[:, UC * tb:UC * tb + UC], ACT.Copy,
                                 scale=stat[:, norm_event[3], 6 + tb:7 + tb])
                        link(ins) if tb == 0 else ins.then_inc(out_act, 1)
            elif name in ("gate", "gate2"):
                dst = (gates if name == "gate" else gates2)[:, 2 * j:2 * j + 2, :]
                fn(dst.rearrange("p a b -> p (a b)"), full, ACT.Copy).then_inc(out_act, 1)
            elif name == "kiwi":
                act.wait_ge(sq_done, 4)
                link(fn(score_b[0][0:8, 0:T], full[0:8, T:2 * T], ACT.Copy, scale=512.0 ** -0.5))
                fn(prob_b[0][:, 0:T], full[:, 0:T], ACT.Copy).then_inc(out_act, 1)
            elif name in ROPED:
                r = rope_of[u]
                if r >= 2:
                    act.wait_ge(rope_done, r - 1)
                fn(prob_b[r % 2][:, :], full, ACT.Copy).then_inc(out_act, 1)
            else:
                raise ValueError(name)

        def squares(event, src, ready, junk=junk):
            for tb in range(TB):
                ready(tb)
                ins = fn(junk[:, :], src[:, tb, :], ACT.Square, accum_out=stat[:, event, tb:tb + 1])
                link(ins) if tb == 0 else ins.then_inc(sq_done, 1)

        def norm_hi(n, g):
            act.wait_ge(f_ready, 4 * n + g + 1)
            fn((x_hi, o_hi)[n][:, 2 * g:2 * g + 2, :].rearrange("p a b -> p (a b)"),
               x_f[:, 2 * g:2 * g + 2, :].rearrange("p a b -> p (a b)"), ACT.Copy).then_inc(xh_ready, 1)

        def column_squares(src, j, count, junk=junk):
            for tb in range(TB):
                ins = fn(junk[:, 0:UC], src(tb), ACT.Square, accum_out=sq_part[:, tb, j:j + 1])
                link(ins) if tb == 0 else ins.then_inc(sq_ready, 1)
            act.wait_ge(sq_ready, count)

        def scores(k):
            s = k % 2
            if kind(k) == "sb":
                act.wait_ge(z_done, k + 1)
                if k >= 2:
                    act.wait_ge(mid_ready, k - 1)
                link(fn(score_b[s][:, 0:CAUSAL], ps[:, 4 + s, 0:CAUSAL], ACT.Abs))
                link(fn(score_b[s][:, 0:CAUSAL], score_b[s][:, 0:CAUSAL], ACT.Exp, scale=-1.0))
                fn(score_b[s][:, 0:CAUSAL], score_b[s][:, 0:CAUSAL], ACT.Ln, bias=1.0).then_inc(exp_done, 1)
            else:
                act.wait_ge(prep_done, k - 7)
                scale = 1.0 if kind(k) == "x" else 0.125
                c = (0, T, 2 * T) if kind(k) == "x" else (0, P, CAUSAL)
                src = ps[:, 4 + s, :] if kind(k) == "x" else score_b[s]
                for tb in range(TB):
                    ins = fn(prob_b[s][:, c[tb]:c[tb + 1]], src[:, c[tb]:c[tb + 1]], ACT.Exp,
                             bias=softmax[:, 8 * s + tb:8 * s + tb + 1], scale=scale,
                             accum_out=softmax[:, 8 * s + 2 + tb:8 * s + 3 + tb])
                    link(ins) if tb == 0 else ins.then_inc(exp_done, 1)

        def middle(k):
            if k >= 12:
                act.wait_ge(mid_done, k + 1)
                fn(right_b[k % 2][:, 0:CAUSAL], ps[:, (6, 2)[k % 2], 0:CAUSAL], ACT.Copy).then_inc(right_ready, 1)
            if kind(k) == "sb":
                act.wait_ge(expo_ready, k + 1)
                fn(right_b[k % 2][:, 0:CAUSAL], expo_b[k % 2][:, 0:CAUSAL], ACT.Exp).then_inc(a_done, 1)

        used = 0
        for step, *arg in plan:
            if step == "norm" and arg[0] == 0:
                squares(norm_event[0], h, lambda tb: act.wait_ge(in_x[tb], 16))
                split(0)
                for g in range(4):
                    norm_hi(0, g)
                split(1)
            elif step == "norm":
                act.wait_ge(in_mem, 16)
                squares(norm_event[1], mem_tok, lambda tb: None)
            elif step == "memory":
                if arg[0] >= 0:
                    norm_hi(1, arg[0])
            elif step == "residual":
                if arg[0] == 1:
                    act.wait_ge(unit_done, G0 + 3 * NF)
                    for tb in range(TB):
                        if tb:
                            act.wait_ge(y_half, 2)
                        for half in range(2):
                            fn(junk[:, 0:512], ps[:, 4 + 2 * tb + half, :], ACT.Square,
                               accum_out=sq_part[:, tb, half:half + 1]).then_inc(sq_half, 1)
                            act.wait_ge(sq_half, 2 * tb + half + 1)
                if used:
                    act.wait_ge(unit_done, used)
                n = arg[0] + 2
                for g in range(4):
                    act.wait_ge(norm_T, 4 * n + g + 1)
                    for c in (2 * g, 2 * g + 1):
                        ins = fn(x_hi[:, c, :], ps[:, 2 + g, T * (c % 2):T * (c % 2) + T], ACT.Copy,
                                 scale=vec[:, gain_at[n] + c:gain_at[n] + c + 1])
                    ins.then_inc(xh_ready, 1)
                act.wait_ge(h_ready, 8 * arg[0] + 8)
                squares(norm_event[n], h, lambda tb: None)
            elif step == "unit":
                u = arg[0]
                used = u + 1
                ending = u in (out0 - 2, out0 - 1, out20 - 3, out20 - 2, out20 - 1)
                if not ending:
                    split(u + 2)
                if units[u]["name"] == "out":
                    j = units[u]["j"]
                    act.wait_ge(unit_done, u + 1)
                    column_squares(lambda tb: ps[:, bank_of[u], UC * tb:UC * tb + UC], j, j + 1)
                elif units[u]["name"] not in BY_VECTOR:
                    evacuate(u)
                if u == out20 - 1:
                    split(out20)
                if (u + 3 < G0 or u >= G0 + 3 * NF) and not ending:
                    split(u + 3)
            elif step == "route":
                r = arg[0]
                act.wait_ge(hg_ready, r + 1)
                column_squares(lambda tb: h[:, tb, UC * r:UC * r + UC], r, 4 + r + 1, y_quad)
            elif step == "sigmoid":
                wait_out(act, (first["merge"], second_merge)[arg[0]] - 1)
                if arg[0] == 1:
                    act.wait_ge(gate2_scaled, 8)
                g = (gates, gates2)[arg[0]]
                for b, j in arg[1]:
                    part = g[:, 8 * b + 2 * j:8 * b + 2 * j + 2, :].rearrange("p a b -> p (a b)")
                    fn(part, part, ACT.Sigmoid).then_inc(sig_ready, 1)
            elif step == "finish":
                j = arg[0]
                act.wait_ge(sum_ready, 2 * (j + 1) if used <= G0 else 8 + j + 1)
                g = gates if used <= G0 else gates2
                fn(x_hi[:, 2 * j:2 * j + 2, :].rearrange("p a b -> p (a b)"),
                   g[:, 2 * j:2 * j + 2, :].rearrange("p a b -> p (a b)"), ACT.Copy).then_inc(sum_hi, 1)
            elif step == "row":
                pass
            elif step == "pool_window":
                act.wait_ge(pool_w, 1)
                for b in range(2):
                    ins = fn(mixed[:, 2 * b:2 * b + 2, :].rearrange("p a b -> p (a b)"), ps[:, 6 + b, :], ACT.Copy)
                    link(ins) if b == 0 else ins.then_inc(pool_mixed, 1)
            elif step == "heads":
                for k in arg[1]:
                    middle(k)
                for k in arg[0]:
                    scores(k)
            elif step == "index":
                for i in (arg[0], arg[0] + 1):
                    act.wait_ge(ix_z, i + 1)
                    if i >= 2:
                        act.wait_ge(ix_acc, i - 1)
                    fn(score_b[i % 2][:, 0:CAUSAL], ps[:, 4 + i % 2, 0:CAUSAL], ACT.Relu).then_inc(ix_relu, 1)
            elif step == "ffn":
                def gate(i):
                    act.wait_ge(gate_out, i + 1)
                    fn(silu_g[:, :], silu_g[:, :], ACT.Silu).then_inc(out_act, 1)

                def triple(i):
                    for j in range(3):
                        split_ffn(i, j)
                        if j == 0:
                            gate(i)

                for j in range(2):
                    split(G0 + j + 2)
                    if j == 0:
                        gate(0)
                ffn_loop(act, triple)
                split(S2 + 3 * (NF - 1) + 2)
                used = G0 + 3 * NF

        act.wait_ge(root_done, moe_event + 1)
        act.wait_ge(route_T, 4)
        for tb in range(TB):
            fn(n3[:, tb, :], n3[:, tb, :], ACT.Copy, scale=stat[:, moe_event, 6 + tb:7 + tb]).then_inc(n3_ready, 1)
        act.wait_ge(route_in, 1)
        fn(exp_out[:, :, :].rearrange("p a b -> p (a b)"), exp_in[:, :, :].rearrange("p a b -> p (a b)"), ACT.Exp)\
            .then_inc(route_exp, 1)

        def quad_body(q):
            e0 = act.snap(q * QUAD) if not isinstance(q, int) else 0
            act.wait_ge(xg_done, q + 1)
            fn(xg[:, 0:4, :].rearrange("p a b -> p (a b)"), ps[:, 2, :], ACT.Copy).then_inc(xg_part, 1)
            act.wait_ge(gt_done, q + 1)
            fn(gate_T[:, :], ps[:, 0, 0:T], ACT.Copy).then_inc(gt_ready, 1)
            for e in range(QUAD):
                act.wait_ge(e_up, e0 + (e + 1))
                fn(silu_e[:, :], ps[:, 4 + e % 2, 0:P], ACT.Silu).then_inc(e_silu, 1)
                act.wait_ge(e_y, e0 + (e + 1))
                for g in (0, 1):
                    fn(y_quad[SLOTS * e:SLOTS * e + SLOTS, UC * g:UC * g + UC],
                       ps[SLOTS * g:SLOTS * g + SLOTS, 7, 0:UC], ACT.Copy).then_inc(e_yA, 1)

        quad_body(0)
        act.wait_ge(passes_ready, 1)
        n_pass = act.value_load(passes_i[0:1, 0:1], min_val=1, max_val=T // SLOTS)
        with act.Fori(1, n_pass * (EXPERTS // QUAD)) as q:
            quad_body(q)
        act.wait_ge(comb_done, n_pass * (EXPERTS // QUAD * TB))
        squares(last_event, h, lambda tb: act.wait_ge(comb_added[tb], n_pass * (EXPERTS // QUAD)), y_quad)

    @block.vector
    def _(dve):
        chain = [0]
        v = nc.vector

        def link(ins):
            chain[0] += 1
            ins.then_inc(dve_chain, 1)
            dve.wait_ge(dve_chain, chain[0])

        next_split = [0]

        def split(u):
            while next_split[0] <= min(u, U - 1):
                split_one(next_split[0])
                next_split[0] += 1

        def split_one(u):
            n = units[u]["kc"] * units[u]["cols"]
            dve.wait_ge(hi_ready, u + 1)
            v.tensor_tensor(w_lo[:, u % 3, 0:n], ring[:, u % 3, 0:n], w_hi[:, u % 3, 0:n].bitcast(F32),
                            ALU.subtract).then_inc(lo_ready, 1)

        def split_ffn(i, j):
            if isinstance(i, int):
                next_split[0] = S2 + 3 * (i - 1) + j + 2
                return split(S2 + 3 * (i - 1) + j + 2)
            s = (S2 + j + 2) % 3
            dve.wait_ge(hi_ready, i * 3 + (S2 - 3 + j + 3))
            v.tensor_tensor(w_lo[:, s, :], ring[:, s, :], w_hi[:, s, :].bitcast(F32), ALU.subtract)\
                .then_inc(lo_ready, 1)

        def flat(x):
            return x.rearrange("p a b -> p (a b)")

        def mean_square(event):
            v.tensor_scalar(stat[:, event, 2:4], stat[:, event, 0:2], 1.0 / D, EPS, ALU.mult, ALU.add)\
                .then_inc(mean_done, 1)

        def gather_squares(event, n):
            link(v.tensor_reduce(stat[:, event, 0:2], sq_part[:, :, 0:n], AX.X, ALU.add))
            mean_square(event)
            dve.wait_ge(root_done, event + 1)

        def take_row(n):
            dve.wait_ge(row_done, n + 1)
            ins = v.tensor_copy(rstd_row[:, :], ps[:, 6 if n < 2 else 2, 0:T])
            if n < 3:
                link(ins)
            else:
                ins.then_inc(row_kept, 1)
                dve.wait_ge(row_kept, 1)

        def norm_full(n, g):
            dve.wait_ge(norm_T, 4 * n + g + 1)
            for c in (2 * g, 2 * g + 1):
                gain = vec[:, gain_at[n] + c:gain_at[n] + c + 1]
                ins = v.scalar_tensor_tensor(x_f[:, c, :], ps[:, 2 + g, T * (c % 2):T * (c % 2) + T], gain,
                                             rstd_row[:, :], ALU.mult, ALU.mult)
                link(ins) if c % 2 == 0 else ins.then_inc(f_ready, 1)

        def norm_lo(n, g):
            dve.wait_ge(xh_ready, 4 * n + g + 1)
            part = slice(2 * g, 2 * g + 2)
            hi, lo = (x_hi, o_hi)[n], (x_lo, o_lo)[n]
            v.tensor_tensor(flat(lo[:, part, :]), flat(x_f[:, part, :]), flat(hi[:, part, :]).bitcast(F32),
                            ALU.subtract).then_inc(x_ready, 1)

        row_twice = rstd_row[:, :].unsqueeze(1).to_broadcast([P, 2, T])

        def halves(x):
            return x.rearrange("p (a b) -> p a b", a=2)

        def post(n):
            if n == 0:
                dve.wait_ge(out_dve, outs(out0 + 3, True))
                gather_squares(post_event[0], 4)
            else:
                dve.wait_ge(unit_done, G0 + 3 * NF)
                dve.wait_ge(in_gain[1], 16)
                for i, tb in enumerate((1, 0)):
                    if i:
                        dve.wait_ge(sq_half, 2)
                    for half in range(2):
                        v.tensor_tensor(y_tok[:, tb, 512 * half:512 * half + 512], ps[:, 4 + 2 * tb + half, :],
                                        gain_rows[1][:, 512 * half:512 * half + 512], ALU.mult).then_inc(y_half, 1)
                dve.wait_ge(y_half, 4)
                dve.wait_ge(sq_half, 4)
                gather_squares(post_event[1], 2)

            def low(g):
                dve.wait_ge(xh_ready, 4 * (n + 2) + g + 1)
                for c in (2 * g, 2 * g + 1):
                    at_c = gain_at[n + 2] + c
                    ins = v.scalar_tensor_tensor(x_lo[:, c, :], ps[:, 2 + g, T * (c % 2):T * (c % 2) + T],
                                                 vec[:, at_c:at_c + 1], x_hi[:, c, :].bitcast(F32), ALU.mult,
                                                 ALU.subtract)
                ins.then_inc(x_ready, 1)

            for g in range(6):
                if g < 4:
                    cols = slice(UC * g, UC * g + UC)
                    for tb in range(TB):
                        v.scalar_tensor_tensor(h[:, tb, cols], y_tok[:, tb, cols],
                                               stat[:, post_event[n], 6 + tb:7 + tb], h[:, tb, cols], ALU.mult,
                                               ALU.add).then_inc(h_ready, 1)
                if g >= 2:
                    low(g - 2)
            dve.wait_ge(sq_done, n + 3)
            mean_square(norm_event[n + 2])

        columns = ((0, P), (P, CAUSAL))

        def maxima(k):
            kd, z, s = kind(k), ps[:, 4 + k % 2, :], k % 2
            dve.wait_ge(z_done, k + 1)
            if kd != "sb":
                if kd == "x":
                    link(v.tensor_reduce(softmax[:, 8 * s + 4:8 * s + 6], z.rearrange("p (a b) -> p a b", a=TB),
                                         AX.X, ALU.max))
                else:
                    hide = const("hide") if kd == "moba" else score[:, :]
                    for tb, (c0, c1) in enumerate(columns):
                        link(v.tensor_tensor_reduce(out=score_b[s][:, c0:c1], in0=z[:, c0:c1],
                                                    in1=hide[:, c0:c1], scale=1.0, scalar=-3e38, op0=ALU.add,
                                                    op1=ALU.max,
                                                    accum_out=softmax[:, 8 * s + 4 + tb:8 * s + 5 + tb]))
                v.tensor_scalar(softmax[:, 8 * s:8 * s + 2], softmax[:, 8 * s + 4:8 * s + 6],
                                -1.0 if kd == "x" else -0.125, None, ALU.mult).then_inc(prep_done, 1)

        def take_middle(k):
            m = ps[:, (6, 2)[k % 2], :]
            dve.wait_ge(mid_done, k + 1)
            if kind(k) == "sb":
                v.tensor_tensor(expo_b[k % 2][:, 0:CAUSAL], expo_b[k % 2][:, 0:CAUSAL], m[:, 0:CAUSAL],
                                ALU.subtract).then_inc(expo_ready, 1)
            else:
                n = 2 * T if kind(k) == "x" else CAUSAL
                v.tensor_copy(right_b[k % 2][:, 0:n], m[:, 0:n]).then_inc(right_ready, 1)

        def take_pair(k):
            if k % 2:
                o, c = ps[:, (7, 3)[k // 2 % 2], 0:T], pair_slot(k)
                dve.wait_ge(o_done, k + 1)
                link(v.tensor_copy(o_hi[:, c, :], o))
                v.tensor_tensor(o_lo[:, c, :], o, o_hi[:, c, :].bitcast(F32), ALU.subtract).then_inc(pair_out, 1)

        def weights(k):
            kd, z, s = kind(k), ps[:, 4 + k % 2, :], k % 2
            dve.wait_ge(exp_done, k + 1)
            if kd == "sb":
                soft = prob_b[s][:, 0:CAUSAL]
                link(v.scalar_tensor_tensor(soft, z[:, 0:CAUSAL], 0.0, score_b[s][:, 0:CAUSAL], ALU.max, ALU.add))
                link(v.tensor_tensor(expo_b[s][:, 0:CAUSAL], z[:, 0:CAUSAL], soft, ALU.subtract))
                v.tensor_tensor(soft, soft, const("keep"), ALU.mult).then_inc(mid_ready, 1)
            else:
                cut = (0, T, 2 * T) if kd == "x" else (0, P, CAUSAL)
                link(v.reciprocal(softmax[:, 8 * s + 6:8 * s + 8], softmax[:, 8 * s + 2:8 * s + 4]))
                for tb in range(TB):
                    part = prob_b[s][:, cut[tb]:cut[tb + 1]]
                    ins = v.tensor_scalar(part, part, softmax[:, 8 * s + 6 + tb:8 * s + 7 + tb], None, ALU.mult)
                    link(ins) if tb == 0 else ins.then_inc(mid_ready, 1)

        def keep_past(k):
            if kind(k) == "sb":
                dve.wait_ge(a_done, k + 1)
                right = right_b[k % 2][:, 0:CAUSAL]
                v.tensor_tensor(right, right, const("keep"), ALU.mult).then_inc(right_ready, 1)

        def merge(u):
            x = units[u]
            g, n = (gates, 8) if u < G0 else (gates2, 8)
            j, b = x["j"], x["b"]
            dve.wait_ge(sig_ready, (j + 1 if b == 0 else 4 + 2 * j + b) if u < G0 else 12 + 4 * b + j + 1)
            part = flat(g[:, n * b + 2 * j:n * b + 2 * j + 2, :])
            v.tensor_tensor(part, part, ps[:, bank_of[u], :], ALU.mult).then_inc(out_dve, 1)

        def finish(j, layer):
            count = 4 * layer + j + 1
            dve.wait_ge(sum_hi, count)
            v.tensor_tensor(flat(x_lo[:, 2 * j:2 * j + 2, :]), flat((gates, gates2)[layer][:, 2 * j:2 * j + 2, :]),
                            flat(x_hi[:, 2 * j:2 * j + 2, :]).bitcast(F32), ALU.subtract).then_inc(merged_ready, 1)

        roped = {"qi": qi, "kb": kb, "qb": qb, "ka": ka, "qa": qa}

        def rope(r, u):
            wait_out(dve, u)
            s, n = r % 2, T if r == 0 else 2 * T
            name = units[u]["name"]
            dst = ki[:, :] if r == 0 else flat(roped[name][:, 2 * units[u]["j"]:2 * units[u]["j"] + 2, :])
            link(v.tensor_tensor(expo_b[s][:, 0:n], prob_b[s][:, 0:n], const("cos")[:, 0:n], ALU.mult))
            dve.wait_ge(rot_done, r + 1)
            link(v.tensor_tensor(right_b[s][:, 0:n], ps[:, 7, 0:n], const("sin")[:, 0:n], ALU.mult))
            v.tensor_tensor(dst, expo_b[s][:, 0:n], right_b[s][:, 0:n], ALU.add).then_inc(rope_done, 1)

        def ffn():
            def gate(i, done):
                dve.wait_ge(unit_done, done)
                if not (isinstance(i, int) and i == 0):
                    dve.wait_ge(act_hi, i)
                v.tensor_tensor(halves(silu_g[:, :]), halves(ps[:, 0, :]), row_twice, ALU.mult).then_inc(gate_out, 1)

            def up(i, done):
                dve.wait_ge(unit_done, done)
                v.tensor_tensor(halves(act_f[:, :]), halves(ps[:, 1, :]), row_twice, ALU.mult).then_inc(out_dve, 1)
                dve.wait_ge(out_dve, i + (outs(G0 - 1, True) + 1))
                dve.wait_ge(out_act, i + (outs(G0 - 1, False) + 1))
                v.tensor_tensor(act_f[:, :], act_f[:, :], silu_g[:, :], ALU.mult).then_inc(up_out, 1)
                dve.wait_ge(up_out, i + 1)

            def parts(i):
                hi, lo = flat(o_hi[:, 0:2, :]), flat(o_lo[:, 0:2, :])
                v.tensor_copy(hi, act_f[:, :]).then_inc(act_hi, 1)
                dve.wait_ge(act_hi, i + 1)
                v.tensor_tensor(lo, act_f[:, :], hi.bitcast(F32), ALU.subtract).then_inc(act_ready, 1)
                dve.wait_ge(act_ready, i + 1)

            def triple(i):
                for j in range(3):
                    split_ffn(i, j)
                    if j == 0:
                        gate(i, i * 3 + (S2 - 3 + 1))
                    elif j == 1:
                        up(i, i * 3 + (S2 - 3 + 2))
                    elif j == 2:
                        dve.wait_ge(unit_done, i * 3 + (S2 - 3 + 3))
                        parts(i)

            split(G0 + 2)
            take_row(2)
            gate(0, G0 + 1)
            split(G0 + 3)
            up(0, G0 + 2)
            parts(0)
            ffn_loop(dve, triple)
            split(S2 + 3 * (NF - 1) + 2)

        v.memset(ones[:, :], 1.0).then_inc(dve_chain, 1)
        chain[0] += 1
        used = 0
        for step, *arg in plan:
            if step == "norm" and arg[0] == 0:
                dve.wait_ge(sq_done, 1)
                mean_square(norm_event[0])
                dve.wait_ge(vec_T, 1)
                link(v.tensor_copy(vec[:, :], ps[:, 7, 0:36]))
                take_row(0)
                for g in range(4):
                    norm_full(0, g)
                    if g:
                        norm_lo(0, g - 1)
                    if g == 1:
                        split(0)
                norm_lo(0, 3)
                split(1)
            elif step == "memory":
                g = arg[0]
                if g < 0:
                    dve.wait_ge(sq_done, 2)
                    mean_square(norm_event[1])
                else:
                    if g == 0:
                        take_row(1)
                    norm_full(1, g)
                    norm_lo(1, g)
            elif step == "norm":
                pass
            elif step == "residual":
                if used:
                    dve.wait_ge(unit_done, used)
                post(arg[0])
            elif step == "row":
                take_row(3)
                for name in ("cos", "sin"):
                    link(v.tensor_tensor(halves(const(name)), halves(const(name)), row_twice, ALU.mult))
                dve.wait_ge(wi_T, 1)
                for tb in range(TB):
                    link(v.tensor_scalar(index_w[:, tb, :], ps[:, 3, 8 * tb:8 * tb + 8],
                                         stat[:, norm_event[3], 6 + tb:7 + tb], None, ALU.mult))
            elif step == "finish":
                finish(arg[0], 0 if used <= G0 else 1)
            elif step == "unit":
                u = arg[0]
                ending = u in (out0 - 2, out0 - 1, out20 - 2, out20 - 1)
                if not ending:
                    split(u + 2)
                used = u + 1
                if units[u]["name"] == "merge":
                    dve.wait_ge(unit_done, u + 1)
                    merge(u)
                    if ending:
                        split(u + 1)
                elif units[u]["name"] == "out":
                    j = units[u]["j"]
                    if j == 0:
                        dve.wait_ge(in_gain[0], 16)
                    dve.wait_ge(sq_ready, j + 1)
                    gain = gain_rows[0][:, UC * j:UC * j + UC].unsqueeze(1).to_broadcast([P, TB, UC])
                    v.tensor_tensor(y_tok[:, :, UC * j:UC * j + UC],
                                    ps[:, bank_of[u], :].rearrange("p (a b) -> p a b", a=TB), gain, ALU.mult)\
                        .then_inc(out_dve, 1)
                elif units[u]["name"] == "out2":
                    j = units[u]["j"]
                    dve.wait_ge(unit_done, u + 1)
                    part = h[:, :, UC * j:UC * j + UC]
                    v.tensor_tensor(part, part, ps[:, bank_of[u], :].rearrange("p (a b) -> p a b", a=TB), ALU.add)\
                        .then_inc(out_dve, 1)
                    dve.wait_ge(out_dve, outs(u, True))
                    if j == 0:
                        dve.wait_ge(in_gain[0], 32)
                    gain = gain_rows[0][:, UC * j:UC * j + UC].unsqueeze(1).to_broadcast([P, TB, UC])
                    v.tensor_tensor(n3[:, :, UC * j:UC * j + UC], part, gain, ALU.mult).then_inc(hg_ready, 1)
            elif step == "pool_mix":
                dve.wait_ge(pool_p, 1)
                for g in range(4):
                    src = ps[:, 6 + g // 2, T * (g % 2):T * (g % 2) + T]
                    gain = vec[:, 16 + g:17 + g]
                    link(v.tensor_scalar(o_hi[:, g, :], src, gain, None, ALU.mult))
                    ins = v.scalar_tensor_tensor(o_lo[:, g, :], src, gain, o_hi[:, g, :].bitcast(F32), ALU.mult,
                                                 ALU.subtract)
                    link(ins) if g < 3 else ins.then_inc(pool_out, 1)
            elif step == "heads":
                if max(sum(arg, [])) < 12:
                    for k in arg[0]:
                        if kind(k) != "sb":
                            maxima(k)
                    for part, ks in ((take_middle, arg[1]), (take_pair, arg[2]), (keep_past, arg[1]),
                                     (weights, arg[0])):
                        for k in ks:
                            part(k)
                else:
                    for part, ks in ((take_pair, arg[2]), (maxima, arg[0]), (weights, arg[0])):
                        for k in ks:
                            part(k)
            elif step == "ffn":
                ffn()
                used = G0 + 3 * NF
            elif step == "route":
                r = arg[0]
                dve.wait_ge(route_T, r + 1)
                v.tensor_copy(flat(n3T[:, 2 * r:2 * r + 2, :]), ps[:, 2 + r, :]).then_inc(route_out, 1)
            elif step == "rope":
                rope(*arg)
            elif step == "index":
                for i in (arg[0], arg[0] + 1):
                    dve.wait_ge(ix_relu, i + 1)
                    for tb, (c0, c1) in enumerate(columns):
                        w, src = index_w[:, tb, i:i + 1], score_b[i % 2][:, c0:c1]
                        if i == 0:
                            ins = v.tensor_scalar(score[:, c0:c1], src, w, None, ALU.mult)
                        else:
                            ins = v.scalar_tensor_tensor(score[:, c0:c1], src, w, score[:, c0:c1], ALU.mult, ALU.add)
                        link(ins) if tb == 0 else ins.then_inc(ix_acc, 1)
                    dve.wait_ge(ix_acc, i + 1)
                if arg[0] == 6:
                    link(v.tensor_tensor(work[:, :], score[:, :], const("hide"), ALU.add))
            elif step == "topk":
                for tb, (c0, c1) in enumerate(columns):
                    link(v.max(best8[:, tb, :], work[:, c0:c1]))
                    link(v.match_replace(work[:, c0:c1], best8[:, tb, :], work[:, c0:c1], TAKEN))
            elif step == "select":
                link(v.tensor_scalar(score[:, :], work[:, :], TAKEN / 2, NEG, ALU.is_gt, ALU.mult))
                link(v.tensor_tensor(score[:, :], score[:, :], const("hide"), ALU.add))

        dve.wait_ge(hg_ready, 4)
        dve.wait_ge(sq_ready, 8)
        gather_squares(moe_event, 4)
        dve.wait_ge(logit_done, 1)
        dve.wait_ge(in_route, 64)
        for tb in range(TB):
            link(v.scalar_tensor_tensor(logits[:, tb, :], ps[:, 6 + tb, 0:36], stat[:, moe_event, 6 + tb:7 + tb],
                                        b_route[:, :], ALU.mult, ALU.add))

        def wide(x, n):
            return x.unsqueeze(2).to_broadcast([P, TB, n])

        def per_token(x, n):
            return x.unsqueeze(1).to_broadcast([P, TB, n])

        def tt(dst, a_, b_, op):
            link(v.tensor_tensor(dst, a_, b_, op))

        def biggest(dst, src, n):
            link(v.tensor_reduce(dst, src, AX.X, ALU.max))

        def first_of(dst, src, top, rev, n, place):
            tt(dst, src, wide(top, n), ALU.is_equal)
            tt(dst, dst, per_token(rev, n), ALU.mult)
            biggest(place, dst, n)
            tt(dst, dst, wide(place, n), ALU.is_equal)

        gmax, place, gsum, best, second, total, share = (r_s[:, i, :] for i in range(7))
        lg, le = logits[:, :, 0:GROUPS], logits[:, :, GROUPS:36]
        biggest(gmax, lg, GROUPS)
        tt(exp_in[:, :, 0:GROUPS], lg, wide(gmax, GROUPS), ALU.subtract)
        first_of(pick_g[:, :, :], lg, gmax, const("revg"), GROUPS, place)
        own = pick_g[:, :, :].unsqueeze(3).to_broadcast([P, TB, GROUPS, PER_GROUP])
        dst, hidden = (t[:, :, :].rearrange("p b (g e) -> p b g e", g=GROUPS) for t in (masked_e, pick))
        tt(dst, le.rearrange("p b (g e) -> p b g e", g=GROUPS), own, ALU.mult)
        link(v.tensor_scalar(hidden, own, 1.0, -NEG, ALU.subtract, ALU.mult))
        tt(dst, dst, hidden, ALU.add)
        biggest(best, masked_e[:, :, :], EXPERTS)
        v.tensor_tensor(exp_in[:, :, GROUPS:36], masked_e[:, :, :], wide(best, EXPERTS), ALU.subtract)\
            .then_inc(route_in, 1)
        first_of(chosen[:, :, :], masked_e[:, :, :], best, const("rev"), EXPERTS, place)
        link(v.scalar_tensor_tensor(masked_e[:, :, :], chosen[:, :, :], 2 * NEG, masked_e[:, :, :], ALU.mult,
                                    ALU.add))
        biggest(second, masked_e[:, :, :], EXPERTS)
        first_of(pick_one[:, :, :], masked_e[:, :, :], second, const("rev"), EXPERTS, place)
        v.tensor_tensor(chosen[:, :, :], chosen[:, :, :], pick_one[:, :, :], ALU.add).then_inc(route_sel, 1)
        dve.wait_ge(route_sel, 1)
        link(v.tensor_scalar(slot_no[:, :], const("slot"), 1.0, None, ALU.add))
        dve.wait_ge(route_exp, 1)
        link(v.tensor_reduce(gsum, exp_out[:, :, 0:GROUPS], AX.X, ALU.add))
        link(v.reciprocal(gsum, gsum))
        link(v.tensor_reduce(total, exp_out[:, :, GROUPS:36], AX.X, ALU.add))
        link(v.reciprocal(total, total))
        tt(gate_e[:, :, :], exp_out[:, :, GROUPS:36], wide(total, EXPERTS), ALU.mult)
        tt(gate_e[:, :, :], gate_e[:, :, :], chosen[:, :, :], ALU.mult)
        link(v.tensor_reduce(share, gate_e[:, :, :], AX.X, ALU.add))
        link(v.reciprocal(share, share))
        tt(share, share, gsum, ALU.mult)
        tt(gate_e[:, :, :], gate_e[:, :, :], wide(share, EXPERTS), ALU.mult)
        dve.wait_ge(rank_done, 1)
        link(v.scalar_tensor_tensor(flat(rank[:, :, :]), ps[:, 1, 0:2 * EXPERTS], 1.0, flat(chosen[:, :, :]), ALU.add,
                                    ALU.mult))

        def count_passes():
            link(v.tensor_reduce(r_s[:, 8, 0:1], ps[:, 1, 64:64 + EXPERTS], AX.X, ALU.max))
            link(v.tensor_scalar(exp_in[:, 0, 0:8], const("steps"), r_s[:, 8, 0:1], None, ALU.is_lt))
            link(v.tensor_reduce(r_s[:, 8, 1:2], exp_in[:, 0, 0:8], AX.X, ALU.add))
            v.tensor_copy(passes_i[:, :], r_s[:, 8, 1:2]).then_inc(passes_ready, 1)
            dve.wait_ge(passes_ready, 1)

        def quad_body(q, i, again=None):
            looped = not isinstance(q, int)
            e0 = dve.snap(q * QUAD) if looped else 0
            at_e = dve.snap(i * QUAD) if looped else i * QUAD
            slots = slot_no[:, :].unsqueeze(1).to_broadcast([P, QUAD, SLOTS])
            if again is not None:
                dve.wait_ge(slot_moved, again)
            for tb in range(TB):
                mine = rank[:, tb, bass.ds(at_e, QUAD)].unsqueeze(2).to_broadcast([P, QUAD, SLOTS])
                hot = one_hot[:, tb, :].rearrange("p (e s) -> p e s", e=QUAD)
                v.tensor_tensor(hot, slots, mine, ALU.is_equal).then_inc(hot_part, 1)
                dve.wait_ge(hot_part, q * 2 + (tb + 1))
            for tb in range(TB):
                hot = one_hot[:, tb, :].rearrange("p (e s) -> p e s", e=QUAD)
                gate = gate_e[:, tb, bass.ds(at_e, QUAD)].unsqueeze(2).to_broadcast([P, QUAD, SLOTS])
                ins = v.tensor_tensor(gated_hot[:, tb, :].rearrange("p (e s) -> p e s", e=QUAD), hot, gate, ALU.mult)
            ins.then_inc(hot_ready, 1)
            if not looped:
                count_passes()
            dve.wait_ge(xg_done, q + 1)
            v.tensor_copy(flat(xg[:, 4:8, :]), ps[:, 3, :]).then_inc(xg_ready, 1)
            for e in range(QUAD):
                done = dve.snap(e0 + (e + 1)) if looped else e + 1
                dve.wait_ge(e_silu, done)
                v.tensor_tensor(hid[:, :], silu_e[:, :], ps[:, 4 + e % 2, P:2 * P], ALU.mult).then_inc(e_hid, 1)
                dve.wait_ge(e_T, done)
                v.tensor_copy(hid_T[:, :], ps[:, 6, 0:P]).then_inc(e_hidT, 1)
                dve.wait_ge(e_y, done)
                for g in (2, 3):
                    v.tensor_copy(y_quad[SLOTS * e:SLOTS * e + SLOTS, UC * g:UC * g + UC],
                                  ps[SLOTS * g:SLOTS * g + SLOTS, 7, 0:UC]).then_inc(e_yD, 1)
            for tb in range(TB):
                dve.wait_ge(comb_done, q * 2 + (tb + 1))
                for half in range(2):
                    part = h[:, tb, 512 * half:512 * half + 512]
                    ins = v.tensor_tensor(part, part, ps[:, 2 * tb + half, :], ALU.add)
                ins.then_inc(comb_added[tb], 1)
                dve.wait_ge(comb_added[tb], q + 1)

        quad_body(0, 0)
        with dve.Fori(1, EXPERTS // QUAD) as i:
            quad_body(i, i)
        n_pass = dve.value_load(passes_i[0:1, 0:1], min_val=1, max_val=T // SLOTS)
        with dve.If(n_pass > 1):
            with dve.Fori(1, n_pass) as again:
                v.tensor_scalar(slot_no[:, :], slot_no[:, :], float(SLOTS), None, ALU.add).then_inc(slot_moved, 1)
                with dve.Fori(0, EXPERTS // QUAD) as i:
                    quad_body(dve.snap(again * (EXPERTS // QUAD) + i), i, again)
            dve.nop()
        dve.wait_ge(in_gain[1], 32)
        for tb in range(TB):
            link(v.tensor_tensor(n3[:, tb, :], h[:, tb, :], gain_rows[1][:, :], ALU.mult))
        dve.wait_ge(sq_done, 5)
        mean_square(last_event)
        dve.wait_ge(root_done, last_event + 1)
        for tb in range(TB):
            v.tensor_scalar(n3[:, tb, :], n3[:, tb, :], stat[:, last_event, 6 + tb:7 + tb], None, ALU.mult)\
                .then_inc(fin_ready, 1)

    block_cm.__exit__(None, None, None)


_INS = ["x", "mem", "norm_mix_pre", "w_in", "w_pool_mix", "pool_scale", "w_pool_o", "w_sb_o", "norm_mem", "w_mem_kv",
        "w_x_o", "w_out", "norm_mix_post", "norm_ffn_pre", "w_ffn_in", "w_ffn_out", "norm_ffn_post", "g_mix_2",
        "w_in_2", "w_proj_a_2", "w_proj_b_2", "w_out_2", "g_ffn_2", "w_group_2", "b_group_2", "w_expert_2",
        "b_expert_2", "w1_2", "w3_2", "w2_2", "g_final_2"]


def kernel(**inputs):
    import concourse.bacc as bacc
    from concourse.bass_utils import run_bass_kernel_spmd

    nc = bacc.Bacc("TRN2", target_bir_lowering=False, num_devices=1)
    arrays, aps = {}, {}
    for name in _INS:
        x = np.ascontiguousarray(inputs[name])
        arrays[f"in_{name}"] = x
        aps[name] = nc.dram_tensor(f"in_{name}", x.shape, mybir.dt.from_np(x.dtype), kind="ExternalInput").ap()
    for name, x in (("table", make_table()), ("windows", make_windows())):
        arrays[f"in_{name}"] = x
        aps[name] = nc.dram_tensor(f"in_{name}", x.shape, F32, kind="ExternalInput").ap()
    out = nc.dram_tensor("out", (1, T, D), F32, kind="ExternalOutput").ap()
    layers_kernel(nc, aps, aps["table"], aps["windows"], out)
    r = run_bass_kernel_spmd(nc, [arrays], core_ids=[0])
    return r.results[0]["out"]
```
